# Optimizing a Trainium2 kernel written in Bass

```python
import jax
import jax.numpy as jnp
from jax import lax
import numpy as np
import math
import jax, jax.numpy as jnp

D_MODEL = 1024
BATCH = 1
SEQ = 256
DEPTH = 1

D_MIX = D_MODEL
ATTN_HEAD_DIM = 64
ATTN_HEADS = (D_MIX // 2) // ATTN_HEAD_DIM
ATTN_WIDTH = ATTN_HEADS * ATTN_HEAD_DIM
DILATED_PATTERNS = ((128, 1), (512, 4), (2048, 16))
ALIBI_MAX_BIAS = 8.0
HGRN_KEY_DIM = 128
HGRN_VAL_DIM = 128
HGRN_HEADS = (D_MIX - ATTN_WIDTH) // HGRN_VAL_DIM
HGRN_WIDTH = HGRN_HEADS * HGRN_VAL_DIM
HGRN_FDIM = HGRN_HEADS * HGRN_KEY_DIM
HGRN_CHUNK = 64
IN_SPLITS = (ATTN_WIDTH, ATTN_WIDTH, ATTN_WIDTH, HGRN_FDIM, HGRN_FDIM, HGRN_FDIM, HGRN_WIDTH, HGRN_WIDTH)
D_IN = 3 * ATTN_WIDTH + 3 * HGRN_FDIM + 2 * HGRN_WIDTH
N_EXPERTS = 16
CAPACITY_FACTOR = 2
D_FF_EXPERT = D_MODEL
NORM_EPS = 1e-6
NEG_INF = -1e30


def rms_norm(x, w):
    xf = x.astype(jnp.float32)
    y = xf * lax.rsqrt(jnp.mean(xf * xf, axis=-1, keepdims=True) + NORM_EPS)
    return (y * w.astype(jnp.float32)).astype(x.dtype)

def alibi_slopes(n_heads):
    return jnp.exp2(-ALIBI_MAX_BIAS * jnp.arange(1, n_heads + 1, dtype=jnp.float32) / n_heads)

def dilated_window_attention(q, k, v, window, dilation, slopes):
    B, S, H, Dh = q.shape
    half = window // (2 * dilation)
    blk = half
    span = dilation * blk
    Sp = -(-S // span) * span
    L = Sp // dilation
    nb = L // blk

    def to_sub(t):
        t = jnp.pad(t, ((0, 0), (0, Sp - S), (0, 0), (0, 0)))
        return t.reshape(B, L, dilation, H, Dh).transpose(0, 2, 1, 3, 4)

    def windows(t):
        t = jnp.pad(t, ((0, 0), (0, 0), (blk, blk), (0, 0), (0, 0))).reshape(B, dilation, nb + 2, blk, H, Dh)
        return jnp.concatenate([t[:, :, :-2], t[:, :, 1:-1], t[:, :, 2:]], axis=3)

    qs = to_sub(q).reshape(B, dilation, nb, blk, H, Dh)
    ks = windows(to_sub(k))
    vs = windows(to_sub(v))

    qi = jnp.arange(blk)
    kj = jnp.arange(3 * blk)
    delta = kj[None, :] - blk - qi[:, None]
    band = jnp.abs(delta) <= half
    l_k = jnp.arange(nb)[:, None] * blk - blk + kj[None, :]
    pos_k = l_k[None] * dilation + jnp.arange(dilation)[:, None, None]
    key_ok = (l_k[None] >= 0) & (pos_k < S)
    mask = band[None, None, None] & key_ok[:, :, None, None, :]
    bias = -slopes[:, None, None] * (dilation * jnp.abs(delta)).astype(jnp.float32)[None]

    s = jnp.einsum('brnqhd,brnkhd->brnhqk', qs, ks)
    s = jnp.where(mask, s + bias, NEG_INF)
    m = jnp.max(s, axis=-1, keepdims=True)
    e = jnp.exp(s - m)
    den = jnp.sum(e, axis=-1)
    num = jnp.einsum('brnhqk,brnkhd->brnqhd', e, vs)

    def back_stat(t):
        t = t.transpose(0, 1, 2, 4, 3).reshape(B, dilation, L, H)
        return t.transpose(0, 2, 1, 3).reshape(B, Sp, H)[:, :S]

    num = num.reshape(B, dilation, L, H, Dh).transpose(0, 2, 1, 3, 4).reshape(B, Sp, H, Dh)[:, :S]
    return back_stat(m[..., 0]), back_stat(den), num

def dilated_attention_mixer(q, k, v, q_norm_w, k_norm_w):
    B, S, _ = q.shape
    shp = (B, S, ATTN_HEADS, ATTN_HEAD_DIM)
    qh = rms_norm(q.reshape(shp), q_norm_w).astype(jnp.float32) * (ATTN_HEAD_DIM ** -0.5)
    kh = rms_norm(k.reshape(shp), k_norm_w).astype(jnp.float32)
    vh = v.reshape(shp).astype(jnp.float32)
    slopes = alibi_slopes(ATTN_HEADS)
    ms, dens, nums = [], [], []
    for window, dilation in DILATED_PATTERNS:
        m, den, num = dilated_window_attention(qh, kh, vh, window, dilation, slopes)
        ms.append(m)
        dens.append(den)
        nums.append(num)
    m_all = jnp.stack(ms)
    scale = jnp.exp(m_all - jnp.max(m_all, axis=0, keepdims=True))
    numer = jnp.sum(scale[..., None] * jnp.stack(nums), axis=0)
    denom = jnp.sum(scale * jnp.stack(dens), axis=0)
    return (numer / denom[..., None]).reshape(B, S, ATTN_WIDTH)

def chunked_gated_recurrence(q, k, v, log_f):
    B, S, H, Dk = q.shape
    Dv = v.shape[-1]
    C = HGRN_CHUNK
    n = S // C

    def to_chunks(t):
        return t.reshape(B, n, C, H, t.shape[-1]).transpose(1, 0, 3, 2, 4)

    incl = jnp.tril(jnp.ones((C, C), dtype=bool))[:, :, None]

    def step(state, inp):
        qb, kb, vb, gb = inp
        b = jnp.cumsum(gb, axis=2)
        o_inter = jnp.einsum('bhck,bhkv->bhcv', qb * jnp.exp(b), state)
        diff = b[:, :, :, None, :] - b[:, :, None, :, :]
        decay = jnp.exp(jnp.where(incl, diff, -jnp.inf))
        a = jnp.einsum('bhtk,bhsk,bhtsk->bhts', qb, kb, decay)
        o_intra = jnp.einsum('bhts,bhsv->bhtv', a, vb)
        b_last = b[:, :, -1:, :]
        k_dec = kb * jnp.exp(b_last - b)
        state = jnp.exp(b_last[:, :, 0, :])[..., None] * state + jnp.einsum('bhsk,bhsv->bhkv', k_dec, vb)
        return state, o_inter + o_intra

    init = jnp.zeros((B, H, Dk, Dv), jnp.float32)
    _, out = lax.scan(step, init, (to_chunks(q), to_chunks(k), to_chunks(v), to_chunks(log_f)))
    return out.transpose(1, 0, 3, 2, 4).reshape(B, S, H, Dv)

def hgrn2_mixer(q, f_fwd, f_bwd, i, g, lb_fwd, lb_bwd, out_norm_w):
    B, S, _ = q.shape

    def heads(t, d):
        return t.reshape(B, S, HGRN_HEADS, d).astype(jnp.float32)

    qh = jax.nn.silu(heads(q, HGRN_KEY_DIM))
    vh = heads(i, HGRN_VAL_DIM)

    def gates(f_raw, lb):
        lb = lb.reshape(HGRN_HEADS, HGRN_KEY_DIM)
        z = heads(f_raw, HGRN_KEY_DIM)
        f = lb + (1.0 - lb) * jax.nn.sigmoid(z)
        return (1.0 - lb) * jax.nn.sigmoid(-z), jnp.log(f)

    k_f, lf_f = gates(f_fwd, lb_fwd)
    k_b, lf_b = gates(f_bwd, lb_bwd)
    o_f = chunked_gated_recurrence(qh, k_f, vh, lf_f)
    flip = lambda t: jnp.flip(t, axis=1)
    o_b = flip(chunked_gated_recurrence(flip(qh), flip(k_b), flip(vh), flip(lf_b)))
    o = rms_norm(o_f + o_b, out_norm_w) * jax.nn.silu(heads(g, HGRN_VAL_DIM))
    return o.reshape(B, S, HGRN_WIDTH)

def expert_choice_moe(h, w_router, w_gate, w_up, w_down):
    B, S, D = h.shape
    cap = max(1, CAPACITY_FACTOR * S // N_EXPERTS)
    logits = jnp.einsum('bsd,de->bse', h, w_router).astype(jnp.float32)
    aff = jax.nn.softmax(logits, axis=-1)
    gate, idx = lax.top_k(aff.transpose(0, 2, 1), cap)
    xin = jax.vmap(lambda hb, ib: hb[ib])(h, idx)
    hid = jax.nn.silu(jnp.einsum('becd,edf->becf', xin, w_gate)) * jnp.einsum('becd,edf->becf', xin, w_up)
    y = jnp.einsum('becf,efd->becd', hid, w_down) * gate[..., None].astype(h.dtype)
    bidx = jnp.arange(B)[:, None, None]
    return jnp.zeros_like(h).at[bidx, idx].add(y)

def first_inputs(seed: int = 0) -> dict:
    key = jax.random.key(seed)
    ks = jax.random.split(key, 16)
    f32 = jnp.float32
    nrm = lambda k, shape, fan_in: jax.random.normal(k, shape, f32) * (fan_in ** -0.5)
    gain = lambda k, shape: 1.0 + 0.02 * jax.random.normal(k, shape, f32)
    return {
        "x": jax.random.normal(ks[0], (BATCH, SEQ, D_MODEL), f32),
        "norm1_w": gain(ks[1], (DEPTH, D_MODEL)),
        "w_in": nrm(ks[2], (DEPTH, D_MODEL, D_IN), D_MODEL),
        "attn_q_norm_w": gain(ks[3], (DEPTH, ATTN_HEAD_DIM)),
        "attn_k_norm_w": gain(ks[4], (DEPTH, ATTN_HEAD_DIM)),
        "hgrn_lb_fwd": 1.0 + 0.1 * jax.random.normal(ks[5], (DEPTH + 1, HGRN_FDIM), f32),
        "hgrn_lb_bwd": 1.0 + 0.1 * jax.random.normal(ks[6], (DEPTH + 1, HGRN_FDIM), f32),
        "hgrn_out_norm_w": gain(ks[7], (DEPTH, HGRN_VAL_DIM)),
        "w_out": nrm(ks[8], (DEPTH, D_MIX, D_MODEL), D_MIX),
        "norm2_w": gain(ks[9], (DEPTH, D_MODEL)),
        "w_router": nrm(ks[10], (DEPTH, D_MODEL, N_EXPERTS), D_MODEL),
        "w_expert_gate": nrm(ks[11], (DEPTH, N_EXPERTS, D_MODEL, D_FF_EXPERT), D_MODEL),
        "w_expert_up": nrm(ks[12], (DEPTH, N_EXPERTS, D_MODEL, D_FF_EXPERT), D_MODEL),
        "w_expert_down": nrm(ks[13], (DEPTH, N_EXPERTS, D_FF_EXPERT, D_MODEL), D_FF_EXPERT),
    }

def first_block(x, norm1_w, w_in, attn_q_norm_w, attn_k_norm_w, hgrn_lb_fwd, hgrn_lb_bwd,
              hgrn_out_norm_w, w_out, norm2_w, w_router, w_expert_gate, w_expert_up, w_expert_down):
    lb_f_all = jnp.cumsum(jax.nn.softmax(hgrn_lb_fwd.astype(jnp.float32), axis=0), axis=0)
    lb_b_all = jnp.cumsum(jax.nn.softmax(hgrn_lb_bwd.astype(jnp.float32), axis=0), axis=0)
    split_at = np.cumsum(IN_SPLITS)[:-1].tolist()
    for l in range(DEPTH):
        h = rms_norm(x, norm1_w[l])
        proj = jnp.einsum('bsd,de->bse', h, w_in[l])
        aq, ak, av, hq, hf_f, hf_b, hi, hg = jnp.split(proj, split_at, axis=-1)
        a_out = dilated_attention_mixer(aq, ak, av, attn_q_norm_w[l], attn_k_norm_w[l])
        b_out = hgrn2_mixer(hq, hf_f, hf_b, hi, hg, lb_f_all[l], lb_b_all[l], hgrn_out_norm_w[l])
        mixed = jnp.concatenate([a_out.astype(x.dtype), b_out.astype(x.dtype)], axis=-1)
        x = x + jnp.einsum('bsm,md->bsd', mixed, w_out[l])
        x = x + expert_choice_moe(rms_norm(x, norm2_w[l]), w_router[l], w_expert_gate[l],
                                  w_expert_up[l], w_expert_down[l])
    return x


DEPTH_2 = 2

MIX_WIDTH = D_MODEL
DA_WIDTH = MIX_WIDTH // 2
SC_WIDTH = MIX_WIDTH // 4
LRU_WIDTH = MIX_WIDTH - DA_WIDTH - SC_WIDTH

DA_HEAD_DIM = 64
DA_HEADS = DA_WIDTH // (2 * DA_HEAD_DIM)
Q_BLOCK = 128
NUM_BUCKETS = 32
MAX_DISTANCE = 128
SUBLN_EPS = 1e-5

SC_KERNEL = 3

LRU_BLOCKS = 4
LRU_BLOCK = LRU_WIDTH // LRU_BLOCKS
LRU_CONV = 4
LRU_C = 8.0

D_FF = 2816
RMS_EPS = 1e-6
NEG_INF_2 = -1e30

IN_SPLIT_WIDTHS = (DA_WIDTH, DA_WIDTH, DA_WIDTH,
                   SC_WIDTH, SC_WIDTH, SC_WIDTH,
                   LRU_WIDTH, LRU_WIDTH)
IN_WIDTH = sum(IN_SPLIT_WIDTHS)
IN_SPLIT_POINTS = tuple(int(v) for v in np.cumsum(IN_SPLIT_WIDTHS)[:-1])


def rms_norm_2(x, g, eps=RMS_EPS):
    xf = x.astype(jnp.float32)
    y = xf * lax.rsqrt(jnp.mean(xf * xf, axis=-1, keepdims=True) + eps)
    return (y * g.astype(jnp.float32)).astype(x.dtype)

def swiglu(x, w_gate, w_up, w_down):
    return (jax.nn.silu(x @ w_gate) * (x @ w_up)) @ w_down

def causal_dwconv(x, w):
    K = w.shape[0]
    S = x.shape[1]
    xp = jnp.pad(x, ((0, 0), (K - 1, 0), (0, 0)))
    return sum(xp[:, k:k + S] * w[k] for k in range(K))

def t5_bucket(n):
    max_exact = NUM_BUCKETS // 2
    nf = jnp.maximum(n, 1).astype(jnp.float32)
    large = max_exact + (jnp.log(nf / max_exact) / math.log(MAX_DISTANCE / max_exact)
                         * (NUM_BUCKETS - max_exact)).astype(jnp.int32)
    large = jnp.minimum(large, NUM_BUCKETS - 1)
    return jnp.where(n < max_exact, n, large)

def diff_attention(q, k, v, lq1, lk1, lq2, lk2, subln_g, rel_bias, lam_init):
    B, S, _ = q.shape
    nblk = S // Q_BLOCK
    q = q.reshape(B, S, DA_HEADS, 2, DA_HEAD_DIM) * (DA_HEAD_DIM ** -0.5)
    k = k.reshape(B, S, DA_HEADS, 2, DA_HEAD_DIM)
    v = v.reshape(B, S, DA_HEADS, 2 * DA_HEAD_DIM)
    f32 = jnp.float32
    lam = (jnp.exp(jnp.sum(lq1.astype(f32) * lk1.astype(f32)))
           - jnp.exp(jnp.sum(lq2.astype(f32) * lk2.astype(f32))) + lam_init)
    k_pos = jnp.arange(S)
    q_blocks = jnp.moveaxis(q.reshape(B, nblk, Q_BLOCK, DA_HEADS, 2, DA_HEAD_DIM), 1, 0)

    def block(args):
        qb, start = args
        q_pos = start + jnp.arange(Q_BLOCK)
        dist = q_pos[:, None] - k_pos[None, :]
        bias = rel_bias[t5_bucket(jnp.maximum(dist, 0))]
        bias = bias.reshape(Q_BLOCK, S, DA_HEADS, 2).transpose(2, 3, 0, 1).astype(f32)
        logits = jnp.einsum('bqhmd,bkhmd->bhmqk', qb, k).astype(f32) + bias
        logits = jnp.where(dist >= 0, logits, NEG_INF_2)
        p = jax.nn.softmax(logits, axis=-1)
        attn = p[:, :, 0] - lam * p[:, :, 1]
        return jnp.einsum('bhqk,bkhe->bqhe', attn.astype(v.dtype), v)

    starts = jnp.arange(nblk) * Q_BLOCK
    o = lax.map(block, (q_blocks, starts))
    o = jnp.moveaxis(o, 0, 1).reshape(B, S, DA_HEADS, 2 * DA_HEAD_DIM)
    o = rms_norm_2(o, subln_g, SUBLN_EPS) * (1.0 - lam_init)
    return o.reshape(B, S, DA_WIDTH)

def block_diag_linear(x, w, b):
    B, S, _ = x.shape
    xb = x.reshape(B, S, LRU_BLOCKS, LRU_BLOCK)
    y = jnp.einsum('bsni,nij->bsnj', xb, w) + b
    return y.reshape(B, S, LRU_WIDTH)

def rg_lru(x, wa, ba, wx, bx, lam):
    f32 = jnp.float32
    r = jax.nn.sigmoid(block_diag_linear(x, wa, ba)).astype(f32)
    i = jax.nn.sigmoid(block_diag_linear(x, wx, bx)).astype(f32)
    log_a = -LRU_C * r * jax.nn.softplus(-lam.astype(f32))
    a = jnp.exp(log_a)
    mult = jnp.sqrt(-jnp.expm1(2.0 * log_a))
    b = mult * (i * x.astype(f32))

    def combine(e, l):
        return (e[0] * l[0], l[0] * e[1] + l[1])

    _, h = lax.associative_scan(combine, (a, b), axis=1)
    return h.astype(x.dtype)

def second_inputs(seed: int = 0) -> dict:
    key = jax.random.key(seed)
    ks = iter(jax.random.split(key, 40))
    f32 = jnp.float32

    def nrm(shape, fan_in):
        return jax.random.normal(next(ks), shape, f32) * fan_in ** -0.5

    def gain(shape):
        return 1.0 + 0.02 * jax.random.normal(next(ks), shape, f32)

    def small(shape, s):
        return s * jax.random.normal(next(ks), shape, f32)

    u = jax.random.uniform(next(ks), (DEPTH_2, LRU_WIDTH), f32, minval=0.9, maxval=0.999)
    a0 = u ** (1.0 / LRU_C)
    lru_lambda = jnp.log(a0) - jnp.log1p(-a0)

    return {
        "x": jax.random.normal(next(ks), (BATCH, SEQ, D_MODEL), f32),
        "rel_bias": small((NUM_BUCKETS, 2 * DA_HEADS), 0.5),
        "ffn1_norm": gain((DEPTH_2, D_MODEL)),
        "ffn1_gate": nrm((DEPTH_2, D_MODEL, D_FF), D_MODEL),
        "ffn1_up": nrm((DEPTH_2, D_MODEL, D_FF), D_MODEL),
        "ffn1_down": nrm((DEPTH_2, D_FF, D_MODEL), D_FF),
        "mix_norm": gain((DEPTH_2, D_MODEL)),
        "w_in": nrm((DEPTH_2, D_MODEL, IN_WIDTH), D_MODEL),
        "w_out": nrm((DEPTH_2, MIX_WIDTH, D_MODEL), MIX_WIDTH),
        "lam_q1": small((DEPTH_2, DA_HEAD_DIM), 0.1),
        "lam_k1": small((DEPTH_2, DA_HEAD_DIM), 0.1),
        "lam_q2": small((DEPTH_2, DA_HEAD_DIM), 0.1),
        "lam_k2": small((DEPTH_2, DA_HEAD_DIM), 0.1),
        "subln_gain": gain((DEPTH_2, 2 * DA_HEAD_DIM)),
        "sc_conv_w": nrm((DEPTH_2, SC_KERNEL, SC_WIDTH), SC_KERNEL),
        "lru_conv_w": nrm((DEPTH_2, LRU_CONV, LRU_WIDTH), LRU_CONV),
        "lru_conv_b": small((DEPTH_2, LRU_WIDTH), 0.01),
        "lru_wa": nrm((DEPTH_2, LRU_BLOCKS, LRU_BLOCK, LRU_BLOCK), LRU_BLOCK),
        "lru_ba": small((DEPTH_2, LRU_BLOCKS, LRU_BLOCK), 0.01),
        "lru_wx": nrm((DEPTH_2, LRU_BLOCKS, LRU_BLOCK, LRU_BLOCK), LRU_BLOCK),
        "lru_bx": small((DEPTH_2, LRU_BLOCKS, LRU_BLOCK), 0.01),
        "lru_lambda": lru_lambda,
        "ffn2_norm": gain((DEPTH_2, D_MODEL)),
        "ffn2_gate": nrm((DEPTH_2, D_MODEL, D_FF), D_MODEL),
        "ffn2_up": nrm((DEPTH_2, D_MODEL, D_FF), D_MODEL),
        "ffn2_down": nrm((DEPTH_2, D_FF, D_MODEL), D_FF),
        "final_norm": gain((D_MODEL,)),
    }

def second_block(x, rel_bias, ffn1_norm, ffn1_gate, ffn1_up, ffn1_down, mix_norm, w_in, w_out,
              lam_q1, lam_k1, lam_q2, lam_k2, subln_gain, sc_conv_w, lru_conv_w, lru_conv_b,
              lru_wa, lru_ba, lru_wx, lru_bx, lru_lambda, ffn2_norm, ffn2_gate, ffn2_up,
              ffn2_down, final_norm):
    for l in range(DEPTH_2):
        h = x + 0.5 * swiglu(rms_norm_2(x, ffn1_norm[l]), ffn1_gate[l], ffn1_up[l], ffn1_down[l])

        u = rms_norm_2(h, mix_norm[l])
        z = u @ w_in[l]
        q, k, v, sc_b, sc_c, sc_x, lru_x, lru_g = jnp.split(z, IN_SPLIT_POINTS, axis=-1)

        lam_init = 0.8 - 0.6 * math.exp(-0.3 * l)
        y_da = diff_attention(q, k, v, lam_q1[l], lam_k1[l], lam_q2[l], lam_k2[l],
                              subln_gain[l], rel_bias, lam_init)
        y_sc = sc_b * causal_dwconv(sc_c * sc_x, sc_conv_w[l])
        xr = causal_dwconv(lru_x, lru_conv_w[l]) + lru_conv_b[l]
        y_lru = jax.nn.gelu(lru_g) * rg_lru(xr, lru_wa[l], lru_ba[l], lru_wx[l], lru_bx[l],
                                            lru_lambda[l])

        h = h + jnp.concatenate([y_da, y_sc, y_lru], axis=-1) @ w_out[l]

        x = h + 0.5 * swiglu(rms_norm_2(h, ffn2_norm[l]), ffn2_gate[l], ffn2_up[l], ffn2_down[l])
    return rms_norm_2(x, final_norm)


def setup_inputs(seed=0):
    out = dict(first_inputs(seed))
    for name, value in second_inputs(seed + 1).items():
        if name != "x":
            out[name + "_2"] = value
    return out


def reference(
    x, norm1_w, w_in, attn_q_norm_w, attn_k_norm_w, hgrn_lb_fwd, hgrn_lb_bwd, hgrn_out_norm_w,
    w_out, norm2_w, w_router, w_expert_gate, w_expert_up, w_expert_down, rel_bias_2,
    ffn1_norm_2, ffn1_gate_2, ffn1_up_2, ffn1_down_2, mix_norm_2, w_in_2, w_out_2, lam_q1_2,
    lam_k1_2, lam_q2_2, lam_k2_2, subln_gain_2, sc_conv_w_2, lru_conv_w_2, lru_conv_b_2,
    lru_wa_2, lru_ba_2, lru_wx_2, lru_bx_2, lru_lambda_2, ffn2_norm_2, ffn2_gate_2, ffn2_up_2,
    ffn2_down_2, final_norm_2,
):
    x = first_block(
        x, norm1_w, w_in, attn_q_norm_w, attn_k_norm_w, hgrn_lb_fwd, hgrn_lb_bwd,
        hgrn_out_norm_w, w_out, norm2_w, w_router, w_expert_gate, w_expert_up, w_expert_down,
    )
    return second_block(
        x, rel_bias_2, ffn1_norm_2, ffn1_gate_2, ffn1_up_2, ffn1_down_2, mix_norm_2, w_in_2,
        w_out_2, lam_q1_2, lam_k1_2, lam_q2_2, lam_k2_2, subln_gain_2, sc_conv_w_2,
        lru_conv_w_2, lru_conv_b_2, lru_wa_2, lru_ba_2, lru_wx_2, lru_bx_2, lru_lambda_2,
        ffn2_norm_2, ffn2_gate_2, ffn2_up_2, ffn2_down_2, final_norm_2,
    )


_drawn_inputs = setup_inputs


def setup_inputs(seed=0):
    import zlib

    import numpy as np

    out = dict(_drawn_inputs(seed))
    spreads = {}
    factors = {'attn_q_norm_w': 6.541,
     'attn_k_norm_w': 5.756,
     'hgrn_lb_fwd': 4.501,
     'hgrn_lb_bwd': 8.0,
     'hgrn_out_norm_w': 3.018,
     'ffn1_norm_2': 4.392,
     'lam_k1_2': 4.543,
     'lam_k2_2': 8.0,
     'subln_gain_2': 21.246,
     'lru_conv_b_2': 141.432,
     'lru_ba_2': 200.0,
     'lru_bx_2': 200.0,
     'ffn2_norm_2': 6.43,
     'final_norm_2': 20.676,
     'lru_wa_2': 34.04,
     'lru_lambda_2': 33.496,
     'lru_conv_w_2': 8.0,
     'lru_wx_2': 8.0}
    for name, (base, spread) in spreads.items():
        noise = np.random.default_rng([zlib.crc32(name.encode()), seed]).standard_normal(out[name].shape)
        drawn = base * np.exp(spread * noise) if base else spread * noise
        out[name] = jnp.asarray(drawn.astype(out[name].dtype))
    for name, factor in factors.items():
        out[name] = (out[name] * factor).astype(out[name].dtype)
    return out
```

```python
import math
from contextlib import ExitStack

import numpy as np

import concourse.bass as bass
from concourse import mybir

F32 = mybir.dt.float32
U32 = mybir.dt.uint32
ALU = mybir.AluOpType
ACT = mybir.ActivationFunctionType
AX = mybir.AxisListType

P = 128
S = 256
D = 1024
TT = S // P
KD = D // P
BANK = 512
EPS = 1e-6

AH, AD = 8, 64
HH, HD = 4, 128
PATTERNS = ((128, 1), (512, 4), (2048, 16))
NE = 16
CAP = 2 * S // NE
FE = 1024
Q4 = P // CAP
LN_LEAST = 2.0 ** -64
SQRT_LEAST = 2.0 ** -116
LEVELS = [S >> (i + 1) for i in range(int(math.log2(S)))]

DEPTH2 = 2
DH, DM = 4, 64
NBUCKET, MAXDIST = 32, 128
SUBLN_EPS = 1e-5
LRU_C = 8.0
GELU_C = math.sqrt(2.0 / math.pi)
DFF = 2816
FS = 256
STEPS = DFF // FS
Z2 = [(1536, 512), (2048, 512), (2560, 256), (0, 512), (512, 512), (1024, 512)]
TBW = P + S - 1
LOG1P_TERMS = 8
NEG = -1e30
LINKS = 76


def fields(*sizes):
    at, out = 0, {}
    for name, n in sizes:
        out[name] = (at, at + n)
        at += n
    return out, at


CONST, CONST_W = fields(("ident", P), ("fold", CAP), ("rank", CAP))
BAND_W = P + S
BAND, BAND_N = fields(("bias", AH * BAND_W), ("count", BAND_W), ("mask", len(LEVELS) * P))
ONE, ONE_N = fields(("norm1", KD), ("norm2", KD), ("q", 1), ("k", 1), ("lb", 4 * HH), ("onorm", HD),
                    ("router", KD * NE))
PRM, PRM_N = fields(("norm0", KD), ("norm1", KD), ("norm2", KD), ("lq1", DM), ("lk1", DM), ("lq2", DM),
                    ("lk2", DM), ("subg", 1), ("lam0", 1), ("oml", 1), ("scw", 6), ("lruw", 8), ("lrub", 2),
                    ("ba", 2), ("bx", 2), ("lam", 2), ("wa", 2 * P), ("wx", 2 * P))


def const_arrays():
    small = np.zeros((P, CONST_W), np.float32)
    small[:, CONST["ident"][0]:CONST["ident"][1]] = np.eye(P)
    small[:, CONST["fold"][0]:CONST["fold"][1]] = np.tile(np.eye(CAP), (Q4, 1))
    small[:, CONST["rank"][0]:CONST["rank"][1]] = np.arange(1, CAP + 1)
    dist = np.abs(P + np.arange(P)[:, None] - np.arange(BAND_W)[None, :])
    count = sum(((dist % dil == 0) & (dist // dil <= win // (2 * dil))).astype(np.float32) for win, dil in PATTERNS)
    slopes = np.exp2(-8.0 * np.arange(1, AH + 1, dtype=np.float32) / AH)
    bias = [np.where(count > 0, -s * dist, NEG) for s in slopes]
    s_at, t_at = np.arange(P)[:, None], np.arange(P)[None, :]
    masks = [(s_at // (2 * w) == t_at // (2 * w)) & (s_at // w != t_at // w) for w in LEVELS[1:]] + [s_at == t_at]
    band = np.concatenate(bias + [count] + masks, axis=1).astype(np.float32)
    n = np.arange(TBW + 1) - (P - 1)
    exact = NBUCKET // 2
    large = exact + (np.log(np.maximum(n, 1).astype(np.float32) / exact) / math.log(MAXDIST / exact)
                     * (NBUCKET - exact)).astype(np.int32)
    bucket = np.where(n < exact, n, np.minimum(large, NBUCKET - 1))
    onehot = ((bucket[None, :] == np.arange(NBUCKET)[:, None]) & (n >= 0)).astype(np.float32)
    future = np.tile(np.where(n < 0, NEG, 0.0), (2 * DH, 1)).astype(np.float32)
    return small, band, onehot, future


class Chain:

    def __init__(self, eng, counter):
        self.eng, self.counter, self.n, self.base = eng, counter, 0, 0

    def step(self, ins):
        ins.then_inc(self.counter, 1)
        self.n += 1

    def settle(self):
        self.eng.wait_ge(self.counter, self.base + self.n)

    def link(self, ins):
        self.step(ins)
        self.settle()


def two_blocks(nc, x_in, w_in, w_out, wg, wu, wd, relb, f1g, f1u, f1d, w_in2, w_out2, f2g, f2u, f2d,
               const, band, onehot, future, one, prm_in, fin_w, out):
    with ExitStack() as ctx:
        def sb(name, n):
            return ctx.enter_context(nc.sbuf_tensor(name, [P, n], F32))

        SLOT = KD * 512
        ring = sb("ring", 6 * SLOT)
        x_sb = sb("x_sb", TT * D)
        xT_sb = sb("xT_sb", KD * S)
        xn_sb = sb("xn_sb", TT * D)
        const_sb = sb("const_sb", CONST_W)
        one_sb = sb("one_sb", ONE_N)
        stat = sb("stat", 256)
        WORK = 19300
        work = sb("work", WORK)
        ps = ctx.enter_context(nc.psum_tensor("ps", [P, 8 * BANK], F32))
        tb_dram = nc.dram_tensor("rel_bias_band", [2 * DH, TBW + 1], F32, kind="Internal")

        x = x_sb[:, :].rearrange("p (t d) -> p t d", t=TT)
        xT = xT_sb[:, :].rearrange("p (k s) -> p k s", k=KD)
        xn = xn_sb[:, :].rearrange("p (t d) -> p t d", t=TT)
        ident = const_sb[:, CONST["ident"][0]:CONST["ident"][1]]
        fold = const_sb[:, CONST["fold"][0]:CONST["fold"][1]]
        rank = const_sb[:, CONST["rank"][0]:CONST["rank"][1]]

        def slot(s, n=512):
            return ring[:, s * SLOT:s * SLOT + KD * n].rearrange("p (k n) -> p k n", k=KD)

        def bank(b, n=1):
            return ps[:, b * BANK:(b + n) * BANK]

        def one_f(name):
            return one_sb[:, ONE[name][0]:ONE[name][1]]

        at = [0]

        def st(n):
            at[0] += n
            assert at[0] <= 256
            return stat[:, at[0] - n:at[0]]

        n_ss, n_ms, n_std, n_rstd = st(TT), st(TT), st(TT), st(TT)
        lbm, lbe, lbr, lb, oml = st(8), st(16), st(8), st(8), st(8)
        qk_ss, qk_ms, qk_std, qk_rstd = st(32), st(32), st(32), st(32)

        def region(buf, n, start=0):
            pos = [start]

            def take(size):
                pos[0] += size
                assert pos[0] <= n, (pos[0], n)
                return buf[:, pos[0] - size:pos[0]]
            return take

        t1 = region(work, WORK)
        hq, kf, kb, bc, rc = [t1(HH * S).rearrange("p (h s) -> p h s", h=HH) for _ in range(5)]
        v_tok, hi_tok, gs_tok = [t1(TT * 512).rearrange("p (t c) -> p t c", t=TT) for _ in range(3)]
        qT, kT = [t1(4 * S).rearrange("p (c s) -> p c s", c=4) for _ in range(2)]
        at_diag, at_off = [t1(HH * TT * P).rearrange("p (h t c) -> p h t c", h=HH, t=TT) for _ in range(2)]
        a_s = [t1(2 * S).rearrange("p (h s) -> p h s", h=2) for _ in range(3)]
        a_eT = [t1(2 * S).rearrange("p (h j s) -> p h j s", h=2, j=TT) for _ in range(2)]
        count = t1(BAND_W)
        masks = t1(len(LEVELS) * P).rearrange("p (l s) -> p l s", l=len(LEVELS))
        a_st = t1(4 * 16)
        a_mx, a_nm, a_den, a_rden = [a_st[:, 16 * i:16 * i + 16] for i in range(4)]
        o_st = t1(4 * 8)
        o_ss, o_ms, o_std, o_rstd = [o_st[:, 8 * i:8 * i + 8] for i in range(4)]
        ones_s = t1(S)
        r1 = region(ring, 3 * SLOT)
        lev_e = [r1(2 * HH * S) for _ in range(2)]
        lev_qk = r1(2 * HH * S)
        sqj = r1(2 * TT * 512).rearrange("p (c t n) -> p c t n", c=2, t=TT)
        abias = r1(AH * BAND_W).rearrange("p (h i) -> p h i", h=AH)
        aq_tok = xn_sb[:, 0:1024].rearrange("p (t c) -> p t c", t=TT)
        ak_tok = xn_sb[:, 1024:2048].rearrange("p (t c) -> p t c", t=TT)
        mixed = xn

        LATE = 2 * PRM_N + 2 * DH * S + D + (TBW + 1) * 3 + 2 * DH
        t2 = region(work, WORK - LATE)
        xin_all = t2(KD * NE * CAP).rearrange("p (k e c) -> p k e c", k=KD, e=NE)
        hot = t2(TT * NE * CAP).rearrange("p (t e c) -> p t e c", t=TT, e=NE)
        aff = t2(TT * NE).rearrange("p (t e) -> p t e", t=TT)
        aff_e = t2(TT * NE).rearrange("p (t e) -> p t e", t=TT)
        posT = t2(TT * NE).rearrange("p (t e) -> p t e", t=TT)
        r_mx, r_nm, r_sum, r_rec = t2(TT), t2(TT), t2(TT), t2(TT)
        affT, topw, chosen, place, ones_e = [t2(S)[0:NE, :] for _ in range(5)]
        top8 = t2(8)[0:NE, :]
        hot_e = t2(TT * P).rearrange("p (t j c) -> p t j c", t=TT, j=Q4)
        back = t2(S)
        xin = t2(KD * CAP).rearrange("p (k c) -> p k c", k=KD)
        g4, u4, y4 = [[t2(512) for _ in range(2)] for _ in range(3)]
        e_sil = [t2(4 * CAP) for _ in range(2)]
        hidT = t2(KD * CAP).rearrange("p (k c) -> p k c", k=KD)

        t3 = region(work, WORK, WORK - LATE)
        prm_all = t3(2 * PRM_N).rearrange("p (l n) -> p l n", l=2)
        tb_raw = t3(2 * DH * S).rearrange("p (h i) -> p h i", h=2 * DH)
        fin_row = t3(D)
        tb_rows, tb_future = t3(TBW + 1)[0:2 * DH, :], t3(TBW + 1)[0:2 * DH, :]
        tb_onehot, tb_rel = t3(TBW + 1)[0:NBUCKET, :], t3(2 * DH)[0:NBUCKET, :]
        t4 = region(work, WORK - LATE)
        prm = t4(PRM_N)
        tb = t4(2 * DH * S).rearrange("p (h i) -> p h i", h=2 * DH)
        f_buf = t4(4 * 512)
        f_sil = [f_buf[:, 512 * i:512 * i + 512] for i in range(2)]
        f_hid = [f_buf[:, 1024 + 512 * i:1536 + 512 * i].rearrange("p (f s) -> p f s", f=2) for i in range(2)]
        d_e = f_buf.rearrange("p (g m h s) -> p g m h s", g=2, m=2, h=2)
        raw_place = tb_raw.rearrange("p h i -> p (h i)")
        qT2, scbc = [raw_place[:, 1024 * i:1024 * i + 1024].rearrange("p (c s) -> p c s", c=4) for i in range(2)]
        kT2 = t4(4 * S).rearrange("p (c s) -> p c s", c=4)
        v2 = t4(TT * 512).rearrange("p (t c) -> p t c", t=TT)
        sc_pad = t4(2 * (S + 2)).rearrange("p (c s) -> p c s", c=2)
        lx_pad = t4(2 * (S + 3)).rearrange("p (c s) -> p c s", c=2)
        lgate, xr, rg, ig, la, lm, lg, yc = [t4(2 * S).rearrange("p (c s) -> p c s", c=2) for _ in range(8)]
        d_attn, d_aT = t4(2 * S).rearrange("p (h s) -> p h s", h=2), t4(2 * S).rearrange("p (h j s) -> p h j s", h=2, j=2)
        lc = t4(32)
        lc_y, lc_ab, lc_u, lc_den, lc_z, lc_z2, lc_p, lc_c, lc_n = [lc[:, 2 * i:2 * i + 2] for i in range(9)]
        lamv = t4(8)
        d_st = t4(8 * 16)
        d_mx, d_nm, d_den, d_rd, d_c1, d_ss, d_ms, d_std = [d_st[:, 16 * i:16 * i + 16] for i in range(8)]
        lam_j = t4(DM)
        d_hold = t4(1)
        f_set = [ring[:, i * 6144:(i + 1) * 6144] for i in range(2)]
        f_gate = [f[:, 0:2048].rearrange("p (k n) -> p k n", k=KD) for f in f_set]
        f_up = [f[:, 2048:4096].rearrange("p (k n) -> p k n", k=KD) for f in f_set]
        f_down = [f[:, 4096:6144].rearrange("p (k n) -> p k n", k=2) for f in f_set]

        def pf(name, i=None):
            a, b = PRM[name]
            return prm[:, a:b] if i is None else prm[:, a + i:a + i + 1]

        names = """x_in const_in one_in band_in w1_in0 w1_in1 w1_in2 ex_in0 ex_in1 ex_in2 ex_in3 ex_in4 ex_in5
            mxT_ps mx_act mx_dve k_scaled late_in tb_out tb_in gu_in0 gu_in1 dn_in0 dn_in1 wm_in0 wm_in1 wm_in2 fin_out
            sq_done ms_ready std_ready rstd_ready xn_dve xn_act xnT_ps xT_act xT_dve acc_done x_act x_dve
            z_ready z_hq z_hf z_hb z_q z_k z_v z_hi z_hg
            lb_max lb_exp lb_done gate_sg gate_lf lev_sub lev_exp lev_q lev_k lev_ps lev_put
            qk_sq qk_ms qk_std qkT_ps qT_done kT_done
            sc_ps sc_nm sc_exp sc_cnt eT_ps eT_act eT_dve o_ps o_put ho_ps ho_sq ho_ms ho_std ho_put gs_done
            masks_zero lg_ps lg_nm lg_exp aff_done affT_ps place_done placeT_ps hot_done xin_ps xin_act xin_dve
            xe_ready hote_done gate_ps up_ps back_ps g4_done u4_done back_done sum_ps esil_done ehid_done
            y_ps y4_act y4_dve scat_done tb_ps tb_rows_done
            prm_ready gu_ps sil_done hid_done dn_done
            z2_ready z2_0 z2_1 z2_2 z2_q z2_k z2_v
            lru_u lru_c lru_xr lru_ps lru_gates lru_a lru_m lru_sq lru_b gelu_in gelu_t ysc_done ylru_done
            d_lamx d_lame d_ps d_nmx d_exp d_comb dT_ps dT_done do_ps do_sq do_ms do_std do_nrm yT_ps yT_done
            fin_put dve_chain pads_zero""".split()
        sem = {n: ctx.enter_context(nc.semaphore(n)) for n in names}
        w1_in = [sem["w1_in0"], sem["w1_in1"], sem["w1_in2"]]
        ex_in = [sem["ex_in0"], sem["ex_in1"], sem["ex_in2"], sem["ex_in3"], sem["ex_in4"], sem["ex_in5"]]
        gu_in, dn_in = [sem["gu_in0"], sem["gu_in1"]], [sem["dn_in0"], sem["dn_in1"]]
        wm_in = [sem["wm_in0"], sem["wm_in1"], sem["wm_in2"]]
        WM_USES = [3, 3, 2]

        PROJ = [("hq", 3, True), ("hf", 4, True), ("hb", 5, True), ("q", 0, False), ("k", 1, False),
                ("v", 2, False), ("hi", 6, False), ("hg", 7, False)]
        Z_FREE = [sem["z_hq"], sem["z_hf"], sem["z_hb"], sem["z_q"], sem["z_k"], sem["z_v"], sem["z_hi"], sem["z_hg"]]
        NLEV = len(LEVELS)
        GROUPS = [(0, 2), (1, 3), (4, 6), (5, 7)]
        NG = TT * len(GROUPS)

        block = ctx.enter_context(nc.Block())

        @block.sync
        def _(sp):
            def weights(w, c0, n):
                return w.rearrange("(k p) n -> p k n", p=P)[:, :, c0:c0 + n]

            sp.dma_start(x, x_in.rearrange("(t p) d -> p t d", p=P)).then_inc(sem["x_in"], 16)
            sp.dma_start(const_sb[:, :], const).then_inc(sem["const_in"], 16)
            sp.dma_start(one_sb[:, :], one).then_inc(sem["one_in"], 16)
            for o in range(len(PROJ) + 2):
                if o >= 3:
                    sp.wait_ge(sem["z_ready"], o - 2)
                w, c = (w_in, PROJ[o][1]) if o < len(PROJ) else (w_out, o - len(PROJ))
                sp.dma_start(slot(3 + o % 3), weights(w, 512 * c, 512)).then_inc(w1_in[o % 3], 16)
                if o == 2:
                    a, b = BAND["mask"]
                    sp.dma_start(masks.rearrange("p l s -> p (l s)"), band[:, a:b]).then_inc(sem["band_in"], 16)
                    a, b = BAND["count"]
                    sp.dma_start(count, band[:, a:b]).then_inc(sem["band_in"], 16)
                    a, b = BAND["bias"]
                    sp.dma_start(abias.rearrange("p h i -> p (h i)"), band[:, a:b]).then_inc(sem["band_in"], 16)

            def expert(e, i, w, c):
                sp.dma_start(slot(i), w[e].rearrange("(k p) n -> p k n", p=P)[:, :, 512 * c:512 * c + 512])\
                    .then_inc(ex_in[i], 16)

            ORDER = [(0, wg, 0), (2, wu, 0), (1, wg, 1), (3, wu, 1), (4, wd, 0), (5, wd, 1)]
            sp.wait_ge(sem["o_put"], TT)
            sp.wait_ge(sem["ho_put"], TT)
            for i, w, c in ORDER[:3]:
                expert(0, i, w, c)
            sp.wait_ge(sem["acc_done"], 1)
            for i, w, c in ORDER[3:]:
                expert(0, i, w, c)
            sp.dma_start(prm_all, prm_in.rearrange("l p n -> p l n")).then_inc(sem["late_in"], 16)
            sp.dma_start(fin_row, fin_w).then_inc(sem["late_in"], 16)
            sp.dma_start(tb_future, future).then_inc(sem["late_in"], 16)
            sp.dma_start(tb_onehot, onehot).then_inc(sem["late_in"], 16)
            sp.dma_start(tb_rel, relb).then_inc(sem["late_in"], 16)
            sp.wait_ge(sem["tb_rows_done"], 1)
            sp.dma_start(tb_dram.ap(), tb_rows).then_inc(sem["tb_out"], 16)
            sp.wait_ge(sem["tb_out"], 16)
            sp.dma_start(tb_raw, bass.AP(tb_dram, 0, [[1, P], [TBW + 1, 2 * DH], [1, S]])).then_inc(sem["tb_in"], 16)
            with sp.Fori(1, NE) as e:
                free = sp.snap(2 * e - 1)
                free2 = sp.snap(2 * e)
                sp.wait_ge(sem["gate_ps"], free)
                expert(e, 0, wg, 0)
                sp.wait_ge(sem["up_ps"], free)
                expert(e, 2, wu, 0)
                sp.wait_ge(sem["gate_ps"], free2)
                expert(e, 1, wg, 1)
                sp.wait_ge(sem["up_ps"], free2)
                expert(e, 3, wu, 1)
                sp.wait_ge(sem["y_ps"], free)
                expert(e, 4, wd, 0)
                sp.wait_ge(sem["y_ps"], free2)
                expert(e, 5, wd, 1)
            sp.wait_ge(sem["scat_done"], NE)

            def ffn_step(L, c, i, w_g, w_u, w_d, first_gu, first_dn):
                if first_gu is not None:
                    sp.wait_ge(sem["gu_ps"], first_gu)
                sp.dma_start(f_gate[i], w_g[L, :, bass.ds(c, FS)].rearrange("(k p) n -> p k n", p=P)).then_inc(gu_in[i], 16)
                sp.dma_start(f_up[i], w_u[L, :, bass.ds(c, FS)].rearrange("(k p) n -> p k n", p=P)).then_inc(gu_in[i], 16)
                if first_dn is not None:
                    sp.wait_ge(sem["dn_done"], first_dn)
                sp.dma_start(f_down[i], w_d[L, bass.ds(c, FS), :].rearrange("(k p) n -> p k n", p=P)).then_inc(dn_in[i], 16)

            def ffn_loads(L, f, w_g, w_u, w_d):
                q = 2 * L + f
                free = sp.snap(3 * L + 1 + f)
                sp.wait_ge(sem["acc_done"], free)
                for c in range(2):
                    ffn_step(L, c * FS, c, w_g, w_u, w_d, None, None)
                with sp.Fori(1, STEPS // 2) as i:
                    for j in range(2):
                        gu, dn = sp.snap(STEPS * q + 2 * i + j - 1), sp.snap((STEPS - 1) * q + 2 * i + j - 1)
                        c = sp.snap(i * (2 * FS) + j * FS)
                        ffn_step(L, c, j, w_g, w_u, w_d, gu, dn)
                gu, dn = sp.snap(STEPS * q + STEPS - 2), sp.snap((STEPS - 1) * q + STEPS - 2)
                ffn_step(L, (STEPS - 1) * FS, (STEPS - 1) % 2, w_g, w_u, w_d, gu, dn)

            with sp.Fori(0, DEPTH2) as L:
                ffn_loads(L, 0, f1g, f1u, f1d)
                for o in range(len(Z2) + 2):
                    if o >= 3:
                        free = sp.snap(len(Z2) * L + o - 2)
                        sp.wait_ge(sem["z2_ready"], free)
                    w, (c0, n) = (w_in2, Z2[o]) if o < len(Z2) else (w_out2, (512 * (o - len(Z2)), 512))
                    sp.dma_start(slot(3 + o % 3, n), w[L].rearrange("(k p) n -> p k n", p=P)[:, :, c0:c0 + n])\
                        .then_inc(wm_in[o % 3], 16)
                ffn_loads(L, 1, f2g, f2u, f2d)
            sp.wait_ge(sem["fin_put"], TT)
            sp.dma_start(out.rearrange("(t p) d -> p t d", p=P), xn).then_inc(sem["fin_out"], 16)
            sp.wait_ge(sem["fin_out"], 16)

        @block.tensor
        def _(pe):
            def turn(b, src, ready):
                for k in range(KD):
                    for t in range(TT):
                        mm = pe.transpose(bank(b + k // 2)[:, (k % 2) * S + t * P:(k % 2) * S + t * P + P],
                                          src[:, t, k * P:k * P + P], ident)
                    if k % 2:
                        mm.then_inc(ready, 1)

            def norm(n):
                pe.wait_ge(sem["xn_dve"], n + 1)
                pe.wait_ge(sem["xn_act"], n + 1)
                turn(4, xn, sem["xnT_ps"])
                pe.wait_ge(sem["xT_act"], n + 1)
                pe.wait_ge(sem["xT_dve"], n + 1)

            def residual():
                for t in range(TT):
                    for n in range(2):
                        pe.matmul(bank(2 * t + n), ident, x[:, t, 512 * n:512 * n + 512], start=True, stop=False,
                                  skip_group_check=True)

            def project(n, w):
                for t in range(TT):
                    for k in range(KD):
                        mm = pe.matmul(bank(2 * t + n), xT[:, k, t * P:t * P + P], w[:, k, :], start=False,
                                       stop=k == KD - 1, skip_group_check=True)
                return mm

            def features(b, w, nf):
                for f in range(nf):
                    for k in range(KD):
                        mm = pe.matmul(bank(b + f // 2)[:, (f % 2) * S:(f % 2) * S + S], w[:, k, f * P:f * P + P],
                                       xT[:, k, :], start=k == 0, stop=k == KD - 1)
                return mm

            def tokens(b, w):
                for t in range(TT):
                    for k in range(KD):
                        mm = pe.matmul(bank(b + t), xT[:, k, t * P:t * P + P], w[:, k, :], start=k == 0,
                                       stop=k == KD - 1)
                return mm

            def proj(o):
                pe.wait_ge(w1_in[o % 3], 16 * (o // 3 + 1))
                if o >= 3:
                    pe.wait_ge(Z_FREE[o - 3], 1)
                (features(2 + 2 * (o % 3), slot(3 + o % 3), 4) if PROJ[o][2] else
                 tokens(2 + 2 * (o % 3), slot(3 + o % 3))).then_inc(sem["z_ready"], 1)

            q_l = lev_qk[:, 0:HH * S].rearrange("p (h s) -> p h s", h=HH)
            k_l = lev_qk[:, HH * S:2 * HH * S].rearrange("p (h s) -> p h s", h=HH)

            def level(i):
                pe.wait_ge(sem["lev_k"], i + 1)
                if i < NLEV:
                    pe.wait_ge(sem["lev_q"], i + 1)
                if i >= 1:
                    pe.wait_ge(sem["lev_put"], i)
                moving = q_l if i < NLEV else hq
                for h in range(HH):
                    for t in range(TT):
                        to = 1 - t if i == 0 else t
                        c = (h % 2) * S + t * P
                        mm = pe.matmul(bank(h // 2)[:, c:c + P], k_l[:, h, t * P:t * P + P],
                                       moving[:, h, to * P:to * P + P], start=True, stop=True)
                mm.then_inc(sem["lev_ps"], 1)

            pe.wait_ge(sem["const_in"], 16)
            norm(0)
            for o in range(len(PROJ)):
                proj(o)
                if o >= 4:
                    for i in {4: [0], 5: [1, 2], 6: [3, 4], 7: range(5, NLEV + 1)}[o]:
                        level(i)

            pe.wait_ge(sem["lev_put"], NLEV + 1)
            for t in range(TT):
                for h in range(HH):
                    o_h = bank(t)[:, h * HD:h * HD + HD]
                    pe.matmul(o_h, at_diag[:, h, t, :], hi_tok[:, t, h * HD:h * HD + HD], start=True, stop=False)
                    mm = pe.matmul(o_h, at_off[:, h, 1 - t, :], hi_tok[:, 1 - t, h * HD:h * HD + HD],
                                   start=False, stop=True)
                mm.then_inc(sem["ho_ps"], 1)

            pe.wait_ge(sem["z_hi"], 1)
            pe.wait_ge(sem["z_hg"], 1)
            for b, src in ((2, aq_tok), (4, ak_tok)):
                for c in range(4):
                    for t in range(TT):
                        mm = pe.transpose(bank(b + c // 2)[:, (c % 2) * S + t * P:(c % 2) * S + t * P + P],
                                          src[:, t, c * P:c * P + P], ident)
                mm.then_inc(sem["qkT_ps"], 1)
            pe.wait_ge(sem["qT_done"], 1)
            pe.wait_ge(sem["kT_done"], 1)
            pe.wait_ge(sem["z_v"], 1)

            def scores(g):
                t = g // len(GROUPS)
                if g >= 2:
                    pe.wait_ge(sem["sc_nm"], g - 1)
                for i, h in enumerate(GROUPS[g % len(GROUPS)]):
                    r = AD * (h % 2)
                    mm = pe.matmul(bank(6 + g % 2)[:, i * S:i * S + S], qT[r:r + AD, h // 2, t * P:t * P + P],
                                   kT[r:r + AD, h // 2, :], start=True, stop=True)
                mm.then_inc(sem["sc_ps"], 1)

            def turn_e(g):
                pe.wait_ge(sem["sc_cnt"], g + 1)
                if g >= 2:
                    pe.wait_ge(sem["eT_dve"] if g % 2 else sem["eT_act"], g // 2)
                for i in range(2):
                    for j in range(TT):
                        mm = pe.transpose(bank(2 + g % 2)[:, (2 * i + j) * P:(2 * i + j) * P + P],
                                          a_s[g % 3][:, i, j * P:j * P + P], ident)
                mm.then_inc(sem["eT_ps"], 1)

            def values(g):
                t = g // len(GROUPS)
                pe.wait_ge(sem["eT_dve"] if g % 2 else sem["eT_act"], g // 2 + 1)
                for i, h in enumerate(GROUPS[g % len(GROUPS)]):
                    for j in range(TT):
                        mm = pe.matmul(bank(4 + t)[:, h * AD:h * AD + AD], a_eT[g % 2][:, i, j, :],
                                       v_tok[:, j, h * AD:h * AD + AD], start=j == 0, stop=j == TT - 1)
                if g % len(GROUPS) == len(GROUPS) - 1:
                    mm.then_inc(sem["o_ps"], 1)

            scores(0)
            scores(1)
            for g in range(NG):
                turn_e(g)
                if g + 2 < NG:
                    scores(g + 2)
                if g >= 1:
                    values(g - 1)
            values(NG - 1)

            pe.wait_ge(sem["o_put"], TT)
            pe.wait_ge(sem["ho_put"], TT)
            turn(4, mixed, sem["mxT_ps"])
            residual()
            pe.wait_ge(sem["mx_act"], 1)
            pe.wait_ge(sem["mx_dve"], 1)
            for n in range(2):
                o = len(PROJ) + n
                pe.wait_ge(w1_in[o % 3], 16 * (o // 3 + 1))
                mm = project(n, slot(3 + o % 3))
            mm.then_inc(sem["acc_done"], 1)

            norm(1)
            router = one_f("router").rearrange("p (k e) -> p k e", k=KD)
            for t in range(TT):
                for k in range(KD):
                    mm = pe.matmul(bank(0)[:, t * NE:t * NE + NE], xT[:, k, t * P:t * P + P], router[:, k, :],
                                   start=k == 0, stop=k == KD - 1)
            mm.then_inc(sem["lg_ps"], 1)
            pe.wait_ge(sem["late_in"], 80)
            pe.matmul(bank(3)[0:2 * DH, 0:TBW + 1], tb_rel, tb_onehot, start=True, stop=True).then_inc(sem["tb_ps"], 1)
            pe.wait_ge(sem["aff_done"], 1)
            for t in range(TT):
                mm = pe.transpose(bank(1)[0:NE, t * P:t * P + P], aff[:, t, :], ident)
            mm.then_inc(sem["affT_ps"], 1)
            pe.wait_ge(sem["place_done"], 1)
            for t in range(TT):
                mm = pe.transpose(bank(2)[:, t * NE:t * NE + NE], place[:, t * P:t * P + P], ident[0:NE, 0:NE])
            mm.then_inc(sem["placeT_ps"], 1)
            pe.wait_ge(sem["hot_done"], 1)
            for k in range(KD):
                if k >= 4:
                    pe.wait_ge(sem["xin_dve"] if k % 2 else sem["xin_act"], (k - 4) // 2 + 1)
                for t in range(TT):
                    mm = pe.matmul(bank(4 + k % 4), xn[:, t, k * P:k * P + P],
                                   hot[:, t, :, :].rearrange("p e c -> p (e c)"), start=t == 0, stop=t == TT - 1)
                mm.then_inc(sem["xin_ps"], 1)
            pe.wait_ge(sem["tb_rows_done"], 1)
            residual()
            pe.wait_ge(sem["xin_act"], KD // 2)
            pe.wait_ge(sem["xin_dve"], KD // 2)

            def quarter(b, stationary, w):
                for r in range(KD // Q4):
                    for j in range(Q4):
                        mm = pe.matmul(bank(b)[j * CAP:j * CAP + CAP, :], stationary[:, Q4 * r + j, :],
                                       w[:, Q4 * r + j, :], start=r == 0, stop=r == KD // Q4 - 1,
                                       skip_group_check=True)
                return mm

            with pe.Fori(0, NE) as e:
                landed = pe.snap(16 * e + 16)
                pe.wait_ge(sem["xe_ready"], e + 1)
                pe.wait_ge(ex_in[0], landed)
                quarter(4, xin, slot(0)).then_inc(sem["gate_ps"], 1)
                pe.wait_ge(ex_in[2], landed)
                quarter(5, xin, slot(2)).then_inc(sem["up_ps"], 1)
                pe.wait_ge(sem["hote_done"], e + 1)
                for t in range(TT):
                    mm = pe.transpose(bank(7)[:, t * P:t * P + P], hot_e[:, t, :, :].rearrange("p j c -> p (j c)"), ident)
                mm.then_inc(sem["back_ps"], 1)
                pe.wait_ge(sem["g4_done"], 2 * e + 1)
                pe.wait_ge(ex_in[1], landed)
                quarter(4, xin, slot(1)).then_inc(sem["gate_ps"], 1)
                pe.wait_ge(sem["u4_done"], 2 * e + 1)
                pe.wait_ge(ex_in[3], landed)
                quarter(5, xin, slot(3)).then_inc(sem["up_ps"], 1)
                pe.wait_ge(sem["back_done"], e + 1)
                for c in range(2):
                    pe.wait_ge(sem["g4_done"], 2 * e + c + 1)
                    pe.wait_ge(sem["u4_done"], 2 * e + c + 1)
                    for i, src in enumerate((g4[c], u4[c])):
                        for f in range(4):
                            a = (4 * i + f) * CAP
                            mm = pe.matmul(bank(6 + c)[:, a:a + CAP], src[:, f * P:f * P + P], fold, start=True, stop=True)
                    mm.then_inc(sem["sum_ps"], 1)
                pe.wait_ge(sem["ehid_done"], 2 * e + 2)
                for n in range(2):
                    pe.wait_ge(ex_in[4 + n], landed)
                    quarter(4 + n, hidT, slot(4 + n)).then_inc(sem["y_ps"], 1)
                for n in range(2):
                    pe.wait_ge(sem["y4_dve"] if n else sem["y4_act"], e + 1)
                    for t in range(TT):
                        mm = pe.matmul(bank(2 * t + n), back[:, t * P:t * P + P], y4[n], start=False, stop=False,
                                       skip_group_check=True)
                mm.then_inc(sem["scat_done"], 1)

            def ffn(L, f):
                q = 2 * L + f

                def gate_up(c, landed):
                    pe.wait_ge(gu_in[c], landed)
                    for b, w in ((4 + c, f_gate[c]), (6 + c, f_up[c])):
                        mm = features(b, w, 2)
                    mm.then_inc(sem["gu_ps"], 1)

                def down(c, landed, hidden, done):
                    pe.wait_ge(dn_in[c], landed)
                    pe.wait_ge(sem["hid_done"], hidden)
                    for k in range(2):
                        for t in range(TT):
                            for n in range(2):
                                mm = pe.matmul(bank(2 * t + n), f_hid[c][:, k, t * P:t * P + P],
                                               f_down[c][:, k, 512 * n:512 * n + 512], start=False,
                                               stop=done is sem["acc_done"] and k == 1, skip_group_check=True)
                    mm.then_inc(done, 1)

                residual()
                gate_up(0, 32 * (6 * q + 1))
                with pe.Fori(0, STEPS // 2) as i:
                    gate_up(1, 32 * (5 * q + 1) + 32 * i)
                    down(0, 16 * (6 * q + 1) + 16 * i, STEPS * q + 1 + 2 * i, sem["dn_done"])
                    gate_up(0, 32 * (6 * q + 2) + 32 * i)
                    down(1, 16 * (5 * q + 1) + 16 * i, STEPS * q + 2 + 2 * i, sem["dn_done"])
                down(0, 16 * (6 * q + 6), STEPS * q + STEPS, sem["acc_done"])

            with pe.Fori(0, DEPTH2) as L:
                norm(3 * L + 2)
                ffn(L, 0)
                norm(3 * L + 3)

                def landed(o):
                    pe.wait_ge(wm_in[o % 3], 16 * WM_USES[o % 3] * L + 16 * (o // 3 + 1))

                def feats(o, b):
                    landed(o)
                    features(b, slot(3 + o % 3, Z2[o][1]), Z2[o][1] // P).then_inc(sem["z2_ready"], 1)

                feats(0, 0)
                feats(1, 2)
                feats(2, 4)
                feats(3, 6)
                pe.wait_ge(sem["z2_0"], L + 1)
                feats(4, 0)
                pe.wait_ge(sem["lru_xr"], L + 1)
                pe.wait_ge(sem["z2_2"], L + 1)
                for b, name in ((5, "wa"), (4, "wx")):
                    for c in range(2):
                        a = PRM[name][0] + c * P
                        mm = pe.matmul(bank(b)[:, c * S:c * S + S], prm[:, a:a + P], xr[:, c, :], start=True, stop=True)
                mm.then_inc(sem["lru_ps"], 1)
                pe.wait_ge(sem["z2_1"], L + 1)
                landed(5)
                tokens(2, slot(5)).then_inc(sem["z2_ready"], 1)
                pe.wait_ge(sem["z2_q"], L + 1)
                pe.wait_ge(sem["z2_k"], L + 1)

                def scores2(g):
                    t, n = g // 2, P * (g // 2 + 1)
                    if g == 1:
                        pe.wait_ge(sem["lru_gates"], L + 1)
                    if g >= 2:
                        pe.wait_ge(sem["d_nmx"], 4 * L + g - 1)
                    for m in range(2):
                        for i in range(2):
                            h = 2 * (g % 2) + i
                            mm = pe.matmul(bank(6 - 2 * (g % 2) + m)[:, i * S:i * S + n],
                                           qT2[m * DM:m * DM + DM, h, t * P:t * P + P],
                                           kT2[m * DM:m * DM + DM, h, 0:n], start=True, stop=True)
                    mm.then_inc(sem["d_ps"], 1)

                def turn_d(g):
                    pe.wait_ge(sem["d_comb"], 4 * L + g + 1)
                    if g == 0:
                        pe.wait_ge(sem["z2_v"], L + 1)
                    if g >= 2:
                        pe.wait_ge(sem["dT_done"], 4 * L + g - 1)
                    for i in range(2):
                        for j in range(g // 2 + 1):
                            mm = pe.transpose(bank(2 + g % 2)[:, (2 * i + j) * P:(2 * i + j) * P + P],
                                              d_attn[:, i, j * P:j * P + P], ident)
                    mm.then_inc(sem["dT_ps"], 1)

                def values2(g):
                    pe.wait_ge(sem["dT_done"], 4 * L + g + 1)
                    for i in range(2):
                        h = 2 * (g % 2) + i
                        for j in range(g // 2 + 1):
                            mm = pe.matmul(bank(g // 2)[:, h * P:h * P + P], d_aT[:, i, j, :], v2[:, j, h * P:h * P + P],
                                           start=j == 0, stop=j == g // 2)
                    mm.then_inc(sem["do_ps"], 1)

                scores2(0)
                scores2(1)
                for g in range(4):
                    turn_d(g)
                    if g + 2 < 4:
                        scores2(g + 2)
                    values2(g)
                pe.wait_ge(sem["do_nrm"], L + 1)
                for h in range(DH):
                    for t in range(TT):
                        mm = pe.transpose(bank(4 + h // 2)[:, (h % 2) * S + t * P:(h % 2) * S + t * P + P],
                                          xn[:, t, h * P:h * P + P], ident)
                mm.then_inc(sem["yT_ps"], 1)
                residual()
                pe.wait_ge(sem["yT_done"], L + 1)
                pe.wait_ge(sem["ysc_done"], L + 1)
                pe.wait_ge(sem["ylru_done"], L + 1)
                for n in range(2):
                    landed(len(Z2) + n)
                    mm = project(n, slot(3 + (len(Z2) + n) % 3))
                mm.then_inc(sem["acc_done"], 1)
                norm(3 * L + 4)
                ffn(L, 1)

        @block.scalar
        def _(act):
            def norm(n, weight):
                for t in range(TT):
                    sq = nc.scalar.activation(xn[:, t, :], x[:, t, :], ACT.Square, accum_out=n_ss[:, t:t + 1])
                sq.then_inc(sem["sq_done"], 1)
                act.wait_ge(sem["ms_ready"], n + 1)
                nc.scalar.activation(n_std, n_ms, ACT.Sqrt).then_inc(sem["std_ready"], 1)
                act.wait_ge(sem["rstd_ready"], n + 1)
                nc.scalar.activation(xn[:, 1, :], x[:, 1, :], ACT.Copy, scale=n_rstd[:, 1:2]).then_inc(sem["xn_act"], 1)
                for k in range(4):
                    if k % 2 == 0:
                        act.wait_ge(sem["xnT_ps"], 4 * n + k // 2 + 1)
                    a = nc.scalar.activation(xT[:, k, :], bank(4 + k // 2)[:, (k % 2) * S:(k % 2) * S + S], ACT.Copy,
                                             scale=weight[:, k:k + 1])
                a.then_inc(sem["xT_act"], 1)

            def update(done):
                act.wait_ge(done[0], done[1])
                nc.scalar.activation(x[:, 0, :], bank(0, 2), ACT.Copy).then_inc(sem["x_act"], 1)

            def x_ready(n):
                act.wait_ge(sem["x_act"], n)
                act.wait_ge(sem["x_dve"], n)

            act.wait_ge(sem["x_in"], 16)
            act.wait_ge(sem["one_in"], 16)
            norm(0, one_f("norm1"))
            act.wait_ge(sem["lb_max"], 1)
            nc.scalar.activation(lbe, lbe, ACT.Exp).then_inc(sem["lb_exp"], 1)
            act.wait_ge(sem["z_ready"], 1)
            nc.scalar.activation(hq.rearrange("p h s -> p (h s)"), bank(2, 2), ACT.Silu).then_inc(sem["z_hq"], 1)
            sg = lev_e[1].rearrange("p (d n) -> p d n", d=2)
            lf = lev_e[0].rearrange("p (d n) -> p d n", d=2)
            for d, (b, k_raw, free) in enumerate(((4, kf, sem["z_hf"]), (6, kb, sem["z_hb"]))):
                act.wait_ge(sem["z_ready"], 2 + d)
                nc.scalar.activation(sg[:, d, :], bank(b, 2), ACT.Sigmoid).then_inc(sem["gate_sg"], 1)
                nc.scalar.activation(k_raw.rearrange("p h s -> p (h s)"), bank(b, 2), ACT.Sigmoid, scale=-1.0)\
                    .then_inc(free, 1)
            act.wait_ge(sem["lb_done"], 1)
            act.wait_ge(sem["gate_sg"], 2)
            for d in range(2):
                for h in range(HH):
                    i = d * HH + h
                    a = nc.scalar.activation(lf[:, d, h * S:h * S + S], sg[:, d, h * S:h * S + S], ACT.Ln,
                                             scale=oml[:, i:i + 1], bias=lb[:, i:i + 1])
                a.then_inc(sem["gate_lf"], 1)

            def decay(i):
                act.wait_ge(sem["lev_sub"], i + 1)
                nc.scalar.activation(lev_e[i % 2], lev_e[i % 2], ACT.Exp).then_inc(sem["lev_exp"], 1)

            decay(0)
            decay(1)
            for c, b in ((0, 2), (1, 4)):
                act.wait_ge(sem["z_ready"], 4 + c)
                nc.scalar.activation(sqj[:, c, :, :].rearrange("p t n -> p (t n)"), bank(b, 2), ACT.Square)\
                    .then_inc(sem["qk_sq"], 1)
            act.wait_ge(sem["qk_ms"], 1)
            nc.scalar.activation(qk_std, qk_ms, ACT.Sqrt).then_inc(sem["qk_std"], 1)
            decay(2)
            decay(3)
            act.wait_ge(sem["z_ready"], 6)
            nc.scalar.activation(v_tok.rearrange("p t n -> p (t n)"), bank(6, 2), ACT.Copy).then_inc(sem["z_v"], 1)
            for i in range(4, NLEV):
                decay(i)
            act.wait_ge(sem["z_ready"], 8)
            nc.scalar.activation(gs_tok.rearrange("p t n -> p (t n)"), bank(4, 2), ACT.Silu).then_inc(sem["z_hg"], 1)
            act.wait_ge(sem["qkT_ps"], 2)
            nc.scalar.activation(kT.rearrange("p c s -> p (c s)"), bank(4, 2), ACT.Copy, scale=one_f("k"))\
                .then_inc(sem["kT_done"], 1)
            act.wait_ge(sem["ho_ps"], 2)
            ho_sqj = sqj[:, 0, :, :].rearrange("p t n -> p (t n)")
            nc.scalar.activation(ho_sqj, bank(0, 2), ACT.Square).then_inc(sem["ho_sq"], 1)
            for g in range(NG + 1):
                if g < NG:
                    act.wait_ge(sem["sc_nm"], g + 1)
                    for i, h in enumerate(GROUPS[g % len(GROUPS)]):
                        c = g // len(GROUPS) * AH + h
                        a = nc.scalar.activation(a_s[g % 3][:, i, :], a_s[g % 3][:, i, :], ACT.Exp, bias=a_nm[:, c:c + 1])
                    a.then_inc(sem["sc_exp"], 1)
                if g >= 1 and (g - 1) % 2 == 0:
                    act.wait_ge(sem["eT_ps"], g)
                    nc.scalar.activation(a_eT[0].rearrange("p h j s -> p (h j s)"), bank(2), ACT.Copy).then_inc(sem["eT_act"], 1)
            act.wait_ge(sem["ho_ms"], 1)
            nc.scalar.activation(o_std, o_ms, ACT.Sqrt).then_inc(sem["ho_std"], 1)
            act.wait_ge(sem["mxT_ps"], 2)
            nc.scalar.activation(xT[:, 0:4, :].rearrange("p k s -> p (k s)"), bank(4, 2), ACT.Copy).then_inc(sem["mx_act"], 1)
            update((sem["acc_done"], 1))

            x_ready(1)
            norm(1, one_f("norm2"))
            act.wait_ge(sem["lg_nm"], 1)
            for t in range(TT):
                a = nc.scalar.activation(aff_e[:, t, :], bank(0)[:, t * NE:t * NE + NE], ACT.Exp, bias=r_nm[:, t:t + 1],
                                         accum_out=r_sum[:, t:t + 1])
            a.then_inc(sem["lg_exp"], 1)
            for k in range(0, KD, 2):
                act.wait_ge(sem["xin_ps"], k + 1)
                nc.scalar.activation(xin_all[:, k, :, :].rearrange("p e c -> p (e c)"), bank(4 + k % 4), ACT.Copy,
                                     scale=one_f("norm2")[:, k:k + 1]).then_inc(sem["xin_act"], 1)
            with act.Fori(0, NE) as e:
                act.wait_ge(sem["gate_ps"], 2 * e + 1)
                nc.scalar.activation(g4[0], bank(4), ACT.Copy).then_inc(sem["g4_done"], 1)
                act.wait_ge(sem["back_ps"], e + 1)
                nc.scalar.activation(back, bank(7)[:, 0:S], ACT.Copy).then_inc(sem["back_done"], 1)
                act.wait_ge(sem["gate_ps"], 2 * e + 2)
                nc.scalar.activation(g4[1], bank(4), ACT.Copy).then_inc(sem["g4_done"], 1)
                for c in range(2):
                    act.wait_ge(sem["sum_ps"], 2 * e + c + 1)
                    nc.scalar.activation(e_sil[c], bank(6 + c)[:, 0:4 * CAP], ACT.Silu).then_inc(sem["esil_done"], 1)
                act.wait_ge(sem["y_ps"], 2 * e + 1)
                nc.scalar.activation(y4[0], bank(4), ACT.Copy).then_inc(sem["y4_act"], 1)
            update((sem["scat_done"], NE))

            def ffn(L, f):
                q = 2 * L + f

                def silu(c, t):
                    act.wait_ge(sem["gu_ps"], t)
                    nc.scalar.activation(f_sil[c], bank(4 + c), ACT.Silu).then_inc(sem["sil_done"], 1)

                silu(0, STEPS * q + 1)
                with act.Fori(0, STEPS // 2) as i:
                    silu(1, STEPS * q + 2 + 2 * i)
                    silu(0, STEPS * q + 3 + 2 * i)
                update((sem["acc_done"], 3 * L + 2 + 2 * f))

            act.wait_ge(sem["late_in"], 80)
            with act.Fori(0, DEPTH2) as L:
                x_ready(3 * L + 2)
                act.wait_ge(sem["prm_ready"], L + 1)
                norm(3 * L + 2, pf("norm0"))
                act.wait_ge(sem["lru_u"], L + 1)
                nc.scalar.activation(lc_u, lc_ab, ACT.Exp, scale=-1.0).then_inc(sem["lru_c"], 1)
                act.wait_ge(sem["d_lamx"], L + 1)
                nc.scalar.activation(lamv[:, 2:4], lamv[:, 0:2], ACT.Exp).then_inc(sem["d_lame"], 1)
                ffn(L, 0)

                x_ready(3 * L + 3)
                norm(3 * L + 3, pf("norm1"))
                act.wait_ge(sem["z2_ready"], 6 * L + 1)
                nc.scalar.activation(scbc.rearrange("p c s -> p (c s)"), bank(0, 2), ACT.Copy).then_inc(sem["z2_0"], 1)
                act.wait_ge(sem["z2_ready"], 6 * L + 3)
                nc.scalar.activation(lgate.rearrange("p c s -> p (c s)"), bank(4), ACT.Copy).then_inc(sem["z2_2"], 1)
                act.wait_ge(sem["z2_ready"], 6 * L + 4)
                nc.scalar.activation(qT2.rearrange("p c s -> p (c s)"), bank(6, 2), ACT.Copy, scale=DM ** -0.5)\
                    .then_inc(sem["z2_q"], 1)
                act.wait_ge(sem["z2_ready"], 6 * L + 5)
                nc.scalar.activation(kT2.rearrange("p c s -> p (c s)"), bank(0, 2), ACT.Copy).then_inc(sem["z2_k"], 1)
                act.wait_ge(sem["lru_ps"], L + 1)
                for b, g, name in ((5, rg, "ba"), (4, ig, "bx")):
                    for c in range(2):
                        a = nc.scalar.activation(g[:, c, :], bank(b)[:, c * S:c * S + S], ACT.Sigmoid, bias=pf(name, c))
                a.then_inc(sem["lru_gates"], 1)
                act.wait_ge(sem["gelu_in"], L + 1)
                nc.scalar.activation(lg, lg, ACT.Tanh, scale=GELU_C).then_inc(sem["gelu_t"], 1)
                act.wait_ge(sem["lru_gates"], L + 1)
                act.wait_ge(sem["lru_b"], L + 1)
                for c in range(2):
                    nc.scalar.activation(lm[:, c, :], rg[:, c, :], ACT.Tanh, scale=lc_n[:, c:c + 1])
                for c in range(2):
                    a = nc.scalar.activation(la[:, c, :], rg[:, c, :], ACT.Exp, scale=lc_c[:, c:c + 1])
                a.then_inc(sem["lru_a"], 1)
                act.wait_ge(sem["lru_m"], L + 1)
                nc.scalar.activation(lm, lm, ACT.Sqrt).then_inc(sem["lru_sq"], 1)
                for g in range(5):
                    if g < 4:
                        act.wait_ge(sem["d_nmx"], 4 * L + g + 1)
                        n = P * (g // 2 + 1)
                        for m in range(2):
                            for i in range(2):
                                c = 4 * g + 2 * m + i
                                e_g = d_e[:, g % 2, m, i, 0:n]
                                a = nc.scalar.activation(e_g, e_g, ACT.Exp, bias=d_nm[:, c:c + 1], accum_out=d_den[:, c:c + 1])
                        a.then_inc(sem["d_exp"], 1)
                    if g >= 1:
                        act.wait_ge(sem["dT_ps"], 4 * L + g)
                        if g >= 2:
                            act.wait_ge(sem["do_ps"], 4 * L + g - 1)
                        n = (g - 1) // 2 + 1
                        nc.scalar.activation(d_aT[:, :, 0:n, :], bank(2 + (g - 1) % 2).rearrange("p (h j s) -> p h j s", h=2, j=2)
                                             [:, :, 0:n, :], ACT.Copy).then_inc(sem["dT_done"], 1)
                act.wait_ge(sem["do_ps"], 4 * L + 4)
                nc.scalar.activation(f_buf[:, 0:1024], bank(0, 2), ACT.Square).then_inc(sem["do_sq"], 1)
                act.wait_ge(sem["do_ms"], L + 1)
                nc.scalar.activation(d_std[:, 0:8], d_ms[:, 0:8], ACT.Sqrt).then_inc(sem["do_std"], 1)
                update((sem["acc_done"], 3 * L + 3))

                x_ready(3 * L + 4)
                norm(3 * L + 4, pf("norm2"))
                ffn(L, 1)

            x_ready(3 * DEPTH2 + 2)
            for t in range(TT):
                a = nc.scalar.activation(xn[:, t, :], x[:, t, :], ACT.Square, accum_out=n_ss[:, t:t + 1])
            a.then_inc(sem["sq_done"], 1)
            act.wait_ge(sem["ms_ready"], 3 * DEPTH2 + 3)
            nc.scalar.activation(n_std, n_ms, ACT.Sqrt).then_inc(sem["std_ready"], 1)

        @block.vector
        def _(dve):
            ch = Chain(dve, sem["dve_chain"])

            def mean_eps(out, ss, width, eps):
                return dve.tensor_scalar(out, ss, 1.0 / width, eps, ALU.mult, ALU.add)

            def norm(n, weight):
                dve.wait_ge(sem["sq_done"], n + 1)
                mean_eps(n_ms, n_ss, D, EPS).then_inc(sem["ms_ready"], 1)
                dve.wait_ge(sem["std_ready"], n + 1)
                dve.reciprocal(n_rstd, n_std).then_inc(sem["rstd_ready"], 1)
                dve.wait_ge(sem["rstd_ready"], n + 1)
                dve.tensor_scalar(xn[:, 0, :], x[:, 0, :], n_rstd[:, 0:1], None, ALU.mult).then_inc(sem["xn_dve"], 1)
                for k in range(4, KD):
                    if k % 2 == 0:
                        dve.wait_ge(sem["xnT_ps"], 4 * n + k // 2 + 1)
                    v = dve.tensor_scalar(xT[:, k, :], bank(4 + k // 2)[:, (k % 2) * S:(k % 2) * S + S],
                                          weight[:, k:k + 1], None, ALU.mult)
                v.then_inc(sem["xT_dve"], 1)

            def update(done):
                dve.wait_ge(done[0], done[1])
                dve.tensor_copy(x[:, 1, :], bank(2, 2)).then_inc(sem["x_dve"], 1)

            dve.wait_ge(sem["one_in"], 16)
            lbp = one_f("lb")
            ch.link(dve.tensor_tensor(lbm, lbp[:, 0:8], lbp[:, 8:16], ALU.max))
            dve.tensor_tensor(lbe[:, 0:8], lbp[:, 0:8], lbm, ALU.subtract)
            dve.tensor_tensor(lbe[:, 8:16], lbp[:, 8:16], lbm, ALU.subtract).then_inc(sem["lb_max"], 1)
            dve.wait_ge(sem["x_in"], 16)
            norm(0, one_f("norm1"))
            dve.wait_ge(sem["lb_exp"], 1)
            ch.link(dve.tensor_tensor(lbr, lbe[:, 0:8], lbe[:, 8:16], ALU.add))
            ch.link(dve.reciprocal(lbr, lbr))
            ch.link(dve.tensor_tensor(lb, lbe[:, 0:8], lbr, ALU.mult))
            ch.link(dve.tensor_scalar(oml, lb, -1.0, 1.0, ALU.mult, ALU.add))
            dve.tensor_scalar(lb, lb, LN_LEAST, None, ALU.max).then_inc(sem["lb_done"], 1)

            dve.wait_ge(sem["lb_done"], 1)
            for d, (k_raw, free) in enumerate(((kf, sem["z_hf"]), (kb, sem["z_hb"]))):
                dve.wait_ge(free, 1)
                for h in range(HH):
                    v = dve.tensor_scalar(k_raw[:, h, :], k_raw[:, h, :], oml[:, d * HH + h:d * HH + h + 1], None, ALU.mult)
                v.then_inc(sem["k_scaled"], 1)
            lf = lev_e[0].rearrange("p (d h n) -> p d h n", d=2, h=HH)
            dve.wait_ge(sem["masks_zero"], 2)
            dve.wait_ge(sem["gate_lf"], 1)
            for h in range(HH):
                ch.step(dve.tensor_tensor_scan(bc[:, h, :], ones_s, lf[:, 0, h, :], 0.0, ALU.mult, ALU.add))
            dve.wait_ge(sem["gate_lf"], 2)
            for h in range(HH):
                ch.step(dve.tensor_tensor_scan(rc[:, h, ::-1], ones_s, lf[:, 1, h, ::-1], 0.0, ALU.mult, ALU.add))
            ch.settle()

            def exponents(i):
                w = LEVELS[i]
                n = HH * S // (2 * w)
                if i >= 2:
                    dve.wait_ge(sem["lev_k"], i - 1)
                    dve.wait_ge(sem["lev_q"], i - 1)
                eq = lev_e[i % 2][:, 0:HH * S].rearrange("p (n f w) -> p n f w", n=n, f=2)
                ek = lev_e[i % 2][:, HH * S:2 * HH * S].rearrange("p (n f w) -> p n f w", n=n, f=2)
                b = bc.rearrange("p h s -> p (h s)").rearrange("p (n f w) -> p n f w", n=n, f=2)
                r = rc.rearrange("p h s -> p (h s)").rearrange("p (n f w) -> p n f w", n=n, f=2)
                b_end = b[:, :, 0, w - 1:w].to_broadcast([P, n, w])
                r_end = r[:, :, 1, 0:1].to_broadcast([P, n, w])
                dve.tensor_tensor(eq[:, :, 1, :], b[:, :, 1, :], b_end, ALU.subtract)
                dve.tensor_tensor(ek[:, :, 0, :], b_end, b[:, :, 0, :], ALU.subtract)
                dve.tensor_tensor(eq[:, :, 0, :], r[:, :, 0, :], r_end, ALU.subtract)
                dve.tensor_tensor(ek[:, :, 1, :], r_end, r[:, :, 1, :], ALU.subtract).then_inc(sem["lev_sub"], 1)

            def decayed_q(i):
                dve.wait_ge(sem["lev_exp"], i + 1)
                if i >= 1:
                    dve.wait_ge(sem["lev_ps"], i)
                dve.tensor_tensor(lev_qk[:, 0:HH * S], hq.rearrange("p h s -> p (h s)"), lev_e[i % 2][:, 0:HH * S],
                                  ALU.mult).then_inc(sem["lev_q"], 1)

            def put(i):
                dve.wait_ge(sem["lev_ps"], i + 1)
                if i == 0:
                    dve.tensor_copy(at_off.rearrange("p h t c -> p (h t c)"), bank(0, 2)).then_inc(sem["lev_put"], 1)
                else:
                    dve.wait_ge(sem["lev_put"], i)
                    mask = masks[:, i - 1, :].bitcast(U32).unsqueeze(1).to_broadcast([P, HH * TT, P])
                    dve.copy_predicated(at_diag.rearrange("p h t c -> p (h t) c"), mask,
                                        bank(0, 2).rearrange("p (n c) -> p n c", c=P)).then_inc(sem["lev_put"], 1)

            exponents(0)
            exponents(1)
            dve.wait_ge(sem["masks_zero"], 2)
            dve.wait_ge(sem["band_in"], 48)
            for i in range(NLEV):
                decayed_q(i)
                if i >= 1:
                    put(i - 1)
                if i + 2 < NLEV:
                    exponents(i + 2)
                if i == 0:
                    dve.wait_ge(sem["qk_sq"], 2)
                    ch.link(dve.tensor_reduce(qk_ss, sqj.rearrange("p c t n -> p (c t n)").rearrange("p (h d) -> p h d", d=AD),
                                              AX.X, ALU.add))
                    mean_eps(qk_ms, qk_ss, AD, EPS).then_inc(sem["qk_ms"], 1)
                    dve.wait_ge(sem["qk_std"], 1)
                    ch.link(dve.reciprocal(qk_rstd, qk_std))
                    for c, (b, dst, free) in enumerate(((2, aq_tok, sem["z_q"]), (4, ak_tok, sem["z_k"]))):
                        rstd = qk_rstd[:, 16 * c:16 * c + 16].unsqueeze(2).to_broadcast([P, 16, AD])
                        dve.tensor_tensor(dst.rearrange("p t n -> p (t n)").rearrange("p (h d) -> p h d", d=AD),
                                          bank(b, 2).rearrange("p (h d) -> p h d", d=AD), rstd, ALU.mult).then_inc(free, 1)
                if i == 3:
                    dve.wait_ge(sem["z_ready"], 7)
                    dve.tensor_copy(hi_tok.rearrange("p t n -> p (t n)"), bank(2, 2)).then_inc(sem["z_hi"], 1)
            put(NLEV - 1)
            put(NLEV)
            dve.wait_ge(sem["qkT_ps"], 1)
            dve.tensor_scalar(qT.rearrange("p c s -> p (c s)"), bank(2, 2), one_f("q"), AD ** -0.5, ALU.mult, ALU.mult)\
                .then_inc(sem["qT_done"], 1)

            def maxima(g):
                t = g // len(GROUPS)
                dve.wait_ge(sem["sc_ps"], g + 1)
                if g >= 3:
                    dve.wait_ge(sem["eT_ps"], g - 2)
                for i, h in enumerate(GROUPS[g % len(GROUPS)]):
                    c = t * AH + h
                    ch.step(dve.tensor_tensor_reduce(a_s[g % 3][:, i, :], bank(6 + g % 2)[:, i * S:i * S + S],
                                                     abias[:, h, P * (1 - t):P * (1 - t) + S], 1.0, -3e38, ALU.add, ALU.max,
                                                     a_mx[:, c:c + 1]))
                c = t * AH + GROUPS[g % len(GROUPS)][0]
                ch.settle()
                dve.tensor_scalar(a_nm[:, c:c + 3:2], a_mx[:, c:c + 3:2], -1.0, None, ALU.mult).then_inc(sem["sc_nm"], 1)

            def weigh(g):
                t = g // len(GROUPS)
                dve.wait_ge(sem["sc_exp"], g + 1)
                for i, h in enumerate(GROUPS[g % len(GROUPS)]):
                    c = t * AH + h
                    v = dve.tensor_tensor_reduce(a_s[g % 3][:, i, :], a_s[g % 3][:, i, :], count[:, P * (1 - t):P * (1 - t) + S],
                                                 1.0, 0.0, ALU.mult, ALU.add, a_den[:, c:c + 1])
                v.then_inc(sem["sc_cnt"], 1)

            def outputs(t):
                dve.wait_ge(sem["sc_cnt"], (t + 1) * len(GROUPS))
                ch.link(dve.reciprocal(a_rden[:, t * AH:t * AH + AH], a_den[:, t * AH:t * AH + AH]))
                dve.wait_ge(sem["o_ps"], t + 1)
                rden = a_rden[:, t * AH:t * AH + AH].unsqueeze(2).to_broadcast([P, AH, AD])
                dve.tensor_tensor(mixed[:, t, 0:512].rearrange("p (h d) -> p h d", d=AD),
                                  bank(4 + t).rearrange("p (h d) -> p h d", d=AD), rden, ALU.mult).then_inc(sem["o_put"], 1)

            maxima(0)
            maxima(1)
            for g in range(NG):
                weigh(g)
                if g + 2 < NG:
                    maxima(g + 2)
                if g % 2 == 0 and g >= 2:
                    dve.wait_ge(sem["eT_ps"], g)
                    dve.tensor_copy(a_eT[1].rearrange("p h j s -> p (h j s)"), bank(3)).then_inc(sem["eT_dve"], 1)
            dve.wait_ge(sem["ho_sq"], 1)
            ch.link(dve.tensor_reduce(o_ss, sqj[:, 0, :, :].rearrange("p t n -> p (t n)").rearrange("p (h d) -> p h d", d=HD),
                                      AX.X, ALU.add))
            mean_eps(o_ms, o_ss, HD, EPS).then_inc(sem["ho_ms"], 1)
            dve.wait_ge(sem["eT_ps"], NG)
            dve.tensor_copy(a_eT[1].rearrange("p h j s -> p (h j s)"), bank(3)).then_inc(sem["eT_dve"], 1)
            dve.wait_ge(sem["ho_std"], 1)
            ch.link(dve.reciprocal(o_rstd, o_std))
            dve.wait_ge(sem["gs_done"], 1)
            dve.wait_ge(sem["z_q"], 1)
            for t in range(TT):
                o_t = mixed[:, t, 512:1024].rearrange("p (h d) -> p h d", d=HD)
                rstd = o_rstd[:, t * HH:t * HH + HH].unsqueeze(2).to_broadcast([P, HH, HD])
                ch.link(dve.tensor_tensor(o_t, bank(t).rearrange("p (h d) -> p h d", d=HD), rstd, ALU.mult))
                dve.tensor_tensor(o_t, o_t, gs_tok[:, t, :].rearrange("p (h d) -> p h d", d=HD), ALU.mult).then_inc(sem["ho_put"], 1)
            for t in range(TT):
                outputs(t)
            dve.wait_ge(sem["mxT_ps"], 4)
            dve.tensor_copy(xT[:, 4:KD, :].rearrange("p k s -> p (k s)"), bank(6, 2)).then_inc(sem["mx_dve"], 1)
            update((sem["acc_done"], 1))

            norm(1, one_f("norm2"))
            dve.wait_ge(sem["lg_ps"], 1)
            ch.link(dve.tensor_reduce(r_mx, bank(0)[:, 0:TT * NE].rearrange("p (t e) -> p t e", t=TT), AX.X, ALU.max))
            dve.tensor_scalar(r_nm, r_mx, -1.0, None, ALU.mult).then_inc(sem["lg_nm"], 1)
            dve.wait_ge(sem["lg_exp"], 1)
            ch.link(dve.reciprocal(r_rec, r_sum))
            for t in range(TT):
                v = dve.tensor_scalar(aff[:, t, :], aff_e[:, t, :], r_rec[:, t:t + 1], None, ALU.mult)
            v.then_inc(sem["aff_done"], 1)
            dve.wait_ge(sem["affT_ps"], 1)
            ch.link(dve.tensor_copy(topw, bank(1)[0:NE, 0:S]))
            for _ in range(CAP // 8):
                ch.link(dve.max(top8, topw))
                ch.link(dve.match_replace(topw, top8, topw, -1.0))
            ch.link(dve.tensor_scalar(chosen, topw, 0.0, None, ALU.is_lt))
            dve.wait_ge(sem["masks_zero"], 3)
            ch.link(dve.tensor_tensor_scan(place, ones_e, chosen, 0.0, ALU.mult, ALU.add))
            dve.tensor_tensor(place, place, chosen, ALU.mult).then_inc(sem["place_done"], 1)
            dve.wait_ge(sem["tb_ps"], 1)
            dve.tensor_tensor(tb_rows, bank(3)[0:2 * DH, 0:TBW + 1], tb_future, ALU.add).then_inc(sem["tb_rows_done"], 1)
            dve.wait_ge(sem["placeT_ps"], 1)
            ch.link(dve.tensor_copy(posT.rearrange("p t e -> p (t e)"), bank(2)[:, 0:TT * NE]))
            for t in range(TT):
                v = dve.tensor_tensor(hot[:, t, :, :], posT[:, t, :].unsqueeze(2).to_broadcast([P, NE, CAP]),
                                      rank.unsqueeze(1).to_broadcast([P, NE, CAP]), ALU.is_equal)
            v.then_inc(sem["hot_done"], 1)
            for k in range(1, KD, 2):
                dve.wait_ge(sem["xin_ps"], k + 1)
                dve.tensor_scalar(xin_all[:, k, :, :].rearrange("p e c -> p (e c)"), bank(4 + k % 4),
                                  one_f("norm2")[:, k:k + 1], None, ALU.mult).then_inc(sem["xin_dve"], 1)
            dve.wait_ge(sem["xin_act"], KD // 2)
            dve.wait_ge(sem["xin_dve"], KD // 2)
            dve.wait_ge(sem["hot_done"], 1)
            with dve.Fori(0, NE) as e:
                dve.tensor_scalar(xin, xin_all[:, :, bass.ds(e, 1), :].rearrange("p k e c -> p k (e c)"), 1.0, None, ALU.mult)\
                    .then_inc(sem["xe_ready"], 1)
                for t in range(TT):
                    v = dve.tensor_scalar(hot_e[:, t, :, :], hot[:, t, bass.ds(e, 1), :].to_broadcast([P, Q4, CAP]),
                                          aff[:, t, bass.ds(e, 1)], None, ALU.mult)
                v.then_inc(sem["hote_done"], 1)
                for c in range(2):
                    dve.wait_ge(sem["up_ps"], 2 * e + c + 1)
                    dve.tensor_copy(u4[c], bank(5)).then_inc(sem["u4_done"], 1)
                for c in range(2):
                    dve.wait_ge(sem["esil_done"], 2 * e + c + 1)
                    dve.tensor_tensor(hidT[:, 4 * c:4 * c + 4, :].rearrange("p k c -> p (k c)"), e_sil[c],
                                      bank(6 + c)[:, 4 * CAP:8 * CAP], ALU.mult).then_inc(sem["ehid_done"], 1)
                dve.wait_ge(sem["y_ps"], 2 * e + 2)
                dve.tensor_copy(y4[1], bank(5)).then_inc(sem["y4_dve"], 1)
            update((sem["scat_done"], NE))

            dve.wait_ge(sem["late_in"], 80)
            dve.wait_ge(sem["tb_in"], 16)
            ch.link(dve.tensor_copy(tb, tb_raw[:, :, ::-1]))

            def ffn(L, f):
                q = 2 * L + f

                def hidden(c, t):
                    dve.wait_ge(sem["sil_done"], t)
                    dve.scalar_tensor_tensor(f_hid[c].rearrange("p f s -> p (f s)"), f_sil[c], 0.5, bank(6 + c), ALU.mult, ALU.mult)\
                        .then_inc(sem["hid_done"], 1)

                hidden(0, STEPS * q + 1)
                with dve.Fori(0, STEPS // 2) as i:
                    hidden(1, STEPS * q + 2 + 2 * i)
                    hidden(0, STEPS * q + 3 + 2 * i)
                update((sem["acc_done"], 3 * L + 2 + 2 * f))

            before = ch.n
            with dve.Fori(0, DEPTH2) as L:
                ch.base, ch.n = dve.snap(LINKS * L + before), 0
                dve.tensor_scalar(prm, prm_all[:, bass.ds(L, 1), :].rearrange("p l n -> p (l n)"), 1.0, None, ALU.mult)\
                    .then_inc(sem["prm_ready"], 1)
                dve.wait_ge(sem["prm_ready"], L + 1)
                norm(3 * L + 2, pf("norm0"))
                ch.link(dve.tensor_scalar(lc_y, pf("lam"), -1.0, None, ALU.mult))
                dve.tensor_tensor(lc_ab, lc_y, pf("lam"), ALU.max).then_inc(sem["lru_u"], 1)
                for i, (a, b) in enumerate((("lq1", "lk1"), ("lq2", "lk2"))):
                    v = dve.tensor_tensor_reduce(lam_j, pf(a), pf(b), 1.0, 0.0, ALU.mult, ALU.add, lamv[:, i:i + 1])
                    ch.link(v) if i == 0 else v.then_inc(sem["d_lamx"], 1)
                dve.wait_ge(sem["lru_c"], L + 1)
                ch.link(dve.tensor_scalar(lc_den, lc_u, 2.0, None, ALU.add))
                ch.link(dve.reciprocal(lc_den, lc_den))
                ch.link(dve.tensor_tensor(lc_z, lc_u, lc_den, ALU.mult))
                ch.link(dve.tensor_tensor(lc_z2, lc_z, lc_z, ALU.mult))
                ch.link(dve.tensor_scalar(lc_p, lc_z2, 1.0 / (2 * LOG1P_TERMS - 1), None, ALU.mult))
                for i in range(LOG1P_TERMS - 2, -1, -1):
                    ch.link(dve.scalar_tensor_tensor(lc_p, lc_p, 1.0 / (2 * i + 1), lc_z2 if i else lc_z, ALU.add, ALU.mult))
                ch.link(dve.tensor_scalar(lc_y, lc_y, 0.0, None, ALU.max))
                ch.link(dve.scalar_tensor_tensor(lc_p, lc_p, 2.0, lc_y, ALU.mult, ALU.add))
                dve.tensor_scalar(lc_c, lc_p, -LRU_C, None, ALU.mult)
                dve.tensor_scalar(lc_n, lc_p, LRU_C, None, ALU.mult).then_inc(sem["lru_b"], 1)
                dve.wait_ge(sem["d_lame"], L + 1)
                ch.link(dve.tensor_tensor(lamv[:, 4:5], lamv[:, 3:4], lamv[:, 2:3], ALU.subtract))
                ch.step(dve.tensor_tensor(lamv[:, 5:6], lamv[:, 4:5], pf("lam0"), ALU.subtract))
                neg_lam = lamv[:, 5:6]
                ffn(L, 0)

                norm(3 * L + 3, pf("norm1"))
                dve.wait_ge(sem["pads_zero"], 2)
                dve.wait_ge(sem["z2_ready"], 6 * L + 2)
                dve.wait_ge(sem["z2_0"], L + 1)
                ch.step(dve.tensor_tensor(sc_pad[:, :, 2:2 + S], scbc[:, 2:4, :], bank(2).rearrange("p (c s) -> p c s", c=2), ALU.mult))
                dve.tensor_copy(lx_pad[:, :, 3:3 + S], bank(3).rearrange("p (c s) -> p c s", c=2)).then_inc(sem["z2_1"], 1)
                dve.wait_ge(sem["z2_1"], L + 1)
                for c in range(2):
                    ch.step(dve.tensor_scalar(xr[:, c, :], lx_pad[:, c, 0:S], pf("lruw", 4 * c), pf("lrub", c), ALU.mult, ALU.add))
                for k in range(1, 4):
                    ch.settle()
                    for c in range(2):
                        v = dve.scalar_tensor_tensor(xr[:, c, :], lx_pad[:, c, k:k + S], pf("lruw", 4 * c + k), xr[:, c, :],
                                                     ALU.mult, ALU.add)
                        if k < 3 or c == 0:
                            ch.step(v)
                v.then_inc(sem["lru_xr"], 1)
                ch.settle()
                for c in range(2):
                    ch.step(dve.tensor_scalar(yc[:, c, :], sc_pad[:, c, 0:S], pf("scw", 3 * c), None, ALU.mult))
                for k in range(1, 3):
                    ch.settle()
                    for c in range(2):
                        ch.step(dve.scalar_tensor_tensor(yc[:, c, :], sc_pad[:, c, k:k + S], pf("scw", 3 * c + k), yc[:, c, :],
                                                         ALU.mult, ALU.add))
                dve.wait_ge(sem["z2_2"], L + 1)
                ch.link(dve.tensor_tensor(lg, lgate, lgate, ALU.mult))
                ch.link(dve.tensor_scalar(lg, lg, 0.044715, 1.0, ALU.mult, ALU.add))
                dve.tensor_tensor(lg, lg, lgate, ALU.mult).then_inc(sem["gelu_in"], 1)
                dve.wait_ge(sem["gelu_t"], L + 1)
                ch.step(dve.scalar_tensor_tensor(lg, lg, 1.0, lgate, ALU.add, ALU.mult))
                dve.wait_ge(sem["lru_a"], L + 1)
                ch.link(dve.tensor_scalar(rg, lm, 1.0, None, ALU.add))
                ch.link(dve.reciprocal(rg, rg))
                ch.link(dve.scalar_tensor_tensor(lm, lm, 2.0, rg, ALU.mult, ALU.mult))
                dve.tensor_scalar(lm, lm, SQRT_LEAST, None, ALU.max).then_inc(sem["lru_m"], 1)
                dve.wait_ge(sem["lru_xr"], L + 1)
                ch.link(dve.tensor_tensor(ig, ig, xr, ALU.mult))
                dve.wait_ge(sem["lru_sq"], L + 1)
                ch.link(dve.tensor_tensor(lm, lm, ig, ALU.mult))
                for c in range(2):
                    ch.step(dve.tensor_tensor_scan(xr[:, c, :], la[:, c, :], lm[:, c, :], 0.0, ALU.mult, ALU.add))
                ch.settle()
                dve.wait_ge(sem["z2_ready"], 6 * L + 6)
                dve.tensor_copy(v2.rearrange("p t c -> p (t c)"), bank(2, 2)).then_inc(sem["z2_v"], 1)
                dve.tensor_tensor(xT[:, 4:6, :], yc, scbc[:, 0:2, :], ALU.mult).then_inc(sem["ysc_done"], 1)
                dve.scalar_tensor_tensor(xT[:, 6:8, :].rearrange("p c s -> p (c s)"), lg.rearrange("p c s -> p (c s)"), 0.5,
                                         xr.rearrange("p c s -> p (c s)"), ALU.mult, ALU.mult).then_inc(sem["ylru_done"], 1)

                def maxima2(g):
                    t, n = g // 2, P * (g // 2 + 1)
                    dve.wait_ge(sem["d_ps"], 4 * L + g + 1)
                    dve.memset(d_hold, 0.0)
                    for m in range(2):
                        for i in range(2):
                            h, c = 2 * (g % 2) + i, 4 * g + 2 * m + i
                            ch.step(dve.tensor_tensor_reduce(d_e[:, g % 2, m, i, 0:n], bank(6 - 2 * (g % 2) + m)[:, i * S:i * S + n],
                                                             tb[:, 2 * h + m, S - n:S], 1.0, -3e38, ALU.add, ALU.max, d_mx[:, c:c + 1]))
                    ch.settle()
                    dve.tensor_scalar(d_nm[:, 4 * g:4 * g + 4], d_mx[:, 4 * g:4 * g + 4], -1.0, None, ALU.mult).then_inc(sem["d_nmx"], 1)

                def combine(g):
                    n = P * (g // 2 + 1)
                    dve.wait_ge(sem["d_exp"], 4 * L + g + 1)
                    ch.link(dve.reciprocal(d_rd[:, 4 * g:4 * g + 4], d_den[:, 4 * g:4 * g + 4]))
                    ch.step(dve.tensor_scalar(d_c1[:, 2 * g:2 * g + 2], d_rd[:, 4 * g + 2:4 * g + 4], neg_lam, None, ALU.mult))
                    if g >= 1:
                        dve.wait_ge(sem["dT_ps"], 4 * L + g)
                    for i in range(2):
                        ch.step(dve.tensor_scalar(d_attn[:, i, 0:n], d_e[:, g % 2, 0, i, 0:n], d_rd[:, 4 * g + i:4 * g + i + 1],
                                                  None, ALU.mult))
                    ch.settle()
                    for i in range(2):
                        v = dve.scalar_tensor_tensor(d_attn[:, i, 0:n], d_e[:, g % 2, 1, i, 0:n], d_c1[:, 2 * g + i:2 * g + i + 1],
                                                     d_attn[:, i, 0:n], ALU.mult, ALU.add)
                    v.then_inc(sem["d_comb"], 1)

                maxima2(0)
                maxima2(1)
                for g in range(4):
                    combine(g)
                    if g + 2 < 4:
                        maxima2(g + 2)
                dve.wait_ge(sem["do_sq"], L + 1)
                ch.link(dve.tensor_reduce(d_ss[:, 0:8], f_buf[:, 0:1024].rearrange("p (h d) -> p h d", d=P), AX.X, ALU.add))
                mean_eps(d_ms[:, 0:8], d_ss[:, 0:8], P, SUBLN_EPS).then_inc(sem["do_ms"], 1)
                dve.wait_ge(sem["do_std"], L + 1)
                ch.link(dve.reciprocal(d_ss[:, 8:16], d_std[:, 0:8]))
                for t in range(TT):
                    v = dve.tensor_tensor(xn[:, t, 0:512].rearrange("p (h d) -> p h d", d=P),
                                          bank(t).rearrange("p (h d) -> p h d", d=P),
                                          d_ss[:, 8 + 4 * t:12 + 4 * t].unsqueeze(2).to_broadcast([P, DH, P]), ALU.mult)
                v.then_inc(sem["do_nrm"], 1)
                dve.wait_ge(sem["yT_ps"], L + 1)
                dve.tensor_scalar(xT[:, 0:4, :].rearrange("p k s -> p (k s)"), bank(4, 2), pf("subg"), pf("oml"), ALU.mult, ALU.mult)\
                    .then_inc(sem["yT_done"], 1)
                update((sem["acc_done"], 3 * L + 3))

                norm(3 * L + 4, pf("norm2"))
                ffn(L, 1)
            assert ch.n == LINKS, ch.n

            dve.wait_ge(sem["sq_done"], 3 * DEPTH2 + 3)
            mean_eps(n_ms, n_ss, D, EPS).then_inc(sem["ms_ready"], 1)
            dve.wait_ge(sem["std_ready"], 3 * DEPTH2 + 3)
            ch.base, ch.n = DEPTH2 * LINKS + before, 0
            ch.link(dve.reciprocal(n_rstd, n_std))
            for t in range(TT):
                dve.scalar_tensor_tensor(xn[:, t, :], x[:, t, :], n_rstd[:, t:t + 1], fin_row, ALU.mult, ALU.mult)\
                    .then_inc(sem["fin_put"], 1)

        @block.gpsimd
        def _(pool):
            pool.memset(at_diag, 0.0).then_inc(sem["masks_zero"], 1)
            pool.memset(ones_s, 1.0).then_inc(sem["masks_zero"], 1)
            e_q = HH * S
            for i in range(NLEV + 1):
                if i < NLEV:
                    pool.wait_ge(sem["lev_exp"], i + 1)
                if i == 0:
                    pool.wait_ge(sem["k_scaled"], 2)
                if i >= 1:
                    pool.wait_ge(sem["lev_ps"], i)
                if i < NLEV:
                    w = LEVELS[i]
                    n = HH * S // (2 * w)

                    def halves(a):
                        return a.rearrange("p (n f w) -> p n f w", n=n, f=2)

                    ek, kl = halves(lev_e[i % 2][:, e_q:2 * e_q]), halves(lev_qk[:, e_q:2 * e_q])
                    kf_n, kb_n = [halves(k.rearrange("p h s -> p (h s)")) for k in (kf, kb)]
                    pool.tensor_tensor(kl[:, :, 0, :], kf_n[:, :, 0, :], ek[:, :, 0, :], ALU.mult)
                    pool.tensor_tensor(kl[:, :, 1, :], kb_n[:, :, 1, :], ek[:, :, 1, :], ALU.mult).then_inc(sem["lev_k"], 1)
                else:
                    pool.tensor_tensor(lev_qk[:, e_q:2 * e_q], kf.rearrange("p h s -> p (h s)"),
                                       kb.rearrange("p h s -> p (h s)"), ALU.add).then_inc(sem["lev_k"], 1)
            pool.wait_ge(sem["z_hg"], 1)
            gs = gs_tok.rearrange("p t n -> p (t n)").rearrange("p (h d) -> p h d", d=HD)
            pool.tensor_tensor(gs, gs, one_f("onorm").unsqueeze(1).to_broadcast([P, TT * HH, HD]), ALU.mult).then_inc(sem["gs_done"], 1)
            pool.wait_ge(sem["acc_done"], 1)
            pool.memset(ones_e, 1.0).then_inc(sem["masks_zero"], 1)
            pool.wait_ge(sem["scat_done"], NE)
            pool.memset(sc_pad[:, :, 0:2], 0.0).then_inc(sem["pads_zero"], 1)
            pool.memset(lx_pad[:, :, 0:3], 0.0).then_inc(sem["pads_zero"], 1)


def kernel(**inputs):
    import concourse.bacc as bacc
    from concourse.bass_utils import run_bass_kernel_spmd

    a = {k: np.asarray(v) for k, v in inputs.items()}
    small, band, onehot, future = const_arrays()

    def cols(v):
        return np.reshape(v, (-1, P)).T

    def rows(v):
        return np.broadcast_to(np.reshape(v, (1, -1)), (P, v.size))

    def taps(w):
        return np.reshape(np.transpose(np.reshape(w, (w.shape[0], -1, P)), (2, 1, 0)), (P, -1))

    def diagonal(w):
        out = np.zeros((P, 2, P), np.float32)
        for i in range(4):
            r = 64 * (i % 2)
            out[r:r + 64, i // 2, r:r + 64] = w[i]
        return out.reshape(P, -1)

    lbs = [cols(a[n][r]) for r in range(2) for n in ("hgrn_lb_fwd", "hgrn_lb_bwd")]
    router = np.reshape(np.transpose(np.reshape(a["w_router"][0], (KD, P, NE)), (1, 0, 2)), (P, -1))
    one = np.concatenate([cols(a["norm1_w"][0]), cols(a["norm2_w"][0]),
                          np.tile(a["attn_q_norm_w"][0], 2)[:, None], np.tile(a["attn_k_norm_w"][0], 2)[:, None],
                          *lbs, rows(a["hgrn_out_norm_w"][0]), router], axis=1)
    layers = []
    for l in range(DEPTH2):
        lam0 = 0.8 - 0.6 * math.exp(-0.3 * l)
        layers.append(np.concatenate(
            [cols(a[n + "_norm_2"][l]) for n in ("ffn1", "mix", "ffn2")]
            + [rows(a[n + "_2"][l]) for n in ("lam_q1", "lam_k1", "lam_q2", "lam_k2")]
            + [cols(a["subln_gain_2"][l]), np.full((P, 1), lam0, np.float32), np.full((P, 1), 1.0 - lam0, np.float32),
               taps(a["sc_conv_w_2"][l]), taps(a["lru_conv_w_2"][l]), cols(a["lru_conv_b_2"][l]), cols(a["lru_ba_2"][l]),
               cols(a["lru_bx_2"][l]), cols(a["lru_lambda_2"][l]), diagonal(a["lru_wa_2"][l]), diagonal(a["lru_wx_2"][l])],
            axis=1))
    feed = [("x", a["x"][0]), ("w_in", a["w_in"][0]), ("w_out", a["w_out"][0]), ("w_expert_gate", a["w_expert_gate"][0]),
            ("w_expert_up", a["w_expert_up"][0]), ("w_expert_down", a["w_expert_down"][0]), ("rel_bias", a["rel_bias_2"]),
            ("ffn1_gate", a["ffn1_gate_2"]), ("ffn1_up", a["ffn1_up_2"]), ("ffn1_down", a["ffn1_down_2"]),
            ("w_in_2", a["w_in_2"]), ("w_out_2", a["w_out_2"]),
            ("ffn2_gate", a["ffn2_gate_2"]), ("ffn2_up", a["ffn2_up_2"]), ("ffn2_down", a["ffn2_down_2"]),
            ("small_constants", small), ("band_constants", band), ("bucket_constants", onehot), ("future_constants", future),
            ("first_block_params", one), ("layer_params", np.stack(layers)), ("final_norm", rows(a["final_norm_2"]))]
    nc = bacc.Bacc("TRN2", target_bir_lowering=False, num_devices=1)
    arrays, args = {}, []
    for name, v in feed:
        v = np.ascontiguousarray(v, dtype=np.float32)
        arrays[name] = v
        args.append(nc.dram_tensor(name, v.shape, F32, kind="ExternalInput").ap())
    args.append(nc.dram_tensor("out", (S, D), F32, kind="ExternalOutput").ap())
    two_blocks(nc, *args)
    r = run_bass_kernel_spmd(nc, [arrays], core_ids=[0])
    return r.results[0]["out"].reshape(1, S, D)
```

```python
import math
from contextlib import ExitStack

import numpy as np

import concourse.bass as bass
from concourse import mybir

F32 = mybir.dt.float32
F32R = mybir.dt.float32r
U32 = mybir.dt.uint32
ALU = mybir.AluOpType
ACT = mybir.ActivationFunctionType
AX = mybir.AxisListType

P = 128
S = 256
D = 1024
TT = S // P
KD = D // P
BANK = 512
EPS = 1e-6

AH, AD = 8, 64
HH, HD = 4, 128
PATTERNS = ((128, 1), (512, 4), (2048, 16))
NE = 16
CAP = 2 * S // NE
FE = 1024
Q4 = P // CAP
LN_LEAST = 2.0 ** -64
SQRT_LEAST = 2.0 ** -116
LEVELS = [S >> (i + 1) for i in range(int(math.log2(S)))]

DEPTH2 = 2
DH, DM = 4, 64
NBUCKET, MAXDIST = 32, 128
SUBLN_EPS = 1e-5
LRU_C = 8.0
GELU_C = math.sqrt(2.0 / math.pi)
DFF = 2816
FS = 256
STEPS = DFF // FS
PIECE = KD * FS
Z_COLS = [1536, 1792, 2048, 2304, 2560, 0, 256, 512, 768, 1024, 1280]
O_ROWS = [512, 768, 0, 256]
MIX_N = (len(Z_COLS) + len(O_ROWS)) // 3
LAYER_N = 2 * STEPS + MIX_N
TBW = P + S - 1
LOG1P_TERMS = 8
NEG = -1e30
LINKS = 83


def fields(*sizes):
    at, out = 0, {}
    for name, n in sizes:
        out[name] = (at, at + n)
        at += n
    return out, at


CONST, CONST_W = fields(("ident", P), ("fold", CAP), ("rank", CAP))
BAND_W = P + S
BAND, BAND_N = fields(("bias", AH * BAND_W), ("count", BAND_W), ("mask", len(LEVELS) * P))
ONE, ONE_N = fields(("norm1", KD), ("norm2", KD), ("q", 1), ("k", 1), ("lb", 4 * HH), ("onorm", HD),
                    ("router", KD * NE))
PRM, PRM_N = fields(("norm0", KD), ("norm1", KD), ("norm2", KD), ("lq1", DM), ("lk1", DM), ("lq2", DM),
                    ("lk2", DM), ("subg", 1), ("lam0", 1), ("oml", 1), ("scw", 6), ("lruw", 8), ("lrub", 2),
                    ("ba", 2), ("bx", 2), ("lam", 2), ("wa", 2 * P), ("wx", 2 * P))


def const_arrays():
    small = np.zeros((P, CONST_W), np.float32)
    small[:, CONST["ident"][0]:CONST["ident"][1]] = np.eye(P)
    small[:, CONST["fold"][0]:CONST["fold"][1]] = np.tile(np.eye(CAP), (Q4, 1))
    small[:, CONST["rank"][0]:CONST["rank"][1]] = np.arange(1, CAP + 1)
    dist = np.abs(P + np.arange(P)[:, None] - np.arange(BAND_W)[None, :])
    count = sum(((dist % dil == 0) & (dist // dil <= win // (2 * dil))).astype(np.float32) for win, dil in PATTERNS)
    slopes = np.exp2(-8.0 * np.arange(1, AH + 1, dtype=np.float32) / AH)
    bias = [np.where(count > 0, -s * dist, NEG) for s in slopes]
    s_at, t_at = np.arange(P)[:, None], np.arange(P)[None, :]
    masks = [(s_at // (2 * w) == t_at // (2 * w)) & (s_at // w != t_at // w) for w in LEVELS[1:]] + [s_at == t_at]
    band = np.concatenate(bias + [count] + masks, axis=1).astype(np.float32)
    n = np.arange(TBW + 1) - (P - 1)
    exact = NBUCKET // 2
    large = exact + (np.log(np.maximum(n, 1).astype(np.float32) / exact) / math.log(MAXDIST / exact)
                     * (NBUCKET - exact)).astype(np.int32)
    bucket = np.where(n < exact, n, np.minimum(large, NBUCKET - 1))
    onehot = ((bucket[None, :] == np.arange(NBUCKET)[:, None]) & (n >= 0)).astype(np.float32)
    future = np.tile(np.where(n < 0, NEG, 0.0), (2 * DH, 1)).astype(np.float32)
    return small, band, onehot, future


class Chain:

    def __init__(self, eng, counter):
        self.eng, self.counter, self.n, self.base = eng, counter, 0, 0

    def step(self, ins):
        ins.then_inc(self.counter, 1)
        self.n += 1

    def settle(self):
        self.eng.wait_ge(self.counter, self.base + self.n)

    def link(self, ins):
        self.step(ins)
        self.settle()


def two_blocks(nc, x_in, w_in, w_out, wg, wu, wd, relb, f1g, f1u, f1d, w_in2, w_out2, f2g, f2u, f2d,
               const, band, onehot, future, one, prm_in, fin_w, out):
    with ExitStack() as ctx:
        def sb(name, n):
            return ctx.enter_context(nc.sbuf_tensor(name, [P, n], F32))

        SLOT = KD * 512
        with nc.sbuf_tensor("ring", [P, 6 * SLOT], F32) as ring:
            pass

        def sb_r(name, n):
            return ctx.enter_context(nc.sbuf_tensor(name, [P, n], F32R))

        raw_sb = sb("raw_sb", 3 * PIECE)
        wh_sb, wl_sb = sb_r("wh_sb", 3 * PIECE), sb_r("wl_sb", 3 * PIECE)
        xTh_sb, xTl_sb = sb_r("xTh_sb", KD * S), sb_r("xTl_sb", KD * S)
        hidh_sb, hidl_sb = sb_r("hidh_sb", 1024), sb_r("hidl_sb", 1024)
        x_sb = sb("x_sb", TT * D)
        xT_sb = sb("xT_sb", KD * S)
        xn_sb = sb("xn_sb", TT * D)
        const_sb = sb("const_sb", CONST_W)
        one_sb = sb("one_sb", ONE_N)
        stat = sb("stat", 256)
        WORK = 19300
        work = sb("work", WORK)
        ps = ctx.enter_context(nc.psum_tensor("ps", [P, 8 * BANK], F32))
        tb_dram = nc.dram_tensor("rel_bias_band", [2 * DH, TBW + 1], F32, kind="Internal")

        x = x_sb[:, :].rearrange("p (t d) -> p t d", t=TT)
        xT = xT_sb[:, :].rearrange("p (k s) -> p k s", k=KD)
        xn = xn_sb[:, :].rearrange("p (t d) -> p t d", t=TT)
        ident = const_sb[:, CONST["ident"][0]:CONST["ident"][1]]
        fold = const_sb[:, CONST["fold"][0]:CONST["fold"][1]]
        rank = const_sb[:, CONST["rank"][0]:CONST["rank"][1]]

        def slot(s, n=512):
            return ring[:, s * SLOT:s * SLOT + KD * n].rearrange("p (k n) -> p k n", k=KD)

        def bank(b, n=1):
            return ps[:, b * BANK:(b + n) * BANK]

        def one_f(name):
            return one_sb[:, ONE[name][0]:ONE[name][1]]

        at = [0]

        def st(n):
            at[0] += n
            assert at[0] <= 256
            return stat[:, at[0] - n:at[0]]

        n_ss, n_ms, n_std, n_rstd, hold = st(TT), st(TT), st(TT), st(TT), st(4)
        lbm, lbe, lbr, lb, oml = st(8), st(16), st(8), st(8), st(8)
        qk_ss, qk_ms, qk_std, qk_rstd = st(32), st(32), st(32), st(32)

        def region(buf, n, start=0):
            pos = [start]

            def take(size):
                pos[0] += size
                assert pos[0] <= n, (pos[0], n)
                return buf[:, pos[0] - size:pos[0]]
            return take

        t1 = region(work, WORK)
        hq, kf, kb, bc, rc = [t1(HH * S).rearrange("p (h s) -> p h s", h=HH) for _ in range(5)]
        v_tok, hi_tok, gs_tok = [t1(TT * 512).rearrange("p (t c) -> p t c", t=TT) for _ in range(3)]
        qT, kT = [t1(4 * S).rearrange("p (c s) -> p c s", c=4) for _ in range(2)]
        at_diag, at_off = [t1(HH * TT * P).rearrange("p (h t c) -> p h t c", h=HH, t=TT) for _ in range(2)]
        a_s = [t1(2 * S).rearrange("p (h s) -> p h s", h=2) for _ in range(3)]
        a_eT = [t1(2 * S).rearrange("p (h j s) -> p h j s", h=2, j=TT) for _ in range(2)]
        count = t1(BAND_W)
        masks = t1(len(LEVELS) * P).rearrange("p (l s) -> p l s", l=len(LEVELS))
        a_st = t1(4 * 16)
        a_mx, a_nm, a_den, a_rden = [a_st[:, 16 * i:16 * i + 16] for i in range(4)]
        o_st = t1(4 * 8)
        o_ss, o_ms, o_std, o_rstd = [o_st[:, 8 * i:8 * i + 8] for i in range(4)]
        ones_s = t1(S)
        r1 = region(ring, 3 * SLOT)
        lev_e = [r1(2 * HH * S) for _ in range(2)]
        lev_qk = r1(2 * HH * S)
        sqj = r1(2 * TT * 512).rearrange("p (c t n) -> p c t n", c=2, t=TT)
        abias = r1(AH * BAND_W).rearrange("p (h i) -> p h i", h=AH)
        aq_tok = xn_sb[:, 0:1024].rearrange("p (t c) -> p t c", t=TT)
        ak_tok = xn_sb[:, 1024:2048].rearrange("p (t c) -> p t c", t=TT)
        mixed = xn

        LATE = 2 * PRM_N + 2 * DH * S + D + (TBW + 1) * 3 + 2 * DH
        t2 = region(work, WORK - LATE)
        xin_all = t2(KD * NE * CAP).rearrange("p (k e c) -> p k e c", k=KD, e=NE)
        hot = t2(TT * NE * CAP).rearrange("p (t e c) -> p t e c", t=TT, e=NE)
        aff = t2(TT * NE).rearrange("p (t e) -> p t e", t=TT)
        aff_e = t2(TT * NE).rearrange("p (t e) -> p t e", t=TT)
        posT = t2(TT * NE).rearrange("p (t e) -> p t e", t=TT)
        r_mx, r_nm, r_sum, r_rec = t2(TT), t2(TT), t2(TT), t2(TT)
        affT, topw, chosen, place, ones_e = [t2(S)[0:NE, :] for _ in range(5)]
        top8 = t2(8)[0:NE, :]
        hot_e = t2(TT * P).rearrange("p (t j c) -> p t j c", t=TT, j=Q4)
        back = t2(S)
        xin = t2(KD * CAP).rearrange("p (k c) -> p k c", k=KD)
        g4, u4, y4 = [[t2(512) for _ in range(2)] for _ in range(3)]
        e_sil = [t2(4 * CAP) for _ in range(2)]
        hidT = t2(KD * CAP).rearrange("p (k c) -> p k c", k=KD)

        t3 = region(work, WORK, WORK - LATE)
        prm_all = t3(2 * PRM_N).rearrange("p (l n) -> p l n", l=2)
        tb_raw = t3(2 * DH * S).rearrange("p (h i) -> p h i", h=2 * DH)
        fin_row = t3(D)
        tb_rows, tb_future = t3(TBW + 1)[0:2 * DH, :], t3(TBW + 1)[0:2 * DH, :]
        tb_onehot, tb_rel = t3(TBW + 1)[0:NBUCKET, :], t3(2 * DH)[0:NBUCKET, :]
        t4 = region(work, WORK - LATE)
        prm = t4(PRM_N)
        tb = t4(2 * DH * S).rearrange("p (h i) -> p h i", h=2 * DH)
        f_buf = t4(4 * 512)
        f_sil = [f_buf[:, 512 * i:512 * i + 512] for i in range(2)]
        f_hid = [f_buf[:, 1024 + 512 * i:1536 + 512 * i].rearrange("p (f s) -> p f s", f=2) for i in range(2)]
        d_e = f_buf.rearrange("p (g m h s) -> p g m h s", g=2, m=2, h=2)
        raw_place = tb_raw.rearrange("p h i -> p (h i)")
        qT2, scbc = [raw_place[:, 1024 * i:1024 * i + 1024].rearrange("p (c s) -> p c s", c=4) for i in range(2)]
        kT2 = t4(4 * S).rearrange("p (c s) -> p c s", c=4)
        v2 = t4(TT * 512).rearrange("p (t c) -> p t c", t=TT)
        sc_pad = t4(2 * (S + 2)).rearrange("p (c s) -> p c s", c=2)
        lx_pad = t4(2 * (S + 3)).rearrange("p (c s) -> p c s", c=2)
        lgate, xr, rg, ig, la, lm = [t4(2 * S).rearrange("p (c s) -> p c s", c=2) for _ in range(6)]
        y_cl = t4(4 * S).rearrange("p (c s) -> p c s", c=4)
        yc, lg = y_cl[:, 0:2, :], y_cl[:, 2:4, :]
        d_attn, d_aT = t4(2 * S).rearrange("p (h s) -> p h s", h=2), t4(2 * S).rearrange("p (h j s) -> p h j s", h=2, j=2)
        lc = t4(32)
        lc_y, lc_ab, lc_u, lc_den, lc_z, lc_z2, lc_p, lc_c, lc_n = [lc[:, 2 * i:2 * i + 2] for i in range(9)]
        lamv = t4(8)
        d_st = t4(8 * 16)
        d_mx, d_nm, d_den, d_rd, d_c1, d_ss, d_ms, d_std = [d_st[:, 16 * i:16 * i + 16] for i in range(8)]
        lam_j = t4(DM)
        raw, wh, wl = [[b[:, j * PIECE:(j + 1) * PIECE] for j in range(3)] for b in (raw_sb, wh_sb, wl_sb)]

        def by_cols(w):
            return w.rearrange("p (k n) -> p k n", k=KD)

        def by_rows(w):
            return w.rearrange("p (k n) -> p k n", n=D)

        xTh, xTl = [b[:, :].rearrange("p (k s) -> p k s", k=KD) for b in (xTh_sb, xTl_sb)]
        hidh, hidl = [[b[:, 512 * c:512 * c + 512].rearrange("p (f s) -> p f s", f=2) for c in range(2)]
                      for b in (hidh_sb, hidl_sb)]

        def pf(name, i=None):
            a, b = PRM[name]
            return prm[:, a:b] if i is None else prm[:, a + i:a + i + 1]

        names = """x_in const_in one_in band_in w1_in0 w1_in1 w1_in2 ex_in0 ex_in1 ex_in2 ex_in3 ex_in4 ex_in5
            mxT_ps mx_act mx_dve k_scaled late_in tb_out tb_in raw_in0 raw_in1 raw_in2 fin_out
            sq_done ms_ready std_ready rstd_ready xn_dve xn_act xnT_ps xT_act xT_dve acc_done x_act x_dve
            z_ready z_hq z_hf z_hb z_q z_k z_v z_hi z_hg
            lb_max lb_exp lb_done gate_sg gate_lf lev_sub lev_exp lev_q lev_k lev_ps lev_put
            qk_sq qk_ms qk_std qkT_ps qT_done kT_done
            sc_ps sc_nm sc_exp sc_cnt eT_ps eT_act eT_dve o_ps o_put ho_ps ho_sq ho_ms ho_std ho_put gs_done
            masks_zero lg_ps lg_nm lg_exp aff_done affT_ps place_done placeT_ps hot_done xin_ps xin_act xin_dve
            xe_ready hote_done used0 used1 used2 back_ps g4_done u4_done back_done sum_ps esil_done ehid_done
            y4_act y4_dve stage_done tb_ps tb_rows_done tb_done
            raw_free0 raw_free1 raw_free2 w_hi xT_hi xT_lo prm_ready sil_done hid_t hid_h hid_done
            z2_0 z2_1 z2_2 z2_q z2_k z2_v
            lru_u lru_c lru_xr lru_ps lru_gates lru_a lru_m lru_sq lru_b gelu_in gelu_t y_done
            d_lamx d_lame d_ps d_nmx d_exp d_comb dT_ps dT_done do_ps do_sq do_ms do_std do_nrm yT_ps
            fin_put dve_chain pads_zero""".split()
        sem = {n: ctx.enter_context(nc.semaphore(n)) for n in names}
        w1_in = [sem["w1_in0"], sem["w1_in1"], sem["w1_in2"]]
        ex_in = [sem["ex_in0"], sem["ex_in1"], sem["ex_in2"], sem["ex_in3"], sem["ex_in4"], sem["ex_in5"]]
        raw_in = [sem["raw_in0"], sem["raw_in1"], sem["raw_in2"]]
        raw_free = [sem["raw_free0"], sem["raw_free1"], sem["raw_free2"]]
        used = [sem["used0"], sem["used1"], sem["used2"]]

        def used_ffn(L, f, j, s):
            return used[j], 2 * NE + ((LAYER_N - 3) * L + (STEPS + MIX_N - 2) * f if j == 2 else nth(L, f, 0)) + s + 1

        def used_mix(L, m):
            return used[m % 3], 2 * NE + ((LAYER_N - 3) * L + STEPS - 1 if m % 3 == 2 else LAYER_N * L + STEPS) + m // 3 + 1

        def nth(L, f, s):
            return LAYER_N * L + (STEPS + MIX_N) * f + s

        def nth_mix(L, m):
            return LAYER_N * L + STEPS + m // 3

        PROJ = [("hq", 3, True), ("hf", 4, True), ("hb", 5, True), ("q", 0, False), ("k", 1, False),
                ("v", 2, False), ("hi", 6, False), ("hg", 7, False)]
        Z_FREE = [sem["z_hq"], sem["z_hf"], sem["z_hb"], sem["z_q"], sem["z_k"], sem["z_v"], sem["z_hi"], sem["z_hg"]]
        NLEV = len(LEVELS)
        GROUPS = [(0, 2), (1, 3), (4, 6), (5, 7)]
        NG = TT * len(GROUPS)

        block = ctx.enter_context(nc.Block())

        @block.sync
        def _(sp):
            def weights(w, c0, n):
                return w.rearrange("(k p) n -> p k n", p=P)[:, :, c0:c0 + n]

            sp.dma_start(x, x_in.rearrange("(t p) d -> p t d", p=P)).then_inc(sem["x_in"], 16)
            sp.dma_start(const_sb[:, :], const).then_inc(sem["const_in"], 16)
            sp.dma_start(one_sb[:, :], one).then_inc(sem["one_in"], 16)
            for o in range(len(PROJ) + 2):
                if o >= 3:
                    sp.wait_ge(sem["z_ready"], o - 2)
                w, c = (w_in, PROJ[o][1]) if o < len(PROJ) else (w_out, o - len(PROJ))
                sp.dma_start(slot(3 + o % 3), weights(w, 512 * c, 512)).then_inc(w1_in[o % 3], 16)
                if o == 2:
                    a, b = BAND["mask"]
                    sp.dma_start(masks.rearrange("p l s -> p (l s)"), band[:, a:b]).then_inc(sem["band_in"], 16)
                    a, b = BAND["count"]
                    sp.dma_start(count, band[:, a:b]).then_inc(sem["band_in"], 16)
                    a, b = BAND["bias"]
                    sp.dma_start(abias.rearrange("p h i -> p (h i)"), band[:, a:b]).then_inc(sem["band_in"], 16)

            def expert(e, i, w, c):
                sp.dma_start(slot(i), w[e].rearrange("(k p) n -> p k n", p=P)[:, :, 512 * c:512 * c + 512])\
                    .then_inc(ex_in[i], 16)

            ORDER = [(0, wg, 0), (2, wu, 0), (1, wg, 1), (3, wu, 1), (4, wd, 0), (5, wd, 1)]
            sp.wait_ge(sem["o_put"], TT)
            sp.wait_ge(sem["ho_put"], TT)
            for i, w, c in ORDER[:3]:
                expert(0, i, w, c)
            sp.wait_ge(sem["acc_done"], 1)
            for i, w, c in ORDER[3:]:
                expert(0, i, w, c)
            sp.dma_start(prm_all, prm_in.rearrange("l p n -> p l n")).then_inc(sem["late_in"], 16)
            sp.dma_start(fin_row, fin_w).then_inc(sem["late_in"], 16)
            sp.dma_start(tb_future, future).then_inc(sem["late_in"], 16)
            sp.dma_start(tb_onehot, onehot).then_inc(sem["late_in"], 16)
            sp.dma_start(tb_rel, relb).then_inc(sem["late_in"], 16)
            sp.wait_ge(sem["tb_rows_done"], 1)
            sp.dma_start(tb_dram.ap(), tb_rows).then_inc(sem["tb_out"], 16)
            sp.wait_ge(sem["tb_out"], 16)
            sp.dma_start(tb_raw, bass.AP(tb_dram, 0, [[1, P], [TBW + 1, 2 * DH], [1, S]])).then_inc(sem["tb_in"], 16)
            with sp.Fori(1, NE) as e:
                free = sp.snap(2 * e - 1)
                free2 = sp.snap(2 * e)
                sp.wait_ge(sem["used0"], free)
                expert(e, 0, wg, 0)
                sp.wait_ge(sem["used1"], free)
                expert(e, 2, wu, 0)
                sp.wait_ge(sem["used0"], free2)
                expert(e, 1, wg, 1)
                sp.wait_ge(sem["used1"], free2)
                expert(e, 3, wu, 1)
                sp.wait_ge(sem["used2"], free)
                expert(e, 4, wd, 0)
                sp.wait_ge(sem["used2"], free2)
                expert(e, 5, wd, 1)
            def piece(j, n, src):
                free = sp.snap(n + 1)
                sp.wait_ge(raw_free[j], free)
                to = by_rows(raw[j]) if src.shape[0] == FS else by_cols(raw[j])
                sp.dma_start(to, src.rearrange("(k p) n -> p k n", p=P)).then_inc(raw_in[j], 16)

            def ffn_loads(L, f, w_g, w_u, w_d):
                def gate_up(s, c):
                    piece(0, nth(L, f, s), w_g[L, :, bass.ds(c, FS)])
                    piece(1, nth(L, f, s), w_u[L, :, bass.ds(c, FS)])

                def down(s, c):
                    piece(2, nth(L, f, s), w_d[L, bass.ds(c, FS), :])

                gate_up(0, 0)
                with sp.Fori(0, STEPS - 1) as i:
                    c, c_next = sp.snap(i * FS), sp.snap(i * FS + FS)
                    gate_up(i + 1, c_next)
                    down(i, c)
                down(STEPS - 1, (STEPS - 1) * FS)

            with sp.Fori(0, DEPTH2) as L:
                ffn_loads(L, 0, f1g, f1u, f1d)
                for m, c in enumerate(Z_COLS):
                    piece(m % 3, nth_mix(L, m), w_in2[L, :, c:c + FS])
                for i, r in enumerate(O_ROWS):
                    m = len(Z_COLS) + i
                    row = sp.snap(D * L + r)
                    piece(m % 3, nth_mix(L, m), w_out2.rearrange("l m d -> (l m) d")[bass.ds(row, FS), :])
                ffn_loads(L, 1, f2g, f2u, f2d)
            sp.wait_ge(sem["fin_put"], TT)
            sp.dma_start(out.rearrange("(t p) d -> p t d", p=P), xn).then_inc(sem["fin_out"], 16)
            sp.wait_ge(sem["fin_out"], 16)

        @block.tensor
        def _(pe):
            def turn(b, src, ready):
                for k in range(KD):
                    for t in range(TT):
                        mm = pe.transpose(bank(b + k // 2)[:, (k % 2) * S + t * P:(k % 2) * S + t * P + P],
                                          src[:, t, k * P:k * P + P], ident)
                    if k % 2:
                        mm.then_inc(ready, 1)

            def norm(n):
                turn_norm(n)
                pe.wait_ge(sem["xT_act"], n + 1)
                pe.wait_ge(sem["xT_dve"], n + 1)

            def turn_norm(n):
                pe.wait_ge(sem["xn_dve"], n + 1)
                pe.wait_ge(sem["xn_act"], n + 1)
                turn(4, xn, sem["xnT_ps"])

            def residual(to=0, tiles=range(TT)):
                for t in tiles:
                    for n in range(2):
                        pe.matmul(bank(to + 2 * t + n), ident, x[:, t, 512 * n:512 * n + 512], start=True, stop=False,
                                  skip_group_check=True)

            def project(n, w):
                for t in range(TT):
                    for k in range(KD):
                        mm = pe.matmul(bank(2 * t + n), xT[:, k, t * P:t * P + P], w[:, k, :], start=False,
                                       stop=k == KD - 1, skip_group_check=True)
                return mm

            def features(b, w, nf):
                for f in range(nf):
                    for k in range(KD):
                        mm = pe.matmul(bank(b + f // 2)[:, (f % 2) * S:(f % 2) * S + S], w[:, k, f * P:f * P + P],
                                       xT[:, k, :], start=k == 0, stop=k == KD - 1)
                return mm

            def tokens(b, w):
                for t in range(TT):
                    for k in range(KD):
                        mm = pe.matmul(bank(b + t), xT[:, k, t * P:t * P + P], w[:, k, :], start=k == 0,
                                       stop=k == KD - 1)
                return mm

            def proj(o):
                pe.wait_ge(w1_in[o % 3], 16 * (o // 3 + 1))
                if o >= 3:
                    pe.wait_ge(Z_FREE[o - 3], 1)
                (features(2 + 2 * (o % 3), slot(3 + o % 3), 4) if PROJ[o][2] else
                 tokens(2 + 2 * (o % 3), slot(3 + o % 3))).then_inc(sem["z_ready"], 1)

            q_l = lev_qk[:, 0:HH * S].rearrange("p (h s) -> p h s", h=HH)
            k_l = lev_qk[:, HH * S:2 * HH * S].rearrange("p (h s) -> p h s", h=HH)

            def level(i):
                pe.wait_ge(sem["lev_k"], i + 1)
                if i < NLEV:
                    pe.wait_ge(sem["lev_q"], i + 1)
                if i >= 1:
                    pe.wait_ge(sem["lev_put"], i)
                moving = q_l if i < NLEV else hq
                for h in range(HH):
                    for t in range(TT):
                        to = 1 - t if i == 0 else t
                        c = (h % 2) * S + t * P
                        mm = pe.matmul(bank(h // 2)[:, c:c + P], k_l[:, h, t * P:t * P + P],
                                       moving[:, h, to * P:to * P + P], start=True, stop=True)
                mm.then_inc(sem["lev_ps"], 1)

            pe.wait_ge(sem["const_in"], 16)
            norm(0)
            for o in range(len(PROJ)):
                proj(o)
                if o >= 4:
                    for i in {4: [0], 5: [1, 2], 6: [3, 4], 7: range(5, NLEV + 1)}[o]:
                        level(i)

            pe.wait_ge(sem["lev_put"], NLEV + 1)
            for t in range(TT):
                for h in range(HH):
                    o_h = bank(t)[:, h * HD:h * HD + HD]
                    pe.matmul(o_h, at_diag[:, h, t, :], hi_tok[:, t, h * HD:h * HD + HD], start=True, stop=False)
                    mm = pe.matmul(o_h, at_off[:, h, 1 - t, :], hi_tok[:, 1 - t, h * HD:h * HD + HD],
                                   start=False, stop=True)
                mm.then_inc(sem["ho_ps"], 1)

            pe.wait_ge(sem["z_hi"], 1)
            pe.wait_ge(sem["z_hg"], 1)
            for b, src in ((2, aq_tok), (4, ak_tok)):
                for c in range(4):
                    for t in range(TT):
                        mm = pe.transpose(bank(b + c // 2)[:, (c % 2) * S + t * P:(c % 2) * S + t * P + P],
                                          src[:, t, c * P:c * P + P], ident)
                mm.then_inc(sem["qkT_ps"], 1)
            pe.wait_ge(sem["qT_done"], 1)
            pe.wait_ge(sem["kT_done"], 1)
            pe.wait_ge(sem["z_v"], 1)

            def scores(g):
                t = g // len(GROUPS)
                if g >= 2:
                    pe.wait_ge(sem["sc_nm"], g - 1)
                for i, h in enumerate(GROUPS[g % len(GROUPS)]):
                    r = AD * (h % 2)
                    mm = pe.matmul(bank(6 + g % 2)[:, i * S:i * S + S], qT[r:r + AD, h // 2, t * P:t * P + P],
                                   kT[r:r + AD, h // 2, :], start=True, stop=True)
                mm.then_inc(sem["sc_ps"], 1)

            def turn_e(g):
                pe.wait_ge(sem["sc_cnt"], g + 1)
                if g >= 2:
                    pe.wait_ge(sem["eT_dve"] if g % 2 else sem["eT_act"], g // 2)
                for i in range(2):
                    for j in range(TT):
                        mm = pe.transpose(bank(2 + g % 2)[:, (2 * i + j) * P:(2 * i + j) * P + P],
                                          a_s[g % 3][:, i, j * P:j * P + P], ident)
                mm.then_inc(sem["eT_ps"], 1)

            def values(g):
                t = g // len(GROUPS)
                pe.wait_ge(sem["eT_dve"] if g % 2 else sem["eT_act"], g // 2 + 1)
                for i, h in enumerate(GROUPS[g % len(GROUPS)]):
                    for j in range(TT):
                        mm = pe.matmul(bank(4 + t)[:, h * AD:h * AD + AD], a_eT[g % 2][:, i, j, :],
                                       v_tok[:, j, h * AD:h * AD + AD], start=j == 0, stop=j == TT - 1)
                if g % len(GROUPS) == len(GROUPS) - 1:
                    mm.then_inc(sem["o_ps"], 1)

            scores(0)
            scores(1)
            for g in range(NG):
                turn_e(g)
                if g + 2 < NG:
                    scores(g + 2)
                if g >= 1:
                    values(g - 1)
            values(NG - 1)

            pe.wait_ge(sem["o_put"], TT)
            pe.wait_ge(sem["ho_put"], TT)
            turn(4, mixed, sem["mxT_ps"])
            residual()
            pe.wait_ge(sem["mx_act"], 1)
            pe.wait_ge(sem["mx_dve"], 1)
            for n in range(2):
                o = len(PROJ) + n
                pe.wait_ge(w1_in[o % 3], 16 * (o // 3 + 1))
                mm = project(n, slot(3 + o % 3))
            mm.then_inc(sem["acc_done"], 1)

            norm(1)
            router = one_f("router").rearrange("p (k e) -> p k e", k=KD)
            for t in range(TT):
                for k in range(KD):
                    mm = pe.matmul(bank(0)[:, t * NE:t * NE + NE], xT[:, k, t * P:t * P + P], router[:, k, :],
                                   start=k == 0, stop=k == KD - 1)
            mm.then_inc(sem["lg_ps"], 1)
            pe.wait_ge(sem["late_in"], 80)
            pe.matmul(bank(3)[0:2 * DH, 0:TBW + 1], tb_rel, tb_onehot, start=True, stop=True).then_inc(sem["tb_ps"], 1)
            pe.wait_ge(sem["aff_done"], 1)
            for t in range(TT):
                mm = pe.transpose(bank(1)[0:NE, t * P:t * P + P], aff[:, t, :], ident)
            mm.then_inc(sem["affT_ps"], 1)
            pe.wait_ge(sem["place_done"], 1)
            for t in range(TT):
                mm = pe.transpose(bank(2)[:, t * NE:t * NE + NE], place[:, t * P:t * P + P], ident[0:NE, 0:NE])
            mm.then_inc(sem["placeT_ps"], 1)
            pe.wait_ge(sem["hot_done"], 1)
            for k in range(KD):
                if k >= 4:
                    pe.wait_ge(sem["xin_dve"] if k % 2 else sem["xin_act"], (k - 4) // 2 + 1)
                for t in range(TT):
                    mm = pe.matmul(bank(4 + k % 4), xn[:, t, k * P:k * P + P],
                                   hot[:, t, :, :].rearrange("p e c -> p (e c)"), start=t == 0, stop=t == TT - 1)
                mm.then_inc(sem["xin_ps"], 1)
            pe.wait_ge(sem["tb_rows_done"], 1)
            residual()
            pe.wait_ge(sem["xin_act"], KD // 2)
            pe.wait_ge(sem["xin_dve"], KD // 2)

            def quarter(b, stationary, w):
                for r in range(KD // Q4):
                    for j in range(Q4):
                        mm = pe.matmul(bank(b)[j * CAP:j * CAP + CAP, :], stationary[:, Q4 * r + j, :],
                                       w[:, Q4 * r + j, :], start=r == 0, stop=r == KD // Q4 - 1,
                                       skip_group_check=True)
                return mm

            with pe.Fori(0, NE) as e:
                landed = pe.snap(16 * e + 16)
                pe.wait_ge(sem["xe_ready"], e + 1)
                pe.wait_ge(ex_in[0], landed)
                quarter(4, xin, slot(0)).then_inc(sem["used0"], 1)
                pe.wait_ge(ex_in[2], landed)
                quarter(5, xin, slot(2)).then_inc(sem["used1"], 1)
                pe.wait_ge(sem["hote_done"], e + 1)
                for t in range(TT):
                    mm = pe.transpose(bank(7)[:, t * P:t * P + P], hot_e[:, t, :, :].rearrange("p j c -> p (j c)"), ident)
                mm.then_inc(sem["back_ps"], 1)
                pe.wait_ge(sem["g4_done"], 2 * e + 1)
                pe.wait_ge(ex_in[1], landed)
                quarter(4, xin, slot(1)).then_inc(sem["used0"], 1)
                pe.wait_ge(sem["u4_done"], 2 * e + 1)
                pe.wait_ge(ex_in[3], landed)
                quarter(5, xin, slot(3)).then_inc(sem["used1"], 1)
                pe.wait_ge(sem["back_done"], e + 1)
                for c in range(2):
                    pe.wait_ge(sem["g4_done"], 2 * e + c + 1)
                    pe.wait_ge(sem["u4_done"], 2 * e + c + 1)
                    for i, src in enumerate((g4[c], u4[c])):
                        for f in range(4):
                            a = (4 * i + f) * CAP
                            mm = pe.matmul(bank(6 + c)[:, a:a + CAP], src[:, f * P:f * P + P], fold, start=True, stop=True)
                    mm.then_inc(sem["sum_ps"], 1)
                pe.wait_ge(sem["ehid_done"], 2 * e + 2)
                for n in range(2):
                    pe.wait_ge(ex_in[4 + n], landed)
                    quarter(4 + n, hidT, slot(4 + n)).then_inc(sem["used2"], 1)
                for n in range(2):
                    pe.wait_ge(sem["y4_dve"] if n else sem["y4_act"], e + 1)
                    for t in range(TT):
                        mm = pe.matmul(bank(2 * t + n), back[:, t * P:t * P + P], y4[n], start=False, stop=False,
                                       skip_group_check=True)
                mm.then_inc(sem["stage_done"], 1)

            def split_ready(j, n):
                pe.wait_ge(raw_free[j], n + 2)

            def features3(b, j, fresh=None):
                w_h, w_l = by_cols(wh[j]), by_cols(wl[j])
                for f in range(FS // P):
                    for k in range(KD):
                        if fresh is not None and f == 0 and k % 2 == 0:
                            pe.wait_ge(sem["xT_lo"], fresh + k // 2 + 1)
                        to, fs = bank(b)[:, f * S:f * S + S], slice(f * P, f * P + P)
                        pe.matmul(to, w_h[:, k, fs], xTh[:, k, :], start=k == 0, stop=False)
                        pe.matmul(to, w_h[:, k, fs], xTl[:, k, :], start=False, stop=False)
                        mm = pe.matmul(to, w_l[:, k, fs], xTh[:, k, :], start=False, stop=k == KD - 1)
                return mm

            def tokens3(b, c0, j):
                w_h, w_l = by_cols(wh[j]), by_cols(wl[j])
                for t in range(TT):
                    for k in range(KD):
                        to, ts = bank(b + t)[:, c0:c0 + FS], slice(t * P, t * P + P)
                        pe.matmul(to, xTh[:, k, ts], w_h[:, k, :], start=k == 0, stop=False)
                        pe.matmul(to, xTh[:, k, ts], w_l[:, k, :], start=False, stop=False)
                        mm = pe.matmul(to, xTl[:, k, ts], w_h[:, k, :], start=False, stop=k == KD - 1)
                return mm

            def rows3(b, left_h, left_l, j, tiles, last):
                w_h, w_l = by_rows(wh[j]), by_rows(wl[j])
                for k in range(2):
                    for t in tiles:
                        for n in range(2):
                            to, ts, ns = bank(b + 2 * t + n), slice(t * P, t * P + P), slice(512 * n, 512 * n + 512)
                            pe.matmul(to, left_h[:, k, ts], w_h[:, k, ns], start=False, stop=False, skip_group_check=True)
                            pe.matmul(to, left_h[:, k, ts], w_l[:, k, ns], start=False, stop=False, skip_group_check=True)
                            mm = pe.matmul(to, left_l[:, k, ts], w_h[:, k, ns], start=False, stop=last and k == 1,
                                           skip_group_check=True)
                return mm

            def ffn(L, f, fresh, done):
                def gate_up(c, s, fresh=None):
                    for j in range(2):
                        split_ready(j, nth(L, f, s))
                        features3(4 + 2 * j + c, j, None if j else fresh).then_inc(used[j], 1)

                def down(c, s, done=used[2]):
                    split_ready(2, nth(L, f, s))
                    pe.wait_ge(sem["hid_done"], STEPS * (2 * L + f) + s + 1)
                    rows3(0, hidh[c], hidl[c], 2, range(TT), done is not used[2]).then_inc(done, 1)

                residual()
                gate_up(0, 0, fresh)
                with pe.Fori(0, STEPS // 2) as i:
                    gate_up(1, 2 * i + 1)
                    down(0, 2 * i)
                    gate_up(0, 2 * i + 2)
                    down(1, 2 * i + 1)
                down(0, STEPS - 1, done)

            with pe.Fori(0, DEPTH2) as L:
                turn_norm(3 * L + 2)
                ffn(L, 0, 14 * L, sem["acc_done"])
                turn_norm(3 * L + 3)

                def piece(m):
                    split_ready(m % 3, nth_mix(L, m))
                    return m % 3

                def feats(m, b, fresh=None):
                    features3(b, piece(m), fresh).then_inc(used[m % 3], 1)

                feats(0, 0, 14 * L + 4)
                feats(1, 1)
                feats(2, 2)
                feats(3, 3)
                feats(4, 4)
                feats(5, 6)
                feats(6, 7)
                pe.wait_ge(sem["lru_xr"], L + 1)
                pe.wait_ge(sem["z2_2"], L + 1)
                for b, name in ((5, "wa"), (4, "wx")):
                    for c in range(2):
                        a = PRM[name][0] + c * P
                        mm = pe.matmul(bank(b)[:, c * S:c * S + S], prm[:, a:a + P], xr[:, c, :], start=True, stop=True)
                mm.then_inc(sem["lru_ps"], 1)
                pe.wait_ge(sem["z2_1"], L + 1)
                feats(7, 2)
                feats(8, 3)
                pe.wait_ge(sem["z2_0"], L + 1)
                tokens3(0, 0, piece(9)).then_inc(used[0], 1)

                def scores2(g):
                    t, n = g // 2, P * (g // 2 + 1)
                    if g == 0:
                        pe.wait_ge(sem["z2_q"], L + 1)
                        pe.wait_ge(sem["z2_k"], L + 1)
                    if g == 1:
                        pe.wait_ge(sem["lru_gates"], L + 1)
                    if g >= 2:
                        pe.wait_ge(sem["d_nmx"], 4 * L + g - 1)
                    for m in range(2):
                        for i in range(2):
                            h = 2 * (g % 2) + i
                            mm = pe.matmul(bank(6 - 2 * (g % 2) + m)[:, i * S:i * S + n],
                                           qT2[m * DM:m * DM + DM, h, t * P:t * P + P],
                                           kT2[m * DM:m * DM + DM, h, 0:n], start=True, stop=True)
                    mm.then_inc(sem["d_ps"], 1)

                def turn_d(g):
                    pe.wait_ge(sem["d_comb"], 4 * L + g + 1)
                    if g >= 2:
                        pe.wait_ge(sem["dT_done"], 4 * L + g - 1)
                    for i in range(2):
                        for j in range(g // 2 + 1):
                            mm = pe.transpose(bank(2 + g % 2)[:, (2 * i + j) * P:(2 * i + j) * P + P],
                                              d_attn[:, i, j * P:j * P + P], ident)
                    mm.then_inc(sem["dT_ps"], 1)

                def values2(g):
                    pe.wait_ge(sem["dT_done"], 4 * L + g + 1)
                    if g == 0:
                        pe.wait_ge(sem["z2_v"], L + 1)
                    for i in range(2):
                        h = 2 * (g % 2) + i
                        for j in range(g // 2 + 1):
                            mm = pe.matmul(bank(g // 2)[:, h * P:h * P + P], d_aT[:, i, j, :], v2[:, j, h * P:h * P + P],
                                           start=j == 0, stop=j == g // 2)
                    mm.then_inc(sem["do_ps"], 1)

                def project3(m, tiles):
                    k = O_ROWS[m - len(Z_COLS)] // P
                    return rows3(4, xTh[:, k:k + 2, :], xTl[:, k:k + 2, :], piece(m), tiles, m == MIX_N * 3 - 1)

                scores2(0)
                scores2(1)
                tokens3(0, FS, piece(10)).then_inc(used[1], 1)
                turn_d(0)
                scores2(2)
                values2(0)
                turn_d(1)
                scores2(3)
                values2(1)
                pe.wait_ge(sem["d_nmx"], 4 * L + 3)
                residual(4, [1])
                turn_d(2)
                pe.wait_ge(sem["y_done"], L + 1)
                project3(11, [1])
                values2(2)
                pe.wait_ge(sem["d_nmx"], 4 * L + 4)
                residual(4, [0])
                turn_d(3)
                project3(12, [1])
                values2(3)
                project3(11, [0]).then_inc(used[2], 1)
                project3(12, [0]).then_inc(used[0], 1)
                pe.wait_ge(sem["do_nrm"], L + 1)
                for h in range(DH):
                    for t in range(TT):
                        mm = pe.transpose(bank(2 + h // 2)[:, (h % 2) * S + t * P:(h % 2) * S + t * P + P],
                                          xn[:, t, h * P:h * P + P], ident)
                    if h % 2:
                        mm.then_inc(sem["yT_ps"], 1)
                pe.wait_ge(sem["xT_lo"], 14 * L + 9)
                project3(13, range(TT)).then_inc(used[1], 1)
                pe.wait_ge(sem["xT_lo"], 14 * L + 10)
                project3(14, range(TT)).then_inc(sem["acc_done"], 1)
                turn_norm(3 * L + 4)
                ffn(L, 1, 14 * L + 10, sem["stage_done"])

        @block.scalar
        def _(act):
            def norm(n, weight, part=None):
                nc.scalar.activation(xn[:, 0, :], x[:, 0, :], ACT.Square, accum_out=n_ss[:, 0:1]).then_inc(sem["sq_done"], 1)
                act.wait_ge(sem["ms_ready"], n + 1)
                nc.scalar.activation(n_std, n_ms, ACT.Sqrt).then_inc(sem["std_ready"], 1)
                act.wait_ge(sem["rstd_ready"], n + 1)
                nc.scalar.activation(xn[:, 0, :], x[:, 0, :], ACT.Copy, scale=n_rstd[:, 0:1]).then_inc(sem["xn_act"], 1)
                to = xT if part is None else xTh
                for k in range(4 if part is None else KD):
                    if k % 2 == 0:
                        act.wait_ge(sem["xnT_ps"], 4 * n + k // 2 + 1)
                    a = nc.scalar.activation(to[:, k, :], bank(4 + k // 2)[:, (k % 2) * S:(k % 2) * S + S], ACT.Copy,
                                             scale=weight[:, k:k + 1])
                    if part is not None and k % 2:
                        a.then_inc(sem["xT_hi"], 1)
                if part is None:
                    a.then_inc(sem["xT_act"], 1)

            def update(done, b=0):
                act.wait_ge(done[0], done[1])
                nc.scalar.activation(x[:, 0, :], bank(b, 2), ACT.Copy).then_inc(sem["x_act"], 1)

            def x_ready(n):
                act.wait_ge(sem["x_act"], n)

            act.wait_ge(sem["x_in"], 16)
            act.wait_ge(sem["one_in"], 16)
            norm(0, one_f("norm1"))
            act.wait_ge(sem["lb_max"], 1)
            nc.scalar.activation(lbe, lbe, ACT.Exp).then_inc(sem["lb_exp"], 1)
            act.wait_ge(sem["z_ready"], 1)
            nc.scalar.activation(hq.rearrange("p h s -> p (h s)"), bank(2, 2), ACT.Silu).then_inc(sem["z_hq"], 1)
            sg = lev_e[1].rearrange("p (d n) -> p d n", d=2)
            lf = lev_e[0].rearrange("p (d n) -> p d n", d=2)
            for d, (b, k_raw, free) in enumerate(((4, kf, sem["z_hf"]), (6, kb, sem["z_hb"]))):
                act.wait_ge(sem["z_ready"], 2 + d)
                nc.scalar.activation(sg[:, d, :], bank(b, 2), ACT.Sigmoid).then_inc(sem["gate_sg"], 1)
                nc.scalar.activation(k_raw.rearrange("p h s -> p (h s)"), bank(b, 2), ACT.Sigmoid, scale=-1.0)\
                    .then_inc(free, 1)
            act.wait_ge(sem["lb_done"], 1)
            act.wait_ge(sem["gate_sg"], 2)
            for d in range(2):
                for h in range(HH):
                    i = d * HH + h
                    a = nc.scalar.activation(lf[:, d, h * S:h * S + S], sg[:, d, h * S:h * S + S], ACT.Ln,
                                             scale=oml[:, i:i + 1], bias=lb[:, i:i + 1])
                a.then_inc(sem["gate_lf"], 1)

            def decay(i):
                act.wait_ge(sem["lev_sub"], i + 1)
                nc.scalar.activation(lev_e[i % 2], lev_e[i % 2], ACT.Exp).then_inc(sem["lev_exp"], 1)

            decay(0)
            decay(1)
            for c, b in ((0, 2), (1, 4)):
                act.wait_ge(sem["z_ready"], 4 + c)
                nc.scalar.activation(sqj[:, c, :, :].rearrange("p t n -> p (t n)"), bank(b, 2), ACT.Square)\
                    .then_inc(sem["qk_sq"], 1)
            act.wait_ge(sem["qk_ms"], 1)
            nc.scalar.activation(qk_std, qk_ms, ACT.Sqrt).then_inc(sem["qk_std"], 1)
            decay(2)
            decay(3)
            act.wait_ge(sem["z_ready"], 6)
            nc.scalar.activation(v_tok.rearrange("p t n -> p (t n)"), bank(6, 2), ACT.Copy).then_inc(sem["z_v"], 1)
            for i in range(4, NLEV):
                decay(i)
            act.wait_ge(sem["z_ready"], 8)
            nc.scalar.activation(gs_tok.rearrange("p t n -> p (t n)"), bank(4, 2), ACT.Silu).then_inc(sem["z_hg"], 1)
            act.wait_ge(sem["qkT_ps"], 2)
            nc.scalar.activation(kT.rearrange("p c s -> p (c s)"), bank(4, 2), ACT.Copy, scale=one_f("k"))\
                .then_inc(sem["kT_done"], 1)
            act.wait_ge(sem["ho_ps"], 2)
            ho_sqj = sqj[:, 0, :, :].rearrange("p t n -> p (t n)")
            nc.scalar.activation(ho_sqj, bank(0, 2), ACT.Square).then_inc(sem["ho_sq"], 1)
            for g in range(NG + 1):
                if g < NG:
                    act.wait_ge(sem["sc_nm"], g + 1)
                    for i, h in enumerate(GROUPS[g % len(GROUPS)]):
                        c = g // len(GROUPS) * AH + h
                        a = nc.scalar.activation(a_s[g % 3][:, i, :], a_s[g % 3][:, i, :], ACT.Exp, bias=a_nm[:, c:c + 1])
                    a.then_inc(sem["sc_exp"], 1)
                if g >= 1 and (g - 1) % 2 == 0:
                    act.wait_ge(sem["eT_ps"], g)
                    nc.scalar.activation(a_eT[0].rearrange("p h j s -> p (h j s)"), bank(2), ACT.Copy).then_inc(sem["eT_act"], 1)
            act.wait_ge(sem["ho_ms"], 1)
            nc.scalar.activation(o_std, o_ms, ACT.Sqrt).then_inc(sem["ho_std"], 1)
            act.wait_ge(sem["mxT_ps"], 2)
            nc.scalar.activation(xT[:, 0:4, :].rearrange("p k s -> p (k s)"), bank(4, 2), ACT.Copy).then_inc(sem["mx_act"], 1)
            update((sem["acc_done"], 1))

            x_ready(1)
            norm(1, one_f("norm2"))
            act.wait_ge(sem["lg_nm"], 1)
            for t in range(TT):
                a = nc.scalar.activation(aff_e[:, t, :], bank(0)[:, t * NE:t * NE + NE], ACT.Exp, bias=r_nm[:, t:t + 1],
                                         accum_out=r_sum[:, t:t + 1])
            a.then_inc(sem["lg_exp"], 1)
            for k in range(0, KD, 2):
                act.wait_ge(sem["xin_ps"], k + 1)
                nc.scalar.activation(xin_all[:, k, :, :].rearrange("p e c -> p (e c)"), bank(4 + k % 4), ACT.Copy,
                                     scale=one_f("norm2")[:, k:k + 1]).then_inc(sem["xin_act"], 1)
            with act.Fori(0, NE) as e:
                act.wait_ge(sem["used0"], 2 * e + 1)
                nc.scalar.activation(g4[0], bank(4), ACT.Copy).then_inc(sem["g4_done"], 1)
                act.wait_ge(sem["back_ps"], e + 1)
                nc.scalar.activation(back, bank(7)[:, 0:S], ACT.Copy).then_inc(sem["back_done"], 1)
                act.wait_ge(sem["used0"], 2 * e + 2)
                nc.scalar.activation(g4[1], bank(4), ACT.Copy).then_inc(sem["g4_done"], 1)
                for c in range(2):
                    act.wait_ge(sem["sum_ps"], 2 * e + c + 1)
                    nc.scalar.activation(e_sil[c], bank(6 + c)[:, 0:4 * CAP], ACT.Silu).then_inc(sem["esil_done"], 1)
                act.wait_ge(sem["used2"], 2 * e + 1)
                nc.scalar.activation(y4[0], bank(4), ACT.Copy).then_inc(sem["y4_act"], 1)

            def hi(j, n, free=None):
                act.wait_ge(raw_in[j], 16 * n + 16)
                if free is not None:
                    act.wait_ge(free[0], free[1])
                nc.scalar.activation(wh[j], raw[j], ACT.Copy).then_inc(sem["w_hi"], 1)

            def hi_first(L, f):
                for j in range(2):
                    hi(j, nth(L, f, 0), used_ffn(L, f, j, -1))

            def ffn(L, f, free):
                def step(c, s, first=False, last=False):
                    q = STEPS * (2 * L + f)
                    if not last:
                        hi(0, nth(L, f, s + 1), used_ffn(L, f, 0, s))
                    act.wait_ge(*used_ffn(L, f, 1, s))
                    nc.scalar.activation(f_sil[c], bank(4 + c), ACT.Silu).then_inc(sem["sil_done"], 1)
                    if not last:
                        hi(1, nth(L, f, s + 1))
                    hi(2, nth(L, f, s), free if first else used_ffn(L, f, 2, s - 1))
                    act.wait_ge(sem["hid_t"], q + s + 1)
                    nc.scalar.activation(hidh[c].rearrange("p f s -> p (f s)"), f_hid[c].rearrange("p f s -> p (f s)"), ACT.Copy)\
                        .then_inc(sem["hid_h"], 1)

                step(0, 0, first=True)
                step(1, 1)
                with act.Fori(1, STEPS // 2) as i:
                    step(0, 2 * i)
                    step(1, 2 * i + 1)
                step(0, STEPS - 1, last=True)

            act.wait_ge(sem["late_in"], 80)
            with act.Fori(0, DEPTH2) as L:
                hi_first(L, 0)
                update((sem["stage_done"], NE + L))
                x_ready(3 * L + 2)
                act.wait_ge(sem["prm_ready"], L + 1)
                norm(3 * L + 2, pf("norm0"), 14 * L)
                act.wait_ge(sem["lru_u"], L + 1)
                nc.scalar.activation(lc_u, lc_ab, ACT.Exp, scale=-1.0).then_inc(sem["lru_c"], 1)
                act.wait_ge(sem["d_lamx"], L + 1)
                nc.scalar.activation(lamv[:, 2:4], lamv[:, 0:2], ACT.Exp).then_inc(sem["d_lame"], 1)
                ffn(L, 0, (sem["stage_done"], NE + L))

                def hi_mix(m):
                    free = (used_ffn(L, 0, m, STEPS - 1) if m < 2 else (sem["acc_done"], 2 * L + 2) if m == 2
                            else used_mix(L, m - 3))
                    hi(m % 3, nth_mix(L, m), free)

                hi_mix(0)
                hi_mix(1)
                update((sem["acc_done"], 2 * L + 2))
                x_ready(3 * L + 3)
                norm(3 * L + 3, pf("norm1"), 14 * L + 4)
                hi_mix(2)
                hi_mix(3)
                hi_mix(4)
                act.wait_ge(sem["tb_done"], 1)
                nc.scalar.activation(scbc.rearrange("p c s -> p (c s)"), bank(0, 2), ACT.Copy).then_inc(sem["z2_0"], 1)
                hi_mix(5)
                hi_mix(6)
                hi_mix(7)
                nc.scalar.activation(lgate.rearrange("p c s -> p (c s)"), bank(4), ACT.Copy).then_inc(sem["z2_2"], 1)
                hi_mix(8)
                hi_mix(9)
                nc.scalar.activation(qT2.rearrange("p c s -> p (c s)"), bank(6, 2), ACT.Copy, scale=DM ** -0.5)\
                    .then_inc(sem["z2_q"], 1)
                act.wait_ge(sem["lru_ps"], L + 1)
                for b, g, name in ((5, rg, "ba"), (4, ig, "bx")):
                    for c in range(2):
                        a = nc.scalar.activation(g[:, c, :], bank(b)[:, c * S:c * S + S], ACT.Sigmoid, bias=pf(name, c))
                a.then_inc(sem["lru_gates"], 1)
                hi_mix(10)
                act.wait_ge(sem["gelu_in"], L + 1)
                nc.scalar.activation(lg, lg, ACT.Tanh, scale=GELU_C).then_inc(sem["gelu_t"], 1)
                act.wait_ge(sem["lru_gates"], L + 1)
                act.wait_ge(sem["lru_b"], L + 1)
                for c in range(2):
                    nc.scalar.activation(lm[:, c, :], rg[:, c, :], ACT.Tanh, scale=lc_n[:, c:c + 1])
                for c in range(2):
                    a = nc.scalar.activation(la[:, c, :], rg[:, c, :], ACT.Exp, scale=lc_c[:, c:c + 1])
                a.then_inc(sem["lru_a"], 1)
                hi_mix(11)
                nc.scalar.activation(kT2.rearrange("p c s -> p (c s)"), bank(2, 2), ACT.Copy).then_inc(sem["z2_k"], 1)
                act.wait_ge(sem["lru_m"], L + 1)
                nc.scalar.activation(lm, lm, ACT.Sqrt).then_inc(sem["lru_sq"], 1)
                hi_mix(12)
                for g in range(5):
                    if g < 4:
                        act.wait_ge(sem["d_nmx"], 4 * L + g + 1)
                        n = P * (g // 2 + 1)
                        for m in range(2):
                            for i in range(2):
                                c = 4 * g + 2 * m + i
                                e_g = d_e[:, g % 2, m, i, 0:n]
                                a = nc.scalar.activation(e_g, e_g, ACT.Exp, bias=d_nm[:, c:c + 1], accum_out=d_den[:, c:c + 1])
                        a.then_inc(sem["d_exp"], 1)
                    if g == 1:
                        hi_mix(13)
                    if g >= 1:
                        act.wait_ge(sem["dT_ps"], 4 * L + g)
                        if g >= 2:
                            act.wait_ge(sem["do_ps"], 4 * L + g - 1)
                        n = (g - 1) // 2 + 1
                        nc.scalar.activation(d_aT[:, :, 0:n, :], bank(2 + (g - 1) % 2).rearrange("p (h j s) -> p h j s", h=2, j=2)
                                             [:, :, 0:n, :], ACT.Copy).then_inc(sem["dT_done"], 1)
                act.wait_ge(sem["do_ps"], 4 * L + 4)
                nc.scalar.activation(f_buf[:, 0:1024], bank(0, 2), ACT.Square).then_inc(sem["do_sq"], 1)
                act.wait_ge(sem["do_ms"], L + 1)
                nc.scalar.activation(d_std[:, 0:8], d_ms[:, 0:8], ACT.Sqrt).then_inc(sem["do_std"], 1)
                hi_mix(14)
                for c in range(2):
                    act.wait_ge(sem["yT_ps"], 2 * L + c + 1)
                    nc.scalar.activation(xTh[:, 2 * c:2 * c + 2, :].rearrange("p k s -> p (k s)"), bank(2 + c), ACT.Copy,
                                         scale=lamv[:, 6:7]).then_inc(sem["xT_hi"], 1)
                hi_first(L, 1)
                update((sem["acc_done"], 2 * L + 3), 4)
                x_ready(3 * L + 4)
                norm(3 * L + 4, pf("norm2"), 14 * L + 10)
                ffn(L, 1, (sem["acc_done"], 2 * L + 3))

            update((sem["stage_done"], NE + DEPTH2))
            x_ready(3 * DEPTH2 + 2)
            nc.scalar.activation(xn[:, 0, :], x[:, 0, :], ACT.Square, accum_out=n_ss[:, 0:1]).then_inc(sem["sq_done"], 1)
            act.wait_ge(sem["ms_ready"], 3 * DEPTH2 + 3)
            nc.scalar.activation(n_std, n_ms, ACT.Sqrt).then_inc(sem["std_ready"], 1)

        @block.vector
        def _(dve):
            ch = Chain(dve, sem["dve_chain"])

            def mean_eps(out, ss, width, eps):
                return dve.tensor_scalar(out, ss, 1.0 / width, eps, ALU.mult, ALU.add)

            def squares():
                dve.memset(hold[:, 0:1], 0.0)
                ch.step(dve.tensor_tensor_reduce(xn[:, 1, :], x[:, 1, :], x[:, 1, :], 1.0, 0.0, ALU.mult, ALU.add, n_ss[:, 1:2]))

            def means(n):
                dve.wait_ge(sem["sq_done"], n + 1)
                ch.settle()
                mean_eps(n_ms, n_ss, D, EPS).then_inc(sem["ms_ready"], 1)

            def norm(n, weight, part=None):
                squares()
                means(n)
                dve.wait_ge(sem["std_ready"], n + 1)
                dve.reciprocal(n_rstd, n_std).then_inc(sem["rstd_ready"], 1)
                dve.wait_ge(sem["rstd_ready"], n + 1)
                dve.tensor_scalar(xn[:, 1, :], x[:, 1, :], n_rstd[:, 1:2], None, ALU.mult).then_inc(sem["xn_dve"], 1)
                for k in range(4 if part is None else 0, KD):
                    if k % 2 == 0:
                        if part is None:
                            dve.wait_ge(sem["xnT_ps"], 4 * n + k // 2 + 1)
                        else:
                            dve.wait_ge(sem["xT_hi"], part + k // 2 + 1)
                    turned = bank(4 + k // 2)[:, (k % 2) * S:(k % 2) * S + S]
                    if part is None:
                        v = dve.tensor_scalar(xT[:, k, :], turned, weight[:, k:k + 1], None, ALU.mult)
                    else:
                        v = dve.scalar_tensor_tensor(xTl[:, k, :], turned, weight[:, k:k + 1], xTh[:, k, :].bitcast(F32),
                                                     ALU.mult, ALU.subtract)
                        if k % 2:
                            v.then_inc(sem["xT_lo"], 1)
                if part is None:
                    v.then_inc(sem["xT_dve"], 1)

            def update(done, b=2):
                dve.wait_ge(done[0], done[1])
                dve.tensor_copy(x[:, 1, :], bank(b, 2)).then_inc(sem["x_dve"], 1)

            dve.wait_ge(sem["one_in"], 16)
            lbp = one_f("lb")
            ch.link(dve.tensor_tensor(lbm, lbp[:, 0:8], lbp[:, 8:16], ALU.max))
            dve.tensor_tensor(lbe[:, 0:8], lbp[:, 0:8], lbm, ALU.subtract)
            dve.tensor_tensor(lbe[:, 8:16], lbp[:, 8:16], lbm, ALU.subtract).then_inc(sem["lb_max"], 1)
            dve.wait_ge(sem["x_in"], 16)
            norm(0, one_f("norm1"))
            dve.wait_ge(sem["lb_exp"], 1)
            ch.link(dve.tensor_tensor(lbr, lbe[:, 0:8], lbe[:, 8:16], ALU.add))
            ch.link(dve.reciprocal(lbr, lbr))
            ch.link(dve.tensor_tensor(lb, lbe[:, 0:8], lbr, ALU.mult))
            ch.link(dve.tensor_scalar(oml, lb, -1.0, 1.0, ALU.mult, ALU.add))
            dve.tensor_scalar(lb, lb, LN_LEAST, None, ALU.max).then_inc(sem["lb_done"], 1)

            dve.wait_ge(sem["lb_done"], 1)
            for d, (k_raw, free) in enumerate(((kf, sem["z_hf"]), (kb, sem["z_hb"]))):
                dve.wait_ge(free, 1)
                for h in range(HH):
                    v = dve.tensor_scalar(k_raw[:, h, :], k_raw[:, h, :], oml[:, d * HH + h:d * HH + h + 1], None, ALU.mult)
                v.then_inc(sem["k_scaled"], 1)
            lf = lev_e[0].rearrange("p (d h n) -> p d h n", d=2, h=HH)
            dve.wait_ge(sem["masks_zero"], 2)
            dve.wait_ge(sem["gate_lf"], 1)
            for h in range(HH):
                ch.step(dve.tensor_tensor_scan(bc[:, h, :], ones_s, lf[:, 0, h, :], 0.0, ALU.mult, ALU.add))
            dve.wait_ge(sem["gate_lf"], 2)
            for h in range(HH):
                ch.step(dve.tensor_tensor_scan(rc[:, h, ::-1], ones_s, lf[:, 1, h, ::-1], 0.0, ALU.mult, ALU.add))
            ch.settle()

            def exponents(i):
                w = LEVELS[i]
                n = HH * S // (2 * w)
                if i >= 2:
                    dve.wait_ge(sem["lev_k"], i - 1)
                    dve.wait_ge(sem["lev_q"], i - 1)
                eq = lev_e[i % 2][:, 0:HH * S].rearrange("p (n f w) -> p n f w", n=n, f=2)
                ek = lev_e[i % 2][:, HH * S:2 * HH * S].rearrange("p (n f w) -> p n f w", n=n, f=2)
                b = bc.rearrange("p h s -> p (h s)").rearrange("p (n f w) -> p n f w", n=n, f=2)
                r = rc.rearrange("p h s -> p (h s)").rearrange("p (n f w) -> p n f w", n=n, f=2)
                b_end = b[:, :, 0, w - 1:w].to_broadcast([P, n, w])
                r_end = r[:, :, 1, 0:1].to_broadcast([P, n, w])
                dve.tensor_tensor(eq[:, :, 1, :], b[:, :, 1, :], b_end, ALU.subtract)
                dve.tensor_tensor(ek[:, :, 0, :], b_end, b[:, :, 0, :], ALU.subtract)
                dve.tensor_tensor(eq[:, :, 0, :], r[:, :, 0, :], r_end, ALU.subtract)
                dve.tensor_tensor(ek[:, :, 1, :], r_end, r[:, :, 1, :], ALU.subtract).then_inc(sem["lev_sub"], 1)

            def decayed_q(i):
                dve.wait_ge(sem["lev_exp"], i + 1)
                if i >= 1:
                    dve.wait_ge(sem["lev_ps"], i)
                dve.tensor_tensor(lev_qk[:, 0:HH * S], hq.rearrange("p h s -> p (h s)"), lev_e[i % 2][:, 0:HH * S],
                                  ALU.mult).then_inc(sem["lev_q"], 1)

            def put(i):
                dve.wait_ge(sem["lev_ps"], i + 1)
                if i == 0:
                    dve.tensor_copy(at_off.rearrange("p h t c -> p (h t c)"), bank(0, 2)).then_inc(sem["lev_put"], 1)
                else:
                    dve.wait_ge(sem["lev_put"], i)
                    mask = masks[:, i - 1, :].bitcast(U32).unsqueeze(1).to_broadcast([P, HH * TT, P])
                    dve.copy_predicated(at_diag.rearrange("p h t c -> p (h t) c"), mask,
                                        bank(0, 2).rearrange("p (n c) -> p n c", c=P)).then_inc(sem["lev_put"], 1)

            exponents(0)
            exponents(1)
            dve.wait_ge(sem["masks_zero"], 2)
            dve.wait_ge(sem["band_in"], 48)
            for i in range(NLEV):
                decayed_q(i)
                if i >= 1:
                    put(i - 1)
                if i + 2 < NLEV:
                    exponents(i + 2)
                if i == 0:
                    dve.wait_ge(sem["qk_sq"], 2)
                    ch.link(dve.tensor_reduce(qk_ss, sqj.rearrange("p c t n -> p (c t n)").rearrange("p (h d) -> p h d", d=AD),
                                              AX.X, ALU.add))
                    mean_eps(qk_ms, qk_ss, AD, EPS).then_inc(sem["qk_ms"], 1)
                    dve.wait_ge(sem["qk_std"], 1)
                    ch.link(dve.reciprocal(qk_rstd, qk_std))
                    for c, (b, dst, free) in enumerate(((2, aq_tok, sem["z_q"]), (4, ak_tok, sem["z_k"]))):
                        rstd = qk_rstd[:, 16 * c:16 * c + 16].unsqueeze(2).to_broadcast([P, 16, AD])
                        dve.tensor_tensor(dst.rearrange("p t n -> p (t n)").rearrange("p (h d) -> p h d", d=AD),
                                          bank(b, 2).rearrange("p (h d) -> p h d", d=AD), rstd, ALU.mult).then_inc(free, 1)
                if i == 3:
                    dve.wait_ge(sem["z_ready"], 7)
                    dve.tensor_copy(hi_tok.rearrange("p t n -> p (t n)"), bank(2, 2)).then_inc(sem["z_hi"], 1)
            put(NLEV - 1)
            put(NLEV)
            dve.wait_ge(sem["qkT_ps"], 1)
            dve.tensor_scalar(qT.rearrange("p c s -> p (c s)"), bank(2, 2), one_f("q"), AD ** -0.5, ALU.mult, ALU.mult)\
                .then_inc(sem["qT_done"], 1)

            def maxima(g):
                t = g // len(GROUPS)
                dve.wait_ge(sem["sc_ps"], g + 1)
                if g >= 3:
                    dve.wait_ge(sem["eT_ps"], g - 2)
                for i, h in enumerate(GROUPS[g % len(GROUPS)]):
                    c = t * AH + h
                    ch.step(dve.tensor_tensor_reduce(a_s[g % 3][:, i, :], bank(6 + g % 2)[:, i * S:i * S + S],
                                                     abias[:, h, P * (1 - t):P * (1 - t) + S], 1.0, -3e38, ALU.add, ALU.max,
                                                     a_mx[:, c:c + 1]))
                c = t * AH + GROUPS[g % len(GROUPS)][0]
                ch.settle()
                dve.tensor_scalar(a_nm[:, c:c + 3:2], a_mx[:, c:c + 3:2], -1.0, None, ALU.mult).then_inc(sem["sc_nm"], 1)

            def weigh(g):
                t = g // len(GROUPS)
                dve.wait_ge(sem["sc_exp"], g + 1)
                for i, h in enumerate(GROUPS[g % len(GROUPS)]):
                    c = t * AH + h
                    v = dve.tensor_tensor_reduce(a_s[g % 3][:, i, :], a_s[g % 3][:, i, :], count[:, P * (1 - t):P * (1 - t) + S],
                                                 1.0, 0.0, ALU.mult, ALU.add, a_den[:, c:c + 1])
                v.then_inc(sem["sc_cnt"], 1)

            def outputs(t):
                dve.wait_ge(sem["sc_cnt"], (t + 1) * len(GROUPS))
                ch.link(dve.reciprocal(a_rden[:, t * AH:t * AH + AH], a_den[:, t * AH:t * AH + AH]))
                dve.wait_ge(sem["o_ps"], t + 1)
                rden = a_rden[:, t * AH:t * AH + AH].unsqueeze(2).to_broadcast([P, AH, AD])
                dve.tensor_tensor(mixed[:, t, 0:512].rearrange("p (h d) -> p h d", d=AD),
                                  bank(4 + t).rearrange("p (h d) -> p h d", d=AD), rden, ALU.mult).then_inc(sem["o_put"], 1)

            maxima(0)
            maxima(1)
            for g in range(NG):
                weigh(g)
                if g + 2 < NG:
                    maxima(g + 2)
                if g % 2 == 0 and g >= 2:
                    dve.wait_ge(sem["eT_ps"], g)
                    dve.tensor_copy(a_eT[1].rearrange("p h j s -> p (h j s)"), bank(3)).then_inc(sem["eT_dve"], 1)
            dve.wait_ge(sem["ho_sq"], 1)
            ch.link(dve.tensor_reduce(o_ss, sqj[:, 0, :, :].rearrange("p t n -> p (t n)").rearrange("p (h d) -> p h d", d=HD),
                                      AX.X, ALU.add))
            mean_eps(o_ms, o_ss, HD, EPS).then_inc(sem["ho_ms"], 1)
            dve.wait_ge(sem["eT_ps"], NG)
            dve.tensor_copy(a_eT[1].rearrange("p h j s -> p (h j s)"), bank(3)).then_inc(sem["eT_dve"], 1)
            dve.wait_ge(sem["ho_std"], 1)
            ch.link(dve.reciprocal(o_rstd, o_std))
            dve.wait_ge(sem["gs_done"], 1)
            dve.wait_ge(sem["z_q"], 1)
            for t in range(TT):
                o_t = mixed[:, t, 512:1024].rearrange("p (h d) -> p h d", d=HD)
                rstd = o_rstd[:, t * HH:t * HH + HH].unsqueeze(2).to_broadcast([P, HH, HD])
                ch.link(dve.tensor_tensor(o_t, bank(t).rearrange("p (h d) -> p h d", d=HD), rstd, ALU.mult))
                dve.tensor_tensor(o_t, o_t, gs_tok[:, t, :].rearrange("p (h d) -> p h d", d=HD), ALU.mult).then_inc(sem["ho_put"], 1)
            for t in range(TT):
                outputs(t)
            dve.wait_ge(sem["mxT_ps"], 4)
            dve.tensor_copy(xT[:, 4:KD, :].rearrange("p k s -> p (k s)"), bank(6, 2)).then_inc(sem["mx_dve"], 1)
            update((sem["acc_done"], 1))

            dve.wait_ge(sem["x_dve"], 1)
            norm(1, one_f("norm2"))
            dve.wait_ge(sem["lg_ps"], 1)
            ch.link(dve.tensor_reduce(r_mx, bank(0)[:, 0:TT * NE].rearrange("p (t e) -> p t e", t=TT), AX.X, ALU.max))
            dve.tensor_scalar(r_nm, r_mx, -1.0, None, ALU.mult).then_inc(sem["lg_nm"], 1)
            dve.wait_ge(sem["lg_exp"], 1)
            ch.link(dve.reciprocal(r_rec, r_sum))
            for t in range(TT):
                v = dve.tensor_scalar(aff[:, t, :], aff_e[:, t, :], r_rec[:, t:t + 1], None, ALU.mult)
            v.then_inc(sem["aff_done"], 1)
            dve.wait_ge(sem["affT_ps"], 1)
            ch.link(dve.tensor_copy(topw, bank(1)[0:NE, 0:S]))
            for _ in range(CAP // 8):
                ch.link(dve.max(top8, topw))
                ch.link(dve.match_replace(topw, top8, topw, -1.0))
            ch.link(dve.tensor_scalar(chosen, topw, 0.0, None, ALU.is_lt))
            dve.wait_ge(sem["masks_zero"], 3)
            ch.link(dve.tensor_tensor_scan(place, ones_e, chosen, 0.0, ALU.mult, ALU.add))
            dve.tensor_tensor(place, place, chosen, ALU.mult).then_inc(sem["place_done"], 1)
            dve.wait_ge(sem["tb_ps"], 1)
            dve.tensor_tensor(tb_rows, bank(3)[0:2 * DH, 0:TBW + 1], tb_future, ALU.add).then_inc(sem["tb_rows_done"], 1)
            dve.wait_ge(sem["placeT_ps"], 1)
            ch.link(dve.tensor_copy(posT.rearrange("p t e -> p (t e)"), bank(2)[:, 0:TT * NE]))
            for t in range(TT):
                v = dve.tensor_tensor(hot[:, t, :, :], posT[:, t, :].unsqueeze(2).to_broadcast([P, NE, CAP]),
                                      rank.unsqueeze(1).to_broadcast([P, NE, CAP]), ALU.is_equal)
            v.then_inc(sem["hot_done"], 1)
            for k in range(1, KD, 2):
                dve.wait_ge(sem["xin_ps"], k + 1)
                dve.tensor_scalar(xin_all[:, k, :, :].rearrange("p e c -> p (e c)"), bank(4 + k % 4),
                                  one_f("norm2")[:, k:k + 1], None, ALU.mult).then_inc(sem["xin_dve"], 1)
            dve.wait_ge(sem["xin_act"], KD // 2)
            dve.wait_ge(sem["xin_dve"], KD // 2)
            dve.wait_ge(sem["hot_done"], 1)
            with dve.Fori(0, NE) as e:
                dve.tensor_scalar(xin, xin_all[:, :, bass.ds(e, 1), :].rearrange("p k e c -> p k (e c)"), 1.0, None, ALU.mult)\
                    .then_inc(sem["xe_ready"], 1)
                for t in range(TT):
                    v = dve.tensor_scalar(hot_e[:, t, :, :], hot[:, t, bass.ds(e, 1), :].to_broadcast([P, Q4, CAP]),
                                          aff[:, t, bass.ds(e, 1)], None, ALU.mult)
                v.then_inc(sem["hote_done"], 1)
                for c in range(2):
                    dve.wait_ge(sem["used1"], 2 * e + c + 1)
                    dve.tensor_copy(u4[c], bank(5)).then_inc(sem["u4_done"], 1)
                for c in range(2):
                    dve.wait_ge(sem["esil_done"], 2 * e + c + 1)
                    dve.tensor_tensor(hidT[:, 4 * c:4 * c + 4, :].rearrange("p k c -> p (k c)"), e_sil[c],
                                      bank(6 + c)[:, 4 * CAP:8 * CAP], ALU.mult).then_inc(sem["ehid_done"], 1)
                dve.wait_ge(sem["used2"], 2 * e + 2)
                dve.tensor_copy(y4[1], bank(5)).then_inc(sem["y4_dve"], 1)

            before = ch.n
            with dve.Fori(0, DEPTH2) as L:
                ch.base, ch.n = dve.snap(LINKS * L + before), 0

                def lo(j, n):
                    dve.wait_ge(sem["w_hi"], 3 * LAYER_N * L + n + 1)
                    dve.tensor_tensor(wl[j], raw[j], wh[j].bitcast(F32), ALU.subtract).then_inc(raw_free[j], 1)

                def lo_first(f):
                    for j in range(2):
                        lo(j, 3 * (STEPS + MIX_N) * f + j)

                def ffn(f):
                    q, n = STEPS * (2 * L + f), 3 * (STEPS + MIX_N) * f + 2

                    def step(c, s, last=False):
                        i = 3 * s
                        if not last:
                            lo(0, n + i)
                        dve.wait_ge(raw_free[2], nth(L, f, s) + 1)
                        dve.wait_ge(sem["sil_done"], q + s + 1)
                        dve.scalar_tensor_tensor(f_hid[c].rearrange("p f s -> p (f s)"), f_sil[c], 0.5, bank(6 + c), ALU.mult, ALU.mult)\
                            .then_inc(sem["hid_t"], 1)
                        if not last:
                            lo(1, n + i + 1)
                        lo(2, n + i + (0 if last else 2))
                        dve.wait_ge(sem["hid_h"], q + s + 1)
                        dve.tensor_tensor(hidl[c].rearrange("p f s -> p (f s)"), f_hid[c].rearrange("p f s -> p (f s)"),
                                          hidh[c].rearrange("p f s -> p (f s)").bitcast(F32), ALU.subtract).then_inc(sem["hid_done"], 1)

                    with dve.Fori(0, STEPS // 2) as i:
                        step(0, 2 * i)
                        step(1, 2 * i + 1)
                    step(0, STEPS - 1, last=True)

                def lo_mix(m):
                    lo(m % 3, 3 * STEPS + m)

                dve.tensor_scalar(prm, prm_all[:, bass.ds(L, 1), :].rearrange("p l n -> p (l n)"), 1.0, None, ALU.mult)\
                    .then_inc(sem["prm_ready"], 1)
                lo_first(0)
                update((sem["stage_done"], NE + L))
                dve.wait_ge(sem["prm_ready"], L + 1)
                dve.wait_ge(sem["x_dve"], 3 * L + 2)
                norm(3 * L + 2, pf("norm0"), 14 * L)
                ch.link(dve.tensor_scalar(lc_y, pf("lam"), -1.0, None, ALU.mult))
                dve.tensor_tensor(lc_ab, lc_y, pf("lam"), ALU.max).then_inc(sem["lru_u"], 1)
                for i, (a, b) in enumerate((("lq1", "lk1"), ("lq2", "lk2"))):
                    v = dve.tensor_tensor_reduce(lam_j, pf(a), pf(b), 1.0, 0.0, ALU.mult, ALU.add, lamv[:, i:i + 1])
                    ch.link(v) if i == 0 else v.then_inc(sem["d_lamx"], 1)
                dve.wait_ge(sem["lru_c"], L + 1)
                ch.link(dve.tensor_scalar(lc_den, lc_u, 2.0, None, ALU.add))
                ch.link(dve.reciprocal(lc_den, lc_den))
                ch.link(dve.tensor_tensor(lc_z, lc_u, lc_den, ALU.mult))
                ch.link(dve.tensor_tensor(lc_z2, lc_z, lc_z, ALU.mult))
                ch.link(dve.tensor_scalar(lc_p, lc_z2, 1.0 / (2 * LOG1P_TERMS - 1), None, ALU.mult))
                for i in range(LOG1P_TERMS - 2, -1, -1):
                    ch.link(dve.scalar_tensor_tensor(lc_p, lc_p, 1.0 / (2 * i + 1), lc_z2 if i else lc_z, ALU.add, ALU.mult))
                ch.link(dve.tensor_scalar(lc_y, lc_y, 0.0, None, ALU.max))
                ch.link(dve.scalar_tensor_tensor(lc_p, lc_p, 2.0, lc_y, ALU.mult, ALU.add))
                dve.tensor_scalar(lc_c, lc_p, -LRU_C, None, ALU.mult)
                dve.tensor_scalar(lc_n, lc_p, LRU_C, None, ALU.mult).then_inc(sem["lru_b"], 1)
                dve.wait_ge(sem["d_lame"], L + 1)
                ch.link(dve.tensor_tensor(lamv[:, 4:5], lamv[:, 3:4], lamv[:, 2:3], ALU.subtract))
                ch.step(dve.tensor_tensor(lamv[:, 5:6], lamv[:, 4:5], pf("lam0"), ALU.subtract))
                ch.step(dve.tensor_tensor(lamv[:, 6:7], pf("subg"), pf("oml"), ALU.mult))
                neg_lam, sub_gain = lamv[:, 5:6], lamv[:, 6:7]
                ffn(0)

                lo_mix(0)
                lo_mix(1)
                update((sem["acc_done"], 2 * L + 2))
                dve.wait_ge(sem["x_dve"], 3 * L + 3)
                norm(3 * L + 3, pf("norm1"), 14 * L + 4)
                for m in range(2, 6):
                    lo_mix(m)
                dve.wait_ge(sem["pads_zero"], 2)
                dve.wait_ge(*used_mix(L, 3))
                dve.wait_ge(sem["z2_0"], L + 1)
                ch.step(dve.tensor_tensor(sc_pad[:, :, 2:2 + S], scbc[:, 2:4, :], bank(2).rearrange("p (c s) -> p c s", c=2), ALU.mult))
                dve.tensor_copy(lx_pad[:, :, 3:3 + S], bank(3).rearrange("p (c s) -> p c s", c=2)).then_inc(sem["z2_1"], 1)
                lo_mix(6)
                dve.wait_ge(sem["z2_1"], L + 1)
                for c in range(2):
                    ch.step(dve.tensor_scalar(xr[:, c, :], lx_pad[:, c, 0:S], pf("lruw", 4 * c), pf("lrub", c), ALU.mult, ALU.add))
                for k in range(1, 4):
                    ch.settle()
                    for c in range(2):
                        v = dve.scalar_tensor_tensor(xr[:, c, :], lx_pad[:, c, k:k + S], pf("lruw", 4 * c + k), xr[:, c, :],
                                                     ALU.mult, ALU.add)
                        if k < 3 or c == 0:
                            ch.step(v)
                v.then_inc(sem["lru_xr"], 1)
                lo_mix(7)
                ch.settle()
                for c in range(2):
                    ch.step(dve.tensor_scalar(yc[:, c, :], sc_pad[:, c, 0:S], pf("scw", 3 * c), None, ALU.mult))
                for k in range(1, 3):
                    ch.settle()
                    for c in range(2):
                        ch.step(dve.scalar_tensor_tensor(yc[:, c, :], sc_pad[:, c, k:k + S], pf("scw", 3 * c + k), yc[:, c, :],
                                                         ALU.mult, ALU.add))
                ch.settle()
                ch.step(dve.tensor_tensor(yc, yc, scbc[:, 0:2, :], ALU.mult))
                lo_mix(8)
                dve.wait_ge(sem["z2_2"], L + 1)
                ch.link(dve.tensor_tensor(lg, lgate, lgate, ALU.mult))
                ch.link(dve.tensor_scalar(lg, lg, 0.044715, 1.0, ALU.mult, ALU.add))
                dve.tensor_tensor(lg, lg, lgate, ALU.mult).then_inc(sem["gelu_in"], 1)
                lo_mix(9)
                lo_mix(10)
                dve.wait_ge(sem["gelu_t"], L + 1)
                ch.step(dve.scalar_tensor_tensor(lg, lg, 1.0, lgate, ALU.add, ALU.mult))
                dve.wait_ge(sem["lru_a"], L + 1)
                ch.link(dve.tensor_scalar(rg, lm, 1.0, None, ALU.add))
                ch.link(dve.reciprocal(rg, rg))
                ch.link(dve.scalar_tensor_tensor(lm, lm, 2.0, rg, ALU.mult, ALU.mult))
                dve.tensor_scalar(lm, lm, SQRT_LEAST, None, ALU.max).then_inc(sem["lru_m"], 1)
                dve.wait_ge(sem["lru_xr"], L + 1)
                ch.link(dve.tensor_tensor(ig, ig, xr, ALU.mult))
                lo_mix(11)
                dve.wait_ge(sem["lru_sq"], L + 1)
                ch.link(dve.tensor_tensor(lm, lm, ig, ALU.mult))
                for c in range(2):
                    ch.step(dve.tensor_tensor_scan(xr[:, c, :], la[:, c, :], lm[:, c, :], 0.0, ALU.mult, ALU.add))
                ch.settle()
                ch.link(dve.scalar_tensor_tensor(lg.rearrange("p c s -> p (c s)"), lg.rearrange("p c s -> p (c s)"), 0.5,
                                                 xr.rearrange("p c s -> p (c s)"), ALU.mult, ALU.mult))
                lo_mix(12)

                def maxima2(g):
                    t, n = g // 2, P * (g // 2 + 1)
                    dve.wait_ge(sem["d_ps"], 4 * L + g + 1)
                    dve.memset(hold[:, 0:1], 0.0)
                    for m in range(2):
                        for i in range(2):
                            h, c = 2 * (g % 2) + i, 4 * g + 2 * m + i
                            ch.step(dve.tensor_tensor_reduce(d_e[:, g % 2, m, i, 0:n], bank(6 - 2 * (g % 2) + m)[:, i * S:i * S + n],
                                                             tb[:, 2 * h + m, S - n:S], 1.0, -3e38, ALU.add, ALU.max, d_mx[:, c:c + 1]))
                    ch.settle()
                    dve.tensor_scalar(d_nm[:, 4 * g:4 * g + 4], d_mx[:, 4 * g:4 * g + 4], -1.0, None, ALU.mult).then_inc(sem["d_nmx"], 1)

                def combine(g):
                    n = P * (g // 2 + 1)
                    dve.wait_ge(sem["d_exp"], 4 * L + g + 1)
                    ch.link(dve.reciprocal(d_rd[:, 4 * g:4 * g + 4], d_den[:, 4 * g:4 * g + 4]))
                    ch.step(dve.tensor_scalar(d_c1[:, 2 * g:2 * g + 2], d_rd[:, 4 * g + 2:4 * g + 4], neg_lam, None, ALU.mult))
                    if g >= 1:
                        dve.wait_ge(sem["dT_ps"], 4 * L + g)
                    for i in range(2):
                        ch.step(dve.tensor_scalar(d_attn[:, i, 0:n], d_e[:, g % 2, 0, i, 0:n], d_rd[:, 4 * g + i:4 * g + i + 1],
                                                  None, ALU.mult))
                    ch.settle()
                    for i in range(2):
                        v = dve.scalar_tensor_tensor(d_attn[:, i, 0:n], d_e[:, g % 2, 1, i, 0:n], d_c1[:, 2 * g + i:2 * g + i + 1],
                                                     d_attn[:, i, 0:n], ALU.mult, ALU.add)
                    v.then_inc(sem["d_comb"], 1)

                dve.wait_ge(sem["tb_done"], 1)
                maxima2(0)
                maxima2(1)
                combine(0)
                dve.wait_ge(*used_mix(L, 10))
                dve.tensor_copy(v2.rearrange("p t c -> p (t c)"), bank(0, 2)).then_inc(sem["z2_v"], 1)
                ch.link(dve.tensor_copy(xTh[:, 4:8, :], y_cl))
                dve.tensor_tensor(xTl[:, 4:8, :], y_cl, xTh[:, 4:8, :].bitcast(F32), ALU.subtract).then_inc(sem["y_done"], 1)
                maxima2(2)
                combine(1)
                lo_mix(13)
                maxima2(3)
                combine(2)
                combine(3)
                dve.wait_ge(sem["do_sq"], L + 1)
                ch.link(dve.tensor_reduce(d_ss[:, 0:8], f_buf[:, 0:1024].rearrange("p (h d) -> p h d", d=P), AX.X, ALU.add))
                mean_eps(d_ms[:, 0:8], d_ss[:, 0:8], P, SUBLN_EPS).then_inc(sem["do_ms"], 1)
                dve.wait_ge(sem["do_std"], L + 1)
                ch.link(dve.reciprocal(d_ss[:, 8:16], d_std[:, 0:8]))
                for t in range(TT):
                    v = dve.tensor_tensor(xn[:, t, 0:512].rearrange("p (h d) -> p h d", d=P),
                                          bank(t).rearrange("p (h d) -> p h d", d=P),
                                          d_ss[:, 8 + 4 * t:12 + 4 * t].unsqueeze(2).to_broadcast([P, DH, P]), ALU.mult)
                v.then_inc(sem["do_nrm"], 1)
                for c in range(2):
                    dve.wait_ge(sem["xT_hi"], 14 * L + 9 + c)
                    dve.scalar_tensor_tensor(xTl[:, 2 * c:2 * c + 2, :].rearrange("p k s -> p (k s)"), bank(2 + c), sub_gain,
                                             xTh[:, 2 * c:2 * c + 2, :].rearrange("p k s -> p (k s)").bitcast(F32),
                                             ALU.mult, ALU.subtract).then_inc(sem["xT_lo"], 1)
                lo_mix(14)
                lo_first(1)
                update((sem["acc_done"], 2 * L + 3), 6)
                dve.wait_ge(sem["x_dve"], 3 * L + 4)
                norm(3 * L + 4, pf("norm2"), 14 * L + 10)
                ffn(1)
            assert ch.n == LINKS, ch.n

            ch.base, ch.n = DEPTH2 * LINKS + before, 0
            update((sem["stage_done"], NE + DEPTH2))
            dve.wait_ge(sem["x_dve"], 3 * DEPTH2 + 2)
            squares()
            means(3 * DEPTH2 + 2)
            dve.wait_ge(sem["std_ready"], 3 * DEPTH2 + 3)
            ch.link(dve.reciprocal(n_rstd, n_std))
            for t in range(TT):
                dve.scalar_tensor_tensor(xn[:, t, :], x[:, t, :], n_rstd[:, t:t + 1], fin_row, ALU.mult, ALU.mult)\
                    .then_inc(sem["fin_put"], 1)

        @block.gpsimd
        def _(pool):
            pool.memset(at_diag, 0.0).then_inc(sem["masks_zero"], 1)
            pool.memset(ones_s, 1.0).then_inc(sem["masks_zero"], 1)
            e_q = HH * S
            for i in range(NLEV + 1):
                if i < NLEV:
                    pool.wait_ge(sem["lev_exp"], i + 1)
                if i == 0:
                    pool.wait_ge(sem["k_scaled"], 2)
                if i >= 1:
                    pool.wait_ge(sem["lev_ps"], i)
                if i < NLEV:
                    w = LEVELS[i]
                    n = HH * S // (2 * w)

                    def halves(a):
                        return a.rearrange("p (n f w) -> p n f w", n=n, f=2)

                    ek, kl = halves(lev_e[i % 2][:, e_q:2 * e_q]), halves(lev_qk[:, e_q:2 * e_q])
                    kf_n, kb_n = [halves(k.rearrange("p h s -> p (h s)")) for k in (kf, kb)]
                    pool.tensor_tensor(kl[:, :, 0, :], kf_n[:, :, 0, :], ek[:, :, 0, :], ALU.mult)
                    pool.tensor_tensor(kl[:, :, 1, :], kb_n[:, :, 1, :], ek[:, :, 1, :], ALU.mult).then_inc(sem["lev_k"], 1)
                else:
                    pool.tensor_tensor(lev_qk[:, e_q:2 * e_q], kf.rearrange("p h s -> p (h s)"),
                                       kb.rearrange("p h s -> p (h s)"), ALU.add).then_inc(sem["lev_k"], 1)
            pool.wait_ge(sem["z_hg"], 1)
            gs = gs_tok.rearrange("p t n -> p (t n)").rearrange("p (h d) -> p h d", d=HD)
            pool.tensor_tensor(gs, gs, one_f("onorm").unsqueeze(1).to_broadcast([P, TT * HH, HD]), ALU.mult).then_inc(sem["gs_done"], 1)
            pool.wait_ge(sem["acc_done"], 1)
            pool.memset(ones_e, 1.0).then_inc(sem["masks_zero"], 1)
            pool.wait_ge(sem["used0"], 2 * NE)
            for j in range(3):
                pool.memset(hold[:, 1 + j:2 + j], 0.0).then_inc(raw_free[j], 1)
            pool.wait_ge(sem["stage_done"], NE)
            pool.memset(sc_pad[:, :, 0:2], 0.0).then_inc(sem["pads_zero"], 1)
            pool.memset(lx_pad[:, :, 0:3], 0.0).then_inc(sem["pads_zero"], 1)
            pool.wait_ge(sem["tb_in"], 16)
            pool.tensor_copy(tb, tb_raw[:, :, ::-1]).then_inc(sem["tb_done"], 1)


def kernel(**inputs):
    import concourse.bacc as bacc
    from concourse.bass_utils import run_bass_kernel_spmd

    a = {k: np.asarray(v) for k, v in inputs.items()}
    small, band, onehot, future = const_arrays()

    def cols(v):
        return np.reshape(v, (-1, P)).T

    def rows(v):
        return np.broadcast_to(np.reshape(v, (1, -1)), (P, v.size))

    def taps(w):
        return np.reshape(np.transpose(np.reshape(w, (w.shape[0], -1, P)), (2, 1, 0)), (P, -1))

    def diagonal(w):
        out = np.zeros((P, 2, P), np.float32)
        for i in range(4):
            r = 64 * (i % 2)
            out[r:r + 64, i // 2, r:r + 64] = w[i]
        return out.reshape(P, -1)

    lbs = [cols(a[n][r]) for r in range(2) for n in ("hgrn_lb_fwd", "hgrn_lb_bwd")]
    router = np.reshape(np.transpose(np.reshape(a["w_router"][0], (KD, P, NE)), (1, 0, 2)), (P, -1))
    one = np.concatenate([cols(a["norm1_w"][0]), cols(a["norm2_w"][0]),
                          np.tile(a["attn_q_norm_w"][0], 2)[:, None], np.tile(a["attn_k_norm_w"][0], 2)[:, None],
                          *lbs, rows(a["hgrn_out_norm_w"][0]), router], axis=1)
    layers = []
    for l in range(DEPTH2):
        lam0 = 0.8 - 0.6 * math.exp(-0.3 * l)
        layers.append(np.concatenate(
            [cols(a[n + "_norm_2"][l]) for n in ("ffn1", "mix", "ffn2")]
            + [rows(a[n + "_2"][l]) for n in ("lam_q1", "lam_k1", "lam_q2", "lam_k2")]
            + [cols(a["subln_gain_2"][l]), np.full((P, 1), lam0, np.float32), np.full((P, 1), 1.0 - lam0, np.float32),
               taps(a["sc_conv_w_2"][l]), taps(a["lru_conv_w_2"][l]), cols(a["lru_conv_b_2"][l]), cols(a["lru_ba_2"][l]),
               cols(a["lru_bx_2"][l]), cols(a["lru_lambda_2"][l]), diagonal(a["lru_wa_2"][l]), diagonal(a["lru_wx_2"][l])],
            axis=1))
    feed = [("x", a["x"][0]), ("w_in", a["w_in"][0]), ("w_out", a["w_out"][0]), ("w_expert_gate", a["w_expert_gate"][0]),
            ("w_expert_up", a["w_expert_up"][0]), ("w_expert_down", a["w_expert_down"][0]), ("rel_bias", a["rel_bias_2"]),
            ("ffn1_gate", a["ffn1_gate_2"]), ("ffn1_up", a["ffn1_up_2"]), ("ffn1_down", a["ffn1_down_2"]),
            ("w_in_2", a["w_in_2"]), ("w_out_2", a["w_out_2"]),
            ("ffn2_gate", a["ffn2_gate_2"]), ("ffn2_up", a["ffn2_up_2"]), ("ffn2_down", a["ffn2_down_2"]),
            ("small_constants", small), ("band_constants", band), ("bucket_constants", onehot), ("future_constants", future),
            ("first_block_params", one), ("layer_params", np.stack(layers)), ("final_norm", rows(a["final_norm_2"]))]
    nc = bacc.Bacc("TRN2", target_bir_lowering=False, num_devices=1)
    arrays, args = {}, []
    for name, v in feed:
        v = np.ascontiguousarray(v, dtype=np.float32)
        arrays[name] = v
        args.append(nc.dram_tensor(name, v.shape, F32, kind="ExternalInput").ap())
    args.append(nc.dram_tensor("out", (S, D), F32, kind="ExternalOutput").ap())
    two_blocks(nc, *args)
    r = run_bass_kernel_spmd(nc, [arrays], core_ids=[0])
    return r.results[0]["out"].reshape(1, S, D)
```

```python
import math
from contextlib import ExitStack

import numpy as np

import concourse.bass as bass
from concourse import mybir

F32 = mybir.dt.float32
F32R = mybir.dt.float32r
U32 = mybir.dt.uint32
ALU = mybir.AluOpType
ACT = mybir.ActivationFunctionType
AX = mybir.AxisListType

P = 128
S = 256
D = 1024
TT = S // P
KD = D // P
BANK = 512
EPS = 1e-6

AH, AD = 8, 64
HH, HD = 4, 128
PATTERNS = ((128, 1), (512, 4), (2048, 16))
NE = 16
CAP = 2 * S // NE
FE = 1024
Q4 = P // CAP
LN_LEAST = 2.0 ** -64
SQRT_LEAST = 2.0 ** -116
LEVELS = [S >> (i + 1) for i in range(int(math.log2(S)))]

DEPTH2 = 2
DH, DM = 4, 64
NBUCKET, MAXDIST = 32, 128
SUBLN_EPS = 1e-5
LRU_C = 8.0
GELU_C = math.sqrt(2.0 / math.pi)
DFF = 2816
FS = 256
STEPS = DFF // FS
PIECE = KD * FS
Z_COLS = [1536, 1792, 2048, 2304, 2560, 0, 256, 512, 768, 1024, 1280]
O_ROWS = [512, 768, 0, 256]
MIX = len(Z_COLS) + len(O_ROWS)
GATE, UP, DOWN = range(3)
TBW = P + S - 1
LOG1P_TERMS = 8
NEG = -1e30
LINKS = 84


def fields(*sizes):
    at, out = 0, {}
    for name, n in sizes:
        out[name] = (at, at + n)
        at += n
    return out, at


CONST, CONST_W = fields(("ident", P), ("fold", CAP), ("rank", CAP))
BAND_W = P + S
BAND, BAND_N = fields(("bias", AH * BAND_W), ("count", BAND_W), ("mask", len(LEVELS) * P))
ONE, ONE_N = fields(("norm1", KD), ("norm2", KD), ("q", 1), ("k", 1), ("lb", 4 * HH), ("onorm", HD),
                    ("router", KD * NE))
PRM, PRM_N = fields(("norm0", KD), ("norm1", KD), ("norm2", KD), ("lq1", DM), ("lk1", DM), ("lq2", DM),
                    ("lk2", DM), ("subg", 1), ("lam0", 1), ("oml", 1), ("scw", 6), ("lruw", 8), ("lrub", 2),
                    ("ba", 2), ("bx", 2), ("lam", 2), ("wa", 2 * P), ("wx", 2 * P))


def const_arrays():
    small = np.zeros((P, CONST_W), np.float32)
    small[:, CONST["ident"][0]:CONST["ident"][1]] = np.eye(P)
    small[:, CONST["fold"][0]:CONST["fold"][1]] = np.tile(np.eye(CAP), (Q4, 1))
    small[:, CONST["rank"][0]:CONST["rank"][1]] = np.arange(1, CAP + 1)
    dist = np.abs(P + np.arange(P)[:, None] - np.arange(BAND_W)[None, :])
    count = sum(((dist % dil == 0) & (dist // dil <= win // (2 * dil))).astype(np.float32) for win, dil in PATTERNS)
    slopes = np.exp2(-8.0 * np.arange(1, AH + 1, dtype=np.float32) / AH)
    bias = [np.where(count > 0, -s * dist, NEG) for s in slopes]
    s_at, t_at = np.arange(P)[:, None], np.arange(P)[None, :]
    masks = [(s_at // (2 * w) == t_at // (2 * w)) & (s_at // w != t_at // w) for w in LEVELS[1:]] + [s_at == t_at]
    band = np.concatenate(bias + [count] + masks, axis=1).astype(np.float32)
    n = np.arange(TBW + 1) - (P - 1)
    exact = NBUCKET // 2
    large = exact + (np.log(np.maximum(n, 1).astype(np.float32) / exact) / math.log(MAXDIST / exact)
                     * (NBUCKET - exact)).astype(np.int32)
    bucket = np.where(n < exact, n, np.minimum(large, NBUCKET - 1))
    onehot = ((bucket[None, :] == np.arange(NBUCKET)[:, None]) & (n >= 0)).astype(np.float32)
    future = np.tile(np.where(n < 0, NEG, 0.0), (2 * DH, 1)).astype(np.float32)
    return small, band, onehot, future


def buffer_plan():
    pieces, products, runs = [0] * 3, [0] * 3, {}
    for f in range(2):
        for r in range(3):
            b, n = (f + r) % 3, STEPS - (r == DOWN)
            runs["ffn", f, r] = b, pieces[b], products[b]
            pieces[b], products[b] = pieces[b] + n, products[b] + n
        runs["last", f] = f, pieces[f]
        pieces[f] += 1
        for m in range(MIX if f == 0 else 0):
            b = (m + 1) % 3
            runs["mix", m] = b, pieces[b], products[b]
            pieces[b], products[b] = pieces[b] + 1, products[b] + (m < MIX - 1)
    return runs, pieces, products


class Chain:

    def __init__(self, eng, counter):
        self.eng, self.counter, self.n, self.base = eng, counter, 0, 0

    def step(self, ins):
        ins.then_inc(self.counter, 1)
        self.n += 1

    def settle(self):
        self.eng.wait_ge(self.counter, self.base + self.n)

    def link(self, ins):
        self.step(ins)
        self.settle()


def two_blocks(nc, x_in, w_in, w_out, wg, wu, wd, relb, f1g, f1u, f1d, w_in2, w_out2, f2g, f2u, f2d,
               const, band, onehot, future, one, prm_in, fin_w, out):
    with ExitStack() as ctx:
        def sb(name, n):
            return ctx.enter_context(nc.sbuf_tensor(name, [P, n], F32))

        SLOT = KD * 512
        def sb_r(name, n, stack=ctx):
            return stack.enter_context(nc.sbuf_tensor(name, [P, n], F32R))

        with nc.sbuf_tensor("ring", [P, 6 * SLOT], F32) as ring:
            pass
        with ExitStack() as first:
            first.enter_context(nc.sbuf_tensor("mixers_place", [P, 3 * SLOT], F32))
            w1h_sb, w1l_sb = sb_r("w1h_sb", 3 * PIECE, first), sb_r("w1l_sb", 3 * PIECE, first)
        raw_sb = sb("raw_sb", 3 * PIECE)
        wh_sb, wl_sb = sb_r("wh_sb", 3 * PIECE), sb_r("wl_sb", 3 * PIECE)
        xTh_sb, xTl_sb = sb_r("xTh_sb", KD * S), sb_r("xTl_sb", KD * S)
        hidh_sb, hidl_sb = sb_r("hidh_sb", 1024), sb_r("hidl_sb", 1024)
        x_sb = sb("x_sb", TT * D)
        with nc.sbuf_tensor("xT_sb", [P, KD * S], F32) as xT_sb:
            pass
        x1h_sb = sb_r("x1h_sb", KD * S)
        xn_sb = sb("xn_sb", TT * D)
        const_sb = sb("const_sb", CONST_W)
        one_sb = sb("one_sb", ONE_N)
        stat = sb("stat", 256)
        diag_sb = sb("diag_sb", TT * P)
        WORK = 19968
        with nc.sbuf_tensor("work", [P, WORK], F32) as work:
            pass
        x1l_sb = sb_r("x1l_sb", KD * S)
        sb("work_rest", WORK - KD * S)
        ps = ctx.enter_context(nc.psum_tensor("ps", [P, 8 * BANK], F32))
        tb_dram = nc.dram_tensor("rel_bias_band", [2 * DH, TBW + 1], F32, kind="Internal")

        x = x_sb[:, :].rearrange("p (t d) -> p t d", t=TT)
        xT = xT_sb[:, :].rearrange("p (k s) -> p k s", k=KD)
        xn = xn_sb[:, :].rearrange("p (t d) -> p t d", t=TT)
        diag = diag_sb[:, :].rearrange("p (t s) -> p t s", t=TT)
        ident = const_sb[:, CONST["ident"][0]:CONST["ident"][1]]
        fold = const_sb[:, CONST["fold"][0]:CONST["fold"][1]]
        rank = const_sb[:, CONST["rank"][0]:CONST["rank"][1]]

        def slot(s, n=512):
            return ring[:, s * SLOT:s * SLOT + KD * n].rearrange("p (k n) -> p k n", k=KD)

        def bank(b, n=1):
            return ps[:, b * BANK:(b + n) * BANK]

        def one_f(name):
            return one_sb[:, ONE[name][0]:ONE[name][1]]

        at = [0]

        def st(n):
            at[0] += n
            assert at[0] <= 256
            return stat[:, at[0] - n:at[0]]

        LAST = 3 * DEPTH2 + 2
        ALL, LEFT, RIGHT = slice(0, D), slice(0, D // 2), slice(D // 2, D)
        n_ss, n_eps, n_std, n_rstd, hold = st(3), st(1), st(TT), st(TT), st(6)
        lbm, lbe, lbr, lb, oml = st(8), st(16), st(8), st(8), st(8)
        qk_ss, qk_ms, qk_std, qk_rstd = st(32), st(32), st(32), st(32)

        def region(buf, n, start=0):
            pos = [start]

            def take(size):
                pos[0] += size
                assert pos[0] <= n, (pos[0], n)
                return buf[:, pos[0] - size:pos[0]]
            return take

        t1 = region(work, WORK, KD * S)
        hq, kf, kb, bc, rc = [t1(HH * S).rearrange("p (h s) -> p h s", h=HH) for _ in range(5)]
        v_tok, hi_tok, gs_tok = [t1(TT * 512).rearrange("p (t c) -> p t c", t=TT) for _ in range(3)]
        qT, kT = [t1(4 * S).rearrange("p (c s) -> p c s", c=4) for _ in range(2)]
        at_diag, at_off = [t1(HH * TT * P).rearrange("p (h t c) -> p h t c", h=HH, t=TT) for _ in range(2)]
        a_place = t1(10 * S)
        a_s = [a_place[:, 2 * S * i:2 * S * i + 2 * S].rearrange("p (h s) -> p h s", h=2) for i in range(3)]
        a_eT = [a_place[:, 2 * S * i:2 * S * i + 2 * S].rearrange("p (h j s) -> p h j s", h=2, j=TT) for i in (3, 4)]
        abias = t1(AH * BAND_W).rearrange("p (h i) -> p h i", h=AH)
        r1 = region(ring, 2 * SLOT)
        lev_e = [r1(2 * HH * S) for _ in range(2)]
        lev_qk = [r1(2 * HH * S), a_place[:, 0:2 * HH * S]]
        count = r1(BAND_W)
        masks = r1(len(LEVELS) * P).rearrange("p (l s) -> p l s", l=len(LEVELS))
        a_st = r1(4 * 16)
        a_mx, a_nm, a_den, a_rden = [a_st[:, 16 * i:16 * i + 16] for i in range(4)]
        o_st = st(4 * 8)
        o_ss, o_ms, o_std, o_rstd = [o_st[:, 8 * i:8 * i + 8] for i in range(4)]
        ones_s = r1(S)
        sqj = a_place[:, 0:2 * TT * 512].rearrange("p (c t n) -> p c t n", c=2, t=TT)
        ho_sqj = a_place[:, 0:TT * 512]
        raw1 = [ring[:, 2 * SLOT + j * PIECE:2 * SLOT + (j + 1) * PIECE] for j in range(2)]
        w1h, w1l = [[b[:, j * PIECE:(j + 1) * PIECE] for j in range(3)] for b in (w1h_sb, w1l_sb)]
        x1h, x1l = [b[:, :].rearrange("p (k s) -> p k s", k=KD) for b in (x1h_sb, x1l_sb)]
        aq_tok = xn_sb[:, 0:1024].rearrange("p (t c) -> p t c", t=TT)
        ak_tok = xn_sb[:, 1024:2048].rearrange("p (t c) -> p t c", t=TT)
        mixed = xn

        LATE = 2 * PRM_N + 2 * DH * S + D + (TBW + 1) * 3 + 2 * DH
        t2 = region(work, WORK - LATE + D)
        hot = t2(TT * (NE + 1) * CAP).rearrange("p (t e c) -> p t e c", t=TT, e=NE + 1)
        hot_next = t2(TT * CAP).rearrange("p (t c) -> p t c", t=TT)
        aff = t2(TT * NE).rearrange("p (t e) -> p t e", t=TT)
        aff_e = t2(TT * NE).rearrange("p (t e) -> p t e", t=TT)
        posT = t2(TT * NE).rearrange("p (t e) -> p t e", t=TT)
        r_mx, r_nm, r_sum, r_rec = t2(TT), t2(TT), t2(TT), t2(TT)
        affT, topw, chosen, place, ones_e = [t2(S)[0:NE, :] for _ in range(5)]
        top8 = t2(8)[0:NE, :]
        hot_e = t2(TT * P).rearrange("p (t j c) -> p t j c", t=TT, j=Q4)
        back = t2(S)
        xin = t2(KD * CAP).rearrange("p (k c) -> p k c", k=KD)
        g4, u4, y4 = [[t2(512) for _ in range(2)] for _ in range(3)]
        e_sil = [t2(4 * CAP) for _ in range(2)]
        hidT = t2(KD * CAP).rearrange("p (k c) -> p k c", k=KD)
        odd_slot = [t2(SLOT).rearrange("p (k n) -> p k n", k=KD) for _ in range(2)]

        t3 = region(work, WORK, WORK - LATE)
        fin_row = t3(D)
        prm_all = t3(2 * PRM_N).rearrange("p (l n) -> p l n", l=2)
        tb_raw = t3(2 * DH * S).rearrange("p (h i) -> p h i", h=2 * DH)
        tb_rows, tb_future = t3(TBW + 1)[0:2 * DH, :], t3(TBW + 1)[0:2 * DH, :]
        tb_onehot, tb_rel = t3(TBW + 1)[0:NBUCKET, :], t3(2 * DH)[0:NBUCKET, :]
        t4 = region(work, WORK - LATE)
        prm = t4(PRM_N)
        tb = t4(2 * DH * S).rearrange("p (h i) -> p h i", h=2 * DH)
        f_buf = t4(4 * 512)
        f_sil = [f_buf[:, 512 * i:512 * i + 512] for i in range(2)]
        f_hid = [f_buf[:, 1024 + 512 * i:1536 + 512 * i].rearrange("p (f s) -> p f s", f=2) for i in range(2)]
        raw_place = tb_raw.rearrange("p h i -> p (h i)")
        qT2, scbc = [raw_place[:, 1024 * i:1024 * i + 1024].rearrange("p (c s) -> p c s", c=4) for i in range(2)]
        kT2 = t4(4 * S).rearrange("p (c s) -> p c s", c=4)
        v2 = t4(TT * 512).rearrange("p (t c) -> p t c", t=TT)
        sc_pad = t4(2 * (S + 2)).rearrange("p (c s) -> p c s", c=2)
        lx_pad = t4(2 * (S + 3)).rearrange("p (c s) -> p c s", c=2)
        lgate, xr, rg, ig, la, lm = [t4(2 * S).rearrange("p (c s) -> p c s", c=2) for _ in range(6)]
        y_cl = t4(4 * S).rearrange("p (c s) -> p c s", c=4)
        yc, lg = y_cl[:, 0:2, :], y_cl[:, 2:4, :]
        la_lm = [b.rearrange("p c s -> p (c s)") for b in (la, lm)]
        d_e = [e.rearrange("p (m h s) -> p m h s", m=2, h=2) for e in (la_lm[0], la_lm[1], f_buf[:, 0:1024], f_buf[:, 1024:2048])]
        d_sq = [d_e[t].rearrange("p m h s -> p (m h s)") for t in range(TT)]
        d_attn = [t4(2 * S).rearrange("p (h s) -> p h s", h=2) for _ in range(2)]
        d_aT = t4(2 * S).rearrange("p (h j s) -> p h j s", h=2, j=2)
        lc = t4(32)
        lc_y, lc_ab, lc_u, lc_den, lc_z, lc_z2, lc_p, lc_c, lc_n = [lc[:, 2 * i:2 * i + 2] for i in range(9)]
        lamv = t4(8)
        d_st = t4(8 * 16)
        d_mx, d_nm, d_den, d_rd, d_c1, d_ss, d_ms, d_std = [d_st[:, 16 * i:16 * i + 16] for i in range(8)]
        lam_j = t4(DM)
        raw, wh, wl = [[b[:, j * PIECE:(j + 1) * PIECE] for j in range(3)] for b in (raw_sb, wh_sb, wl_sb)]

        def by_cols(w):
            return w.rearrange("p (k n) -> p k n", k=KD)

        def by_rows(w):
            return w.rearrange("p (k n) -> p k n", n=D)

        xTh, xTl = [b[:, :].rearrange("p (k s) -> p k s", k=KD) for b in (xTh_sb, xTl_sb)]
        hidh, hidl = [[b[:, 512 * c:512 * c + 512].rearrange("p (f s) -> p f s", f=2) for c in range(2)]
                      for b in (hidh_sb, hidl_sb)]
        y_h, y_l = [b[:, :].rearrange("p (c s) -> p c s", c=4) for b in (hidh_sb, hidl_sb)]
        O_LEFT = [(y_h[:, 0:2, :], y_l[:, 0:2, :]), (y_h[:, 2:4, :], y_l[:, 2:4, :]),
                  (xTh[:, 0:2, :], xTl[:, 0:2, :]), (xTh[:, 2:4, :], xTl[:, 2:4, :])]

        def d_scores(g, m, i):
            return bank(6 + m)[:, (2 * g + i) * P:(2 * g + i) * P + P] if g < 2 else bank(6 + m)[:, i * S:i * S + S]

        def pf(name, i=None):
            a, b = PRM[name]
            return prm[:, a:b] if i is None else prm[:, a + i:a + i + 1]

        names = """x_in0 x_in1 const_in one_in band_in mask_in w1_in0 w1_in1 w1_hi w1_lo ex_in0 ex_in1 ex_in2 ex_in3 ex_in4 ex_in5 odd_in0 odd_in1
            mxT_ps k_scaled late_in tb_out tb_in raw_in0 raw_in1 raw_in2 fin_out
            half_done sq_done ss_ready std_ready rstd_ready diag_dve diag_act xn_dve xn_act xnT_ps xT_act xT_dve acc_done x_act x_dve
            z_ready z_hq z_hf z_hb z_q z_k z_v z_hi z_hg
            lb_max lb_exp lb_done gate_sg gate_lf lev_sub lev_exp lev_q lev_k lev_ps lev_put
            qk_sq qk_ms qk_std qkT_ps qT_done kT_done
            sc_ps sc_nm sc_exp sc_cnt eT_ps eT_act eT_dve o_ps o_put ho_ps ho_sq ho_ms ho_std ho_put gs_done
            masks_zero lg_ps lg_nm lg_exp aff_done affT_ps place_done placeT_ps hot_done xin_ps
            xe_ready hote_done used0 used1 used2 back_ps g4_done u4_done back_done sum_ps esil_done ehid_done
            y4_act y4_dve stage_done tb_ps tb_rows_done tb_done
            raw_free0 raw_free1 raw_free2 w_hi xT_hi xT_lo prm_ready sil_done hid_t hid_h hid_done
            z2_0 z2_1 z2_2 z2_q z2_k z2_v
            lru_u lru_c lru_xr lru_ps lru_gates lru_a lru_m lru_sq lru_b gelu_in gelu_t y_done
            d_lamx d_lame d_ps d_nmx d_exp d_comb dT_ps dT_done do_ps do_sq do_ms do_std do_nrm yT_ps
            fin_put dve_chain pads_zero""".split()
        sem = {n: ctx.enter_context(nc.semaphore(n)) for n in names}
        w1_in = [sem["w1_in0"], sem["w1_in1"]]
        ex_in = [sem["ex_in0"], sem["ex_in1"], sem["ex_in2"], sem["ex_in3"], sem["ex_in4"], sem["ex_in5"]]
        raw_in = [sem["raw_in0"], sem["raw_in1"], sem["raw_in2"]]
        raw_free = [sem["raw_free0"], sem["raw_free1"], sem["raw_free2"]]
        used = [sem["used0"], sem["used1"], sem["used2"]]

        RUNS, PIECES, PRODUCTS = buffer_plan()

        def buf(f, r):
            return RUNS["ffn", f, r][0]

        def buf_mix(m):
            return RUNS["mix", m][0]

        def nth(L, f, r, s):
            return PIECES[buf(f, r)] * L + RUNS["ffn", f, r][1] + s

        def nth_last(L, f):
            return PIECES[f] * L + RUNS["last", f][1]

        def nth_mix(L, m):
            return PIECES[buf_mix(m)] * L + RUNS["mix", m][1]

        def used_ffn(L, f, r, s):
            return used[buf(f, r)], 2 * NE + PRODUCTS[buf(f, r)] * L + RUNS["ffn", f, r][2] + s + 1

        def used_mix(L, m):
            return used[buf_mix(m)], 2 * NE + PRODUCTS[buf_mix(m)] * L + RUNS["mix", m][2] + 1

        PROJ = [("q", 0, False), ("k", 1, False), ("v", 2, False), ("hf", 4, True), ("hb", 5, True), ("hq", 3, True),
                ("hi", 6, False), ("hg", 7, False)]
        Z_BANK = [2, 4, 0, 6, 4, 6, 4, 6]
        Z_READ = [sem["z_" + name] for name, _, _ in PROJ]
        W1_IN = 2 * len(PROJ)
        O1_ROWS = [0, 256, 512, 768]
        W1 = W1_IN + len(O1_ROWS)
        XT1 = 8
        NLEV = len(LEVELS)
        GROUPS = [(0, 2), (1, 3), (4, 6), (5, 7)]
        NG = TT * len(GROUPS)

        block = ctx.enter_context(nc.Block())

        @block.sync
        def _(sp):
            def weights(w, c0, n):
                return w.rearrange("(k p) n -> p k n", p=P)[:, :, c0:c0 + n]

            sp.dma_start(const_sb[:, :], const).then_inc(sem["const_in"], 16)
            for t in range(TT):
                sp.dma_start(x[:, t, :], x_in[t * P:t * P + P, :]).then_inc(sem["x_in1" if t else "x_in0"], 16)
            for p in range(W1):
                if p >= 2:
                    sp.wait_ge(sem["w1_lo"], p - 1)
                if p < W1_IN:
                    src = weights(w_in, 512 * PROJ[p // 2][1] + FS * (p % 2), FS)
                    sp.dma_start(by_cols(raw1[p % 2]), src).then_inc(w1_in[p % 2], 16)
                else:
                    r = O1_ROWS[p - W1_IN]
                    src = w_out[r:r + FS, :].rearrange("(k p) n -> p k n", p=P)
                    sp.dma_start(by_rows(raw1[p % 2]), src).then_inc(w1_in[p % 2], 16)
                if p == 0:
                    sp.dma_start(one_sb[:, :], one).then_inc(sem["one_in"], 16)
                if p == 3:
                    a, b = BAND["count"]
                    sp.dma_start(count, band[:, a:b]).then_inc(sem["band_in"], 16)
                    a, b = BAND["bias"]
                    sp.dma_start(abias.rearrange("p h i -> p (h i)"), band[:, a:b]).then_inc(sem["band_in"], 16)
                if p == 9:
                    a, b = BAND["mask"]
                    sp.dma_start(masks.rearrange("p l s -> p (l s)"), band[:, a:b]).then_inc(sem["mask_in"], 16)

            def half(row, w, c, to, landed):
                rows = w.rearrange("e d f -> (e d) f")[bass.ds(row, D), 512 * c:512 * c + 512]
                sp.dma_start(to, rows.rearrange("(k p) n -> p k n", p=P)).then_inc(landed, 16)

            def first_half(row, odd):
                half(row, wg, 0, odd_slot[0] if odd else slot(0), sem["odd_in0"] if odd else ex_in[0])
                half(row, wu, 0, odd_slot[1] if odd else slot(2), sem["odd_in1"] if odd else ex_in[2])

            REST = [(1, wg, 1), (3, wu, 1), (5, wd, 1), (4, wd, 0)]

            sp.wait_ge(sem["lev_q"], NLEV)
            sp.wait_ge(sem["lev_k"], NLEV)
            half(0, wg, 0, slot(0), ex_in[0])
            sp.wait_ge(sem["lev_put"], NLEV + 1)
            half(0, wg, 1, slot(1), ex_in[1])
            sp.wait_ge(sem["o_put"], TT)
            sp.wait_ge(sem["ho_put"], TT)
            sp.dma_start(prm_all, prm_in.rearrange("l p n -> p l n")).then_inc(sem["late_in"], 16)
            sp.dma_start(tb_future, future).then_inc(sem["late_in"], 16)
            sp.dma_start(tb_onehot, onehot).then_inc(sem["late_in"], 16)
            sp.dma_start(tb_rel, relb).then_inc(sem["late_in"], 16)
            sp.wait_ge(sem["w1_lo"], W1)
            half(0, wu, 0, slot(2), ex_in[2])
            sp.wait_ge(sem["acc_done"], 1)
            for i, w, c in REST[1:]:
                half(0, w, c, slot(i), ex_in[i])
            first_half(D, True)
            sp.wait_ge(sem["tb_rows_done"], 1)
            sp.dma_start(tb_dram.ap(), tb_rows).then_inc(sem["tb_out"], 16)

            def loads(e, j, downs_last=True):
                def value(v):
                    return v if isinstance(v, int) else sp.snap(v)

                half_free, free = value(2 * e + 1), value(2 * e + 2)
                row, row_next = value(D * e + D), value(D * e + 2 * D)

                def next_half(r, w):
                    sp.wait_ge(used[r], half_free)
                    half(row_next, w, 0, odd_slot[r] if j else slot(2 * r), sem[f"odd_in{r}"] if j else ex_in[2 * r])

                for r, w in enumerate((wg, wu)):
                    if downs_last:
                        next_half(r, w)
                    sp.wait_ge(used[r], free)
                    half(row, w, 1, slot(2 * r + 1), ex_in[2 * r + 1])
                sp.wait_ge(used[2], free)
                for c in (1, 0):
                    half(row, wd, c, slot(4 + c), ex_in[4 + c])
                if not downs_last:
                    for r, w in enumerate((wg, wu)):
                        next_half(r, w)

            with sp.Fori(0, NE // 2 - 2) as i:
                for j in range(2):
                    loads(sp.snap(2 * i + j), j)
            loads(NE - 4, 0)
            loads(NE - 3, 1, downs_last=False)
            for r, (i, w, c) in enumerate(REST):
                if r < 3:
                    sp.wait_ge(used[r], 2 * (NE - 1))
                half(D * (NE - 1), w, c, slot(i), ex_in[i])
            def piece(j, n, src):
                free = sp.snap(n + 1)
                sp.wait_ge(raw_free[j], free)
                to = by_rows(raw[j]) if src.shape[0] == FS else by_cols(raw[j])
                sp.dma_start(to, src.rearrange("(k p) n -> p k n", p=P)).then_inc(raw_in[j], 16)

            def ffn_loads(L, f, w_g, w_u, w_d):
                def gate_up(s, c):
                    piece(buf(f, GATE), nth(L, f, GATE, s), w_g[L, :, bass.ds(c, FS)])
                    piece(buf(f, UP), nth(L, f, UP, s), w_u[L, :, bass.ds(c, FS)])

                gate_up(0, 0)
                with sp.Fori(0, STEPS - 1) as i:
                    c, c_next = sp.snap(i * FS), sp.snap(i * FS + FS)
                    gate_up(i + 1, c_next)
                    piece(buf(f, DOWN), nth(L, f, DOWN, i), w_d[L, bass.ds(c, FS), :])
                piece(f, nth_last(L, f), w_d[L, bass.ds((STEPS - 1) * FS, FS), :])

            with sp.Fori(0, DEPTH2) as L:
                ffn_loads(L, 0, f1g, f1u, f1d)
                for m, c in enumerate(Z_COLS):
                    piece(buf_mix(m), nth_mix(L, m), w_in2[L, :, c:c + FS])
                for i, r in enumerate(O_ROWS):
                    m = len(Z_COLS) + i
                    row = sp.snap(D * L + r)
                    piece(buf_mix(m), nth_mix(L, m), w_out2.rearrange("l m d -> (l m) d")[bass.ds(row, FS), :])
                ffn_loads(L, 1, f2g, f2u, f2d)
            for t in range(TT):
                sp.wait_ge(sem["fin_put"], t + 1)
                sp.dma_start(out[t * P:t * P + P, :], xn[:, t, :]).then_inc(sem["fin_out"], 16)
            sp.wait_ge(sem["fin_out"], 16 * TT)

        @block.tensor
        def _(pe):
            def turn(b, src, ready):
                for k in range(KD):
                    for t in range(TT):
                        mm = pe.transpose(bank(b + k // 2)[:, (k % 2) * S + t * P:(k % 2) * S + t * P + P],
                                          src[:, t, k * P:k * P + P], ident)
                    if k % 2:
                        mm.then_inc(ready, 1)

            def turn_x(n, t, ks):
                for k in ks:
                    mm = pe.matmul(bank(4 + k // 2)[:, (k % 2) * S + t * P:(k % 2) * S + t * P + P],
                                   x[:, t, k * P:k * P + P], diag[:, t, :], start=True, stop=True)
                    if t == TT - 1 and k % 2:
                        mm.then_inc(sem["xnT_ps"], 1)

            def residual(to=0, tiles=range(TT)):
                for t in tiles:
                    for n in range(2):
                        pe.matmul(bank(to + 2 * t + n), ident, x[:, t, 512 * n:512 * n + 512], start=True, stop=False,
                                  skip_group_check=True)

            def turn_norm(n, summed=False, b=0):
                first = KD if b == 0 else KD // 2
                pe.wait_ge(sem["x_act"], 2 * n - 1)
                if summed:
                    residual(0, [0])
                pe.wait_ge(sem["diag_act"], n + 1)
                turn_x(n, 0, range(first))
                pe.wait_ge(sem["x_act"], 2 * n)
                pe.wait_ge(sem["x_dve"], n)
                turn_x(n, 0, range(first, KD))
                pe.wait_ge(sem["diag_dve"], n + 1)
                turn_x(n, 1, range(KD))
                if summed:
                    residual(0, [1])

            def features3(b, w, x_parts, fresh=None):
                (w_h, w_l), (x_h, x_l) = [by_cols(p) for p in w], x_parts
                for f in range(FS // P):
                    for k in range(KD):
                        if fresh is not None and f == 0 and k % 2 == 0:
                            pe.wait_ge(sem["xT_lo"], fresh + k // 2 + 1)
                        to, fs = bank(b)[:, f * S:f * S + S], slice(f * P, f * P + P)
                        pe.matmul(to, w_h[:, k, fs], x_h[:, k, :], start=k == 0, stop=False)
                        pe.matmul(to, w_h[:, k, fs], x_l[:, k, :], start=False, stop=False)
                        mm = pe.matmul(to, w_l[:, k, fs], x_h[:, k, :], start=False, stop=k == KD - 1)
                return mm

            def tokens3(b, c0, w, x_parts, fresh=None):
                (w_h, w_l), (x_h, x_l) = [by_cols(p) for p in w], x_parts
                for t in range(TT):
                    for k in range(KD):
                        if fresh is not None and t == 0 and k % 2 == 0:
                            pe.wait_ge(sem["xT_lo"], fresh + k // 2 + 1)
                        to, ts = bank(b + t)[:, c0:c0 + FS], slice(t * P, t * P + P)
                        pe.matmul(to, x_h[:, k, ts], w_h[:, k, :], start=k == 0, stop=False)
                        pe.matmul(to, x_h[:, k, ts], w_l[:, k, :], start=False, stop=False)
                        mm = pe.matmul(to, x_l[:, k, ts], w_h[:, k, :], start=False, stop=k == KD - 1)
                return mm

            def rows3(b, left, w, tiles, last):
                (w_h, w_l), (left_h, left_l) = [by_rows(p) for p in w], left
                for k in range(2):
                    for t in tiles:
                        for n in range(2):
                            to, ts, ns = bank(b + 2 * t + n), slice(t * P, t * P + P), slice(512 * n, 512 * n + 512)
                            pe.matmul(to, left_h[:, k, ts], w_h[:, k, ns], start=False, stop=False, skip_group_check=True)
                            pe.matmul(to, left_h[:, k, ts], w_l[:, k, ns], start=False, stop=False, skip_group_check=True)
                            mm = pe.matmul(to, left_l[:, k, ts], w_h[:, k, ns], start=False, stop=last and k == 1,
                                           skip_group_check=True)
                return mm

            def parts1(p):
                pe.wait_ge(sem["w1_lo"], p + 1)
                return w1h[p % 3], w1l[p % 3]

            def proj(p):
                o, i = p // 2, p % 2
                b, w, x_parts = Z_BANK[o], parts1(p), (x1h, x1l)
                if i == 0 and b in Z_BANK[:o]:
                    pe.wait_ge(Z_READ[max(j for j in range(o) if Z_BANK[j] == b)], 1)
                (features3(b + i, w, x_parts) if PROJ[o][2] else
                 tokens3(b, FS * i, w, x_parts, 0 if p == 0 else None)).then_inc(sem["z_ready"], 1)

            q_l, k_l = [[b[:, i * HH * S:(i + 1) * HH * S].rearrange("p (h s) -> p h s", h=HH) for b in lev_qk] for i in range(2)]

            def level(i):
                pe.wait_ge(sem["lev_k"], i + 1)
                if i < NLEV:
                    pe.wait_ge(sem["lev_q"], i + 1)
                if i == 0:
                    pe.wait_ge(sem["sc_nm"], NG)
                elif i == 1:
                    pe.wait_ge(sem["eT_dve"], NG // 2)
                    pe.wait_ge(sem["o_put"], TT)
                else:
                    pe.wait_ge(sem["lev_put"], i - 1)
                moving = q_l[i % 2] if i < NLEV else hq
                for h in range(HH):
                    for t in range(TT):
                        to = 1 - t if i == 0 else t
                        c = (h % 2) * S + t * P
                        mm = pe.matmul(bank(2 * (i % 2) + h // 2)[:, c:c + P], k_l[i % 2][:, h, t * P:t * P + P],
                                       moving[:, h, to * P:to * P + P], start=True, stop=True)
                mm.then_inc(sem["lev_ps"], 1)

            def recurrence():
                pe.wait_ge(sem["lev_put"], NLEV + 1)
                for t in range(TT):
                    for h in range(HH):
                        o_h = bank(t)[:, h * HD:h * HD + HD]
                        pe.matmul(o_h, at_diag[:, h, t, :], hi_tok[:, t, h * HD:h * HD + HD], start=True, stop=False)
                        mm = pe.matmul(o_h, at_off[:, h, 1 - t, :], hi_tok[:, 1 - t, h * HD:h * HD + HD],
                                       start=False, stop=True)
                    mm.then_inc(sem["ho_ps"], 1)

            def turn_qk():
                pe.wait_ge(sem["z_q"], 1)
                pe.wait_ge(sem["z_k"], 1)
                pe.wait_ge(sem["z_v"], 1)
                for b, src in ((0, aq_tok), (2, ak_tok)):
                    for c in range(4):
                        for t in range(TT):
                            mm = pe.transpose(bank(b + c // 2)[:, (c % 2) * S + t * P:(c % 2) * S + t * P + P],
                                              src[:, t, c * P:c * P + P], ident)
                    mm.then_inc(sem["qkT_ps"], 1)

            def scores(g):
                t = g // len(GROUPS)
                if g == 0:
                    pe.wait_ge(sem["qT_done"], 1)
                    pe.wait_ge(sem["kT_done"], 1)
                if g >= 2:
                    pe.wait_ge(sem["sc_nm"], g - 1)
                for i, h in enumerate(GROUPS[g % len(GROUPS)]):
                    r = AD * (h % 2)
                    mm = pe.matmul(bank(g % 2)[:, i * S:i * S + S], qT[r:r + AD, h // 2, t * P:t * P + P],
                                   kT[r:r + AD, h // 2, :], start=True, stop=True)
                mm.then_inc(sem["sc_ps"], 1)

            def turn_e(g):
                pe.wait_ge(sem["sc_cnt"], g + 1)
                if g >= 1:
                    pe.wait_ge(sem["eT_act"] if g % 2 else sem["eT_dve"], (g + 1) // 2)
                for i in range(2):
                    for j in range(TT):
                        mm = pe.transpose(bank(2)[:, (2 * i + j) * P:(2 * i + j) * P + P],
                                          a_s[g % 3][:, i, j * P:j * P + P], ident)
                mm.then_inc(sem["eT_ps"], 1)

            def values(g):
                t = g // len(GROUPS)
                pe.wait_ge(sem["eT_dve"] if g % 2 else sem["eT_act"], g // 2 + 1)
                if g == len(GROUPS):
                    pe.wait_ge(sem["o_put"], 1)
                for i, h in enumerate(GROUPS[g % len(GROUPS)]):
                    for j in range(TT):
                        mm = pe.matmul(bank(3)[:, h * AD:h * AD + AD], a_eT[g % 2][:, i, j, :],
                                       v_tok[:, j, h * AD:h * AD + AD], start=j == 0, stop=j == TT - 1)
                if g % len(GROUPS) == len(GROUPS) - 1:
                    mm.then_inc(sem["o_ps"], 1)

            def turn_mixed(b, k0):
                for k in range(4):
                    for t in range(TT):
                        mm = pe.transpose(bank(b + k // 2)[:, (k % 2) * S + t * P:(k % 2) * S + t * P + P],
                                          mixed[:, t, (k0 + k) * P:(k0 + k) * P + P], ident)
                    if k % 2:
                        mm.then_inc(sem["mxT_ps"], 1)

            def project1(i):
                k, last = O1_ROWS[i] // P, i == len(O1_ROWS) - 1
                pe.wait_ge(sem["xT_lo"], 5 + i)
                left, w = (x1h[:, k:k + 2, :], x1l[:, k:k + 2, :]), parts1(W1_IN + i)
                if last:
                    rows3(4, left, w, [0], last).then_inc(sem["half_done"], 1)
                    rows3(4, left, w, [1], last).then_inc(sem["acc_done"], 1)
                else:
                    rows3(4, left, w, range(TT), last).then_inc(sem["z_ready"], 1)

            pe.wait_ge(sem["const_in"], 16)
            for t in range(TT):
                pe.wait_ge(sem["diag_dve" if t else "diag_act"], 1)
                turn_x(0, t, range(KD))
            for p in range(6):
                proj(p)
            proj(6)
            turn_qk()
            proj(7)
            scores(0)
            scores(1)
            for n in range(1, NG // 2 + 1):
                proj(7 + n)
                if n >= 2:
                    values(2 * n - 4)
                    values(2 * n - 3)
                turn_e(2 * n - 2)
                if n < NG // 2:
                    scores(2 * n)
                turn_e(2 * n - 1)
                if n < NG // 2:
                    scores(2 * n + 1)
            proj(12)
            values(NG - 2)
            values(NG - 1)
            for i in range(3):
                proj(13 + i)
                level(i)
            pe.wait_ge(sem["z_hi"], 1)
            turn_mixed(4, 0)
            level(3)
            pe.wait_ge(sem["z_hg"], 1)
            pe.wait_ge(sem["xT_lo"], 6)
            residual(4)
            level(4)
            project1(0)
            level(5)
            for i in range(6, NLEV + 1):
                level(i)
            recurrence()
            project1(1)
            pe.wait_ge(sem["ho_put"], TT)
            turn_mixed(2, 4)
            project1(2)
            project1(3)

            turn_norm(1, True, 4)
            pe.wait_ge(sem["xT_act"], 1)
            pe.wait_ge(sem["xT_dve"], 1)
            router = one_f("router").rearrange("p (k e) -> p k e", k=KD)
            for t in range(TT):
                for k in range(KD):
                    mm = pe.matmul(bank(4)[:, t * NE:t * NE + NE], xT[:, k, t * P:t * P + P], router[:, k, :],
                                   start=k == 0, stop=k == KD - 1)
            mm.then_inc(sem["lg_ps"], 1)
            pe.wait_ge(sem["late_in"], 64)
            pe.matmul(bank(7)[0:2 * DH, 0:TBW + 1], tb_rel, tb_onehot, start=True, stop=True).then_inc(sem["tb_ps"], 1)
            pe.wait_ge(sem["aff_done"], 1)
            for t in range(TT):
                mm = pe.transpose(bank(5)[0:NE, t * P:t * P + P], aff[:, t, :], ident)
            mm.then_inc(sem["affT_ps"], 1)
            pe.wait_ge(sem["place_done"], 1)
            for t in range(TT):
                mm = pe.transpose(bank(6)[:, t * NE:t * NE + NE], place[:, t * P:t * P + P], ident[0:NE, 0:NE])
            mm.then_inc(sem["placeT_ps"], 1)

            def gather():
                for k in range(KD):
                    for t in range(TT):
                        mm = pe.matmul(bank(4)[:, k * CAP:k * CAP + CAP], xn[:, t, k * P:k * P + P], hot_next[:, t, :],
                                       start=t == 0, stop=t == TT - 1)
                mm.then_inc(sem["xin_ps"], 1)

            pe.wait_ge(sem["xn_act"], 1)
            pe.wait_ge(sem["xn_dve"], 1)

            def quarter(b, stationary, w):
                for r in range(KD // Q4):
                    for j in range(Q4):
                        mm = pe.matmul(bank(b)[j * CAP:j * CAP + CAP, :], stationary[:, Q4 * r + j, :],
                                       w[:, Q4 * r + j, :], start=r == 0, stop=r == KD // Q4 - 1,
                                       skip_group_check=True)
                return mm

            def expert(i, odd):
                e = pe.snap(2 * i + odd)
                landed, first = pe.snap(16 * e + 16), pe.snap(16 * i + 16)
                pe.wait_ge(sem["hot_done"], e + 1)
                gather()
                pe.wait_ge(sem["xe_ready"], e + 1)
                pe.wait_ge(sem["odd_in0"] if odd else ex_in[0], first)
                quarter(4, xin, odd_slot[0] if odd else slot(0)).then_inc(sem["used0"], 1)
                pe.wait_ge(sem["odd_in1"] if odd else ex_in[2], first)
                quarter(5, xin, odd_slot[1] if odd else slot(2)).then_inc(sem["used1"], 1)
                pe.wait_ge(sem["hote_done"], e + 1)
                for t in range(TT):
                    mm = pe.transpose(bank(7)[:, t * P:t * P + P], hot_e[:, t, :, :].rearrange("p j c -> p (j c)"), ident)
                mm.then_inc(sem["back_ps"], 1)
                pe.wait_ge(sem["g4_done"], 2 * e + 1)
                pe.wait_ge(ex_in[1], landed)
                quarter(4, xin, slot(1)).then_inc(sem["used0"], 1)
                pe.wait_ge(sem["u4_done"], 2 * e + 1)
                pe.wait_ge(ex_in[3], landed)
                quarter(5, xin, slot(3)).then_inc(sem["used1"], 1)
                pe.wait_ge(sem["back_done"], e + 1)
                for c in range(2):
                    pe.wait_ge(sem["g4_done"], 2 * e + c + 1)
                    pe.wait_ge(sem["u4_done"], 2 * e + c + 1)
                    for i, src in enumerate((g4[c], u4[c])):
                        for f in range(4):
                            a = (4 * i + f) * CAP
                            mm = pe.matmul(bank(6 + c)[:, a:a + CAP], src[:, f * P:f * P + P], fold, start=True, stop=True)
                    mm.then_inc(sem["sum_ps"], 1)
                pe.wait_ge(sem["ehid_done"], 2 * e + 2)
                for n in (1, 0):
                    pe.wait_ge(ex_in[4 + n], landed)
                    quarter(4 + n, hidT, slot(4 + n)).then_inc(sem["used2"], 1)
                for t in range(TT):
                    for n in (1, 0):
                        if t == 0:
                            pe.wait_ge(sem["y4_dve"] if n else sem["y4_act"], e + 1)
                        mm = pe.matmul(bank(2 * t + n), back[:, t * P:t * P + P], y4[n], start=False, stop=False,
                                       skip_group_check=True)
                    mm.then_inc(sem["stage_done" if t else "half_done"], 1)

            pe.wait_ge(sem["tb_rows_done"], 1)
            with pe.Fori(0, NE // 2) as i:
                expert(i, 0)
                expert(i, 1)

            def parts(j, n):
                pe.wait_ge(raw_free[j], n + 2)
                return wh[j], wl[j]

            xT_parts = (xTh, xTl)

            def ffn(L, f, fresh, done):
                def gate_up(c, s, fresh=None):
                    for r in (GATE, UP):
                        j = buf(f, r)
                        w = parts(j, nth(L, f, r, s))
                        features3(4 + 2 * r + c, w, xT_parts, fresh if r == GATE else None).then_inc(used[j], 1)

                def down(c, s, done=None):
                    j, n = (buf(f, DOWN), nth(L, f, DOWN, s)) if done is None else (f, nth_last(L, f))
                    w = parts(j, n)
                    pe.wait_ge(sem["hid_done"], STEPS * (2 * L + f) + s + 1)
                    if done is None:
                        rows3(0, (hidh[c], hidl[c]), w, range(TT), False).then_inc(used[j], 1)
                    else:
                        rows3(0, (hidh[c], hidl[c]), w, [0], True).then_inc(sem["half_done"], 1)
                        rows3(0, (hidh[c], hidl[c]), w, [1], True).then_inc(done, 1)

                gate_up(0, 0, fresh)
                with pe.Fori(0, STEPS // 2) as i:
                    gate_up(1, 2 * i + 1)
                    down(0, 2 * i)
                    gate_up(0, 2 * i + 2)
                    down(1, 2 * i + 1)
                down(0, STEPS - 1, done)

            with pe.Fori(0, DEPTH2) as L:
                turn_norm(3 * L + 2, True)
                ffn(L, 0, XT1 + 14 * L, sem["acc_done"])
                turn_norm(3 * L + 3)

                def piece(m):
                    return parts(buf_mix(m), nth_mix(L, m))

                def feats(m, b, fresh=None):
                    features3(b, piece(m), xT_parts, fresh).then_inc(used[buf_mix(m)], 1)

                feats(0, 0, XT1 + 14 * L + 4)
                feats(1, 1)
                feats(2, 2)
                feats(3, 3)
                feats(4, 4)
                feats(5, 6)
                feats(6, 7)
                pe.wait_ge(sem["lru_xr"], L + 1)
                pe.wait_ge(sem["z2_2"], L + 1)
                for b, name in ((5, "wa"), (4, "wx")):
                    for c in range(2):
                        a = PRM[name][0] + c * P
                        mm = pe.matmul(bank(b)[:, c * S:c * S + S], prm[:, a:a + P], xr[:, c, :], start=True, stop=True)
                mm.then_inc(sem["lru_ps"], 1)
                pe.wait_ge(sem["z2_1"], L + 1)
                feats(7, 2)
                feats(8, 3)
                pe.wait_ge(sem["z2_0"], L + 1)
                tokens3(0, 0, piece(9), xT_parts).then_inc(used[buf_mix(9)], 1)

                def scores2(g):
                    t, n = g // 2, P * (g // 2 + 1)
                    if g == 0:
                        pe.wait_ge(sem["z2_q"], L + 1)
                        pe.wait_ge(sem["z2_k"], L + 1)
                    if g >= 2:
                        pe.wait_ge(sem["d_nmx"], 4 * L + g)
                    for m in range(2):
                        for i in range(2):
                            h = 2 * (g % 2) + i
                            mm = pe.matmul(d_scores(g, m, i),
                                           qT2[m * DM:m * DM + DM, h, t * P:t * P + P],
                                           kT2[m * DM:m * DM + DM, h, 0:n], start=True, stop=True)
                    mm.then_inc(sem["d_ps"], 1)

                def turn_d(g):
                    pe.wait_ge(sem["d_comb"], 4 * L + g + 1)
                    if g >= 2:
                        pe.wait_ge(sem["dT_done"], 4 * L + g - 1)
                    for i in range(2):
                        for j in range(g // 2 + 1):
                            mm = pe.transpose(bank(2 + g % 2)[:, (2 * i + j) * P:(2 * i + j) * P + P],
                                              d_attn[g % 2][:, i, j * P:j * P + P], ident)
                    mm.then_inc(sem["dT_ps"], 1)

                def values2(g):
                    pe.wait_ge(sem["dT_done"], 4 * L + g + 1)
                    if g == 0:
                        pe.wait_ge(sem["z2_v"], L + 1)
                    for i in range(2):
                        h = 2 * (g % 2) + i
                        for j in range(g // 2 + 1):
                            mm = pe.matmul(bank(g // 2)[:, h * P:h * P + P], d_aT[:, i, g if g < 2 else j, :], v2[:, j, h * P:h * P + P],
                                           start=j == 0, stop=j == g // 2)
                    mm.then_inc(sem["do_ps"], 1)

                def project3(m, tiles):
                    return rows3(4, O_LEFT[m - len(Z_COLS)], piece(m), tiles, m == MIX - 1)

                scores2(0)
                scores2(1)
                tokens3(0, FS, piece(10), xT_parts).then_inc(used[buf_mix(10)], 1)
                scores2(2)
                pe.wait_ge(sem["lru_gates"], L + 1)
                residual(4, [0])
                pe.wait_ge(sem["y_done"], L + 1)
                project3(11, [0])
                turn_d(0)
                turn_d(1)
                scores2(3)
                project3(12, [0])
                values2(0)
                values2(1)
                pe.wait_ge(sem["d_nmx"], 4 * L + 4)
                residual(4, [1])
                turn_d(2)
                project3(11, [1]).then_inc(used[buf_mix(11)], 1)
                values2(2)
                turn_d(3)

                def turn_heads(t):
                    pe.wait_ge(sem["do_nrm"], 2 * L + t + 1)
                    for h in range(DH):
                        mm = pe.transpose(bank(t)[:, h * P:h * P + P], xn[:, t, h * P:h * P + P], ident)
                    mm.then_inc(sem["yT_ps"], 1)

                turn_heads(0)
                values2(3)
                pe.wait_ge(sem["xT_lo"], XT1 + 14 * L + 9)
                project3(13, [0])
                project3(12, [1]).then_inc(used[buf_mix(12)], 1)
                turn_heads(1)
                project3(14, [0]).then_inc(sem["half_done"], 1)
                pe.wait_ge(sem["xT_lo"], XT1 + 14 * L + 10)
                project3(13, [1]).then_inc(used[buf_mix(13)], 1)
                project3(14, [1]).then_inc(sem["acc_done"], 1)
                turn_norm(3 * L + 4, True, 4)
                ffn(L, 1, XT1 + 14 * L + 10, sem["stage_done"])

        @block.scalar
        def _(act):
            def norm(n, weight, part=None, xT_hi=xTh, between=lambda: None):
                between()
                to = xT if part is None else xT_hi
                for k in range(4 if part is None else KD):
                    if k % 2 == 0:
                        act.wait_ge(sem["xnT_ps"], 4 * n + k // 2 + 1)
                    a = nc.scalar.activation(to[:, k, :], bank(4 + k // 2)[:, (k % 2) * S:(k % 2) * S + S], ACT.Copy,
                                             scale=weight[:, k:k + 1])
                    if part is not None and k % 2:
                        a.then_inc(sem["xT_hi"], 1)
                if part is None:
                    a.then_inc(sem["xT_act"], 1)

            def squares(t, ns, of):
                nc.scalar.activation(xn[:, t, ns], of, ACT.Square, accum_out=n_ss[:, t:t + 1]).then_inc(sem["sq_done"], 1)

            def root(t):
                nc.scalar.activation(n_std[:, t:t + 1], n_ss[:, t:t + 1], ACT.Sqrt, scale=1.0 / D, bias=n_eps)\
                    .then_inc(sem["std_ready"], 1)

            def scale_first(n, meanwhile=lambda: None):
                act.wait_ge(sem["sq_done"], 2 * n + 1)
                root(0)
                meanwhile()
                act.wait_ge(sem["rstd_ready"], 2 * n + 1)
                nc.scalar.activation(diag[:, 0, :], ident, ACT.Copy, scale=n_rstd[:, 0:1]).then_inc(sem["diag_act"], 1)

            def scale_second(n):
                act.wait_ge(sem["ss_ready"], n + 2)
                root(1)

            def update(n, half, done, b=0):
                act.wait_ge(sem["half_done"], half)
                squares(0, ALL, bank(b, 2))
                scale_first(n, lambda: nc.scalar.activation(x[:, 0, :], bank(b, 2), ACT.Copy).then_inc(sem["x_act"], 1))
                act.wait_ge(done[0], done[1])
                squares(1, LEFT, bank(b + 2))
                nc.scalar.activation(x[:, 1, LEFT], bank(b + 2), ACT.Copy).then_inc(sem["x_act"], 1)
                scale_second(n)

            def sqrt_table():
                nc.scalar.activation(hold[:, 4:5], ident[:, 0:1], ACT.Sqrt)

            act.wait_ge(sem["const_in"], 16)
            act.wait_ge(sem["ss_ready"], 1)
            sqrt_table()
            act.wait_ge(sem["x_in0"], 16)
            squares(0, ALL, x[:, 0, :])
            scale_first(0)
            act.wait_ge(sem["x_in1"], 16)
            squares(1, LEFT, x[:, 1, LEFT])
            scale_second(0)
            act.wait_ge(sem["one_in"], 16)

            def hi1(p):
                act.wait_ge(w1_in[p % 2], 16 * (p // 2 + 1))
                if p >= 3:
                    act.wait_ge(sem["z_ready"], p - 2)
                nc.scalar.activation(w1h[p % 3], raw1[p % 2], ACT.Copy).then_inc(sem["w1_hi"], 1)

            def squares_qk(c):
                act.wait_ge(sem["z_ready"], 2 + 2 * c)
                nc.scalar.activation(sqj[:, c, :, :].rearrange("p t n -> p (t n)"), bank(Z_BANK[c], 2), ACT.Square)\
                    .then_inc(sem["qk_sq"], 1)

            sg = lev_e[1].rearrange("p (d n) -> p d n", d=2)
            lf = lev_e[0].rearrange("p (d n) -> p d n", d=2)

            def gates(d):
                act.wait_ge(sem["z_ready"], 8 + 2 * d)
                b, k_raw, free = ((Z_BANK[3], kf, sem["z_hf"]), (Z_BANK[4], kb, sem["z_hb"]))[d]
                nc.scalar.activation(sg[:, d, :], bank(b, 2), ACT.Sigmoid).then_inc(sem["gate_sg"], 1)
                nc.scalar.activation(k_raw.rearrange("p h s -> p (h s)"), bank(b, 2), ACT.Sigmoid, scale=-1.0).then_inc(free, 1)

            def logs():
                act.wait_ge(sem["lb_done"], 1)
                act.wait_ge(sem["gate_sg"], 2)
                for d in range(2):
                    for h in range(HH):
                        i = d * HH + h
                        a = nc.scalar.activation(lf[:, d, h * S:h * S + S], sg[:, d, h * S:h * S + S], ACT.Ln,
                                                 scale=oml[:, i:i + 1], bias=lb[:, i:i + 1])
                    a.then_inc(sem["gate_lf"], 1)

            def decay(i):
                act.wait_ge(sem["lev_sub"], i + 1)
                nc.scalar.activation(lev_e[i % 2], lev_e[i % 2], ACT.Exp).then_inc(sem["lev_exp"], 1)

            def exps(g):
                act.wait_ge(sem["sc_nm"], g + 1)
                for i, h in enumerate(GROUPS[g % len(GROUPS)]):
                    c = g // len(GROUPS) * AH + h
                    a = nc.scalar.activation(a_s[g % 3][:, i, :], a_s[g % 3][:, i, :], ACT.Exp, bias=a_nm[:, c:c + 1])
                a.then_inc(sem["sc_exp"], 1)

            def copy_eT(g):
                act.wait_ge(sem["eT_ps"], g + 1)
                nc.scalar.activation(a_eT[0].rearrange("p h j s -> p (h j s)"), bank(2), ACT.Copy).then_inc(sem["eT_act"], 1)

            def hi_mixed(b, k0):
                for c in range(2):
                    k = k0 + 2 * c
                    act.wait_ge(sem["mxT_ps"], k // 2 + 1)
                    nc.scalar.activation(x1h[:, k:k + 2, :].rearrange("p k s -> p (k s)"), bank(b + c), ACT.Copy)\
                        .then_inc(sem["xT_hi"], 1)

            norm(0, one_f("norm1"), 0, x1h, lambda: hi1(0))
            hi1(1)
            hi1(2)
            act.wait_ge(sem["lb_max"], 1)
            nc.scalar.activation(lbe, lbe, ACT.Exp).then_inc(sem["lb_exp"], 1)
            hi1(3)
            squares_qk(0)
            hi1(4)
            hi1(5)
            squares_qk(1)
            hi1(6)
            sqrt_table()
            act.wait_ge(sem["qk_ms"], 1)
            nc.scalar.activation(qk_std, qk_ms, ACT.Sqrt).then_inc(sem["qk_std"], 1)
            hi1(7)
            act.wait_ge(sem["z_ready"], 6)
            nc.scalar.activation(v_tok.rearrange("p t n -> p (t n)"), bank(Z_BANK[2], 2), ACT.Copy).then_inc(sem["z_v"], 1)
            hi1(8)
            act.wait_ge(sem["qkT_ps"], 2)
            nc.scalar.activation(kT.rearrange("p c s -> p (c s)"), bank(2, 2), ACT.Copy, scale=one_f("k"))\
                .then_inc(sem["kT_done"], 1)
            hi1(9)
            hi1(10)
            gates(0)
            exps(0)
            exps(1)
            for n in range(1, NG // 2):
                hi1(10 + n)
                copy_eT(2 * n - 2)
                exps(2 * n)
                exps(2 * n + 1)
                if n == 2:
                    gates(1)
            logs()
            hi1(14)
            copy_eT(NG - 2)
            act.wait_ge(sem["z_ready"], 12)
            nc.scalar.activation(hq.rearrange("p h s -> p (h s)"), bank(Z_BANK[5], 2), ACT.Silu).then_inc(sem["z_hq"], 1)
            decay(0)
            hi1(15)
            decay(1)
            decay(2)
            hi1(16)
            decay(3)
            hi1(17)
            decay(4)
            act.wait_ge(sem["z_ready"], 16)
            nc.scalar.activation(gs_tok.rearrange("p t n -> p (t n)"), bank(Z_BANK[7], 2), ACT.Silu).then_inc(sem["z_hg"], 1)
            hi_mixed(4, 0)
            for i in range(5, NLEV):
                decay(i)
            hi1(18)
            sqrt_table()
            act.wait_ge(sem["ho_ps"], 2)
            nc.scalar.activation(ho_sqj, bank(0, 2), ACT.Square).then_inc(sem["ho_sq"], 1)
            act.wait_ge(sem["ho_ms"], 1)
            nc.scalar.activation(o_std, o_ms, ACT.Sqrt).then_inc(sem["ho_std"], 1)
            hi1(19)
            hi_mixed(2, 4)
            sqrt_table()
            update(1, 1, (sem["acc_done"], 1), 4)

            norm(1, one_f("norm2"))
            nc.scalar.activation(xn[:, 0, :], x[:, 0, :], ACT.Copy, scale=n_rstd[:, 0:1]).then_inc(sem["xn_act"], 1)
            act.wait_ge(sem["lg_nm"], 1)
            for t in range(TT):
                a = nc.scalar.activation(aff_e[:, t, :], bank(4)[:, t * NE:t * NE + NE], ACT.Exp, bias=r_nm[:, t:t + 1],
                                         accum_out=r_sum[:, t:t + 1])
            a.then_inc(sem["lg_exp"], 1)
            with act.Fori(0, NE) as e:
                act.wait_ge(sem["used0"], 2 * e + 1)
                nc.scalar.activation(g4[0], bank(4), ACT.Copy).then_inc(sem["g4_done"], 1)
                act.wait_ge(sem["back_ps"], e + 1)
                nc.scalar.activation(back, bank(7)[:, 0:S], ACT.Copy).then_inc(sem["back_done"], 1)
                act.wait_ge(sem["used0"], 2 * e + 2)
                nc.scalar.activation(g4[1], bank(4), ACT.Copy).then_inc(sem["g4_done"], 1)
                for c in range(2):
                    act.wait_ge(sem["sum_ps"], 2 * e + c + 1)
                    nc.scalar.activation(e_sil[c], bank(6 + c)[:, 0:4 * CAP], ACT.Silu).then_inc(sem["esil_done"], 1)
                act.wait_ge(sem["used2"], 2 * e + 2)
                nc.scalar.activation(y4[0], bank(4), ACT.Copy).then_inc(sem["y4_act"], 1)

            def hi(j, n, free=None):
                act.wait_ge(raw_in[j], 16 * n + 16)
                if free is not None:
                    act.wait_ge(free[0], free[1])
                nc.scalar.activation(wh[j], raw[j], ACT.Copy).then_inc(sem["w_hi"], 1)

            def ffn(L, f, free):
                def step(c, s, first=False, last=False):
                    q = STEPS * (2 * L + f)
                    if last:
                        hi(f, nth_last(L, f), used_ffn(L, f, GATE, s))
                    else:
                        hi(buf(f, GATE), nth(L, f, GATE, s + 1), used_ffn(L, f, GATE, s))
                    act.wait_ge(*used_ffn(L, f, UP, s))
                    nc.scalar.activation(f_sil[c], bank(4 + c), ACT.Silu).then_inc(sem["sil_done"], 1)
                    if not last:
                        hi(buf(f, UP), nth(L, f, UP, s + 1))
                        hi(buf(f, DOWN), nth(L, f, DOWN, s), free if first else used_ffn(L, f, DOWN, s - 1))
                    act.wait_ge(sem["hid_t"], q + s + 1)
                    nc.scalar.activation(hidh[c].rearrange("p f s -> p (f s)"), f_hid[c].rearrange("p f s -> p (f s)"), ACT.Copy)\
                        .then_inc(sem["hid_h"], 1)

                step(0, 0, first=True)
                step(1, 1)
                with act.Fori(1, STEPS // 2) as i:
                    step(0, 2 * i)
                    step(1, 2 * i + 1)
                step(0, STEPS - 1, last=True)

            act.wait_ge(sem["late_in"], 64)
            act.wait_ge(sem["tb_out"], 16)
            nc.scalar.dma_start(tb_raw, bass.AP(tb_dram, 0, [[1, P], [TBW + 1, 2 * DH], [1, S]])).then_inc(sem["tb_in"], 16)
            act.wait_ge(used[1], 2 * NE)
            nc.scalar.dma_start(fin_row, fin_w).then_inc(sem["late_in"], 16)
            with act.Fori(0, DEPTH2) as L:
                sqrt_table()
                update(3 * L + 2, NE + 3 * L + 1, (sem["stage_done"], NE + L))
                act.wait_ge(sem["prm_ready"], L + 1)
                norm(3 * L + 2, pf("norm0"), XT1 + 14 * L,
                     between=lambda: hi(buf(0, GATE), nth(L, 0, GATE, 0), (used[0], 2 * NE + PRODUCTS[0] * L)))
                hi(buf(0, UP), nth(L, 0, UP, 0))
                act.wait_ge(sem["lru_u"], L + 1)
                nc.scalar.activation(lc_u, lc_ab, ACT.Exp, scale=-1.0).then_inc(sem["lru_c"], 1)
                act.wait_ge(sem["d_lamx"], L + 1)
                nc.scalar.activation(lamv[:, 2:4], lamv[:, 0:2], ACT.Exp).then_inc(sem["d_lame"], 1)
                ffn(L, 0, (sem["stage_done"], NE + L))

                def hi_mix(m):
                    free = (used_ffn(L, 0, UP, STEPS - 1) if m == 0 else used_ffn(L, 0, DOWN, STEPS - 2) if m == 1
                            else (sem["acc_done"], 2 * L + 2) if m == 2 else used_mix(L, m - 3))
                    hi(buf_mix(m), nth_mix(L, m), free)

                hi_mix(0)
                hi_mix(1)
                sqrt_table()
                update(3 * L + 3, NE + 3 * L + 2, (sem["acc_done"], 2 * L + 2))
                norm(3 * L + 3, pf("norm1"), XT1 + 14 * L + 4)
                hi_mix(2)
                hi_mix(3)
                hi_mix(4)
                act.wait_ge(sem["tb_done"], 1)
                nc.scalar.activation(scbc.rearrange("p c s -> p (c s)"), bank(0, 2), ACT.Copy).then_inc(sem["z2_0"], 1)
                hi_mix(5)
                hi_mix(6)
                hi_mix(7)
                nc.scalar.activation(lgate.rearrange("p c s -> p (c s)"), bank(4), ACT.Copy).then_inc(sem["z2_2"], 1)
                hi_mix(8)
                hi_mix(9)
                nc.scalar.activation(qT2.rearrange("p c s -> p (c s)"), bank(6, 2), ACT.Copy, scale=DM ** -0.5)\
                    .then_inc(sem["z2_q"], 1)
                act.wait_ge(sem["lru_ps"], L + 1)
                for b, g, name in ((5, rg, "ba"), (4, ig, "bx")):
                    for c in range(2):
                        a = nc.scalar.activation(g[:, c, :], bank(b)[:, c * S:c * S + S], ACT.Sigmoid, bias=pf(name, c))
                a.then_inc(sem["lru_gates"], 1)
                hi_mix(10)
                act.wait_ge(sem["gelu_in"], L + 1)
                nc.scalar.activation(lg, lg, ACT.Tanh, scale=GELU_C).then_inc(sem["gelu_t"], 1)
                act.wait_ge(sem["lru_gates"], L + 1)
                act.wait_ge(sem["lru_b"], L + 1)
                for c in range(2):
                    nc.scalar.activation(lm[:, c, :], rg[:, c, :], ACT.Tanh, scale=lc_n[:, c:c + 1])
                for c in range(2):
                    a = nc.scalar.activation(la[:, c, :], rg[:, c, :], ACT.Exp, scale=lc_c[:, c:c + 1])
                a.then_inc(sem["lru_a"], 1)
                act.wait_ge(*used_mix(L, 8))
                nc.scalar.activation(kT2.rearrange("p c s -> p (c s)"), bank(2, 2), ACT.Copy).then_inc(sem["z2_k"], 1)
                act.wait_ge(sem["lru_m"], L + 1)
                nc.scalar.activation(lm, lm, ACT.Sqrt).then_inc(sem["lru_sq"], 1)
                hi_mix(11)

                def exps2(g):
                    act.wait_ge(sem["d_nmx"], 4 * L + g + 1)
                    for m in range(2):
                        for i in range(2):
                            c = 4 * g + 2 * m + i
                            a = nc.scalar.activation(d_e[g][:, m, i, :], d_e[g][:, m, i, :], ACT.Exp, bias=d_nm[:, c:c + 1],
                                                     accum_out=d_den[:, c:c + 1])
                    a.then_inc(sem["d_exp"], 1)

                def copy_dT(g):
                    act.wait_ge(sem["dT_ps"], 4 * L + g + 1)
                    if g >= 2:
                        act.wait_ge(sem["do_ps"], 4 * L + g)
                    j0, n = (g, 1) if g < 2 else (0, 2)
                    nc.scalar.activation(d_aT[:, :, j0:j0 + n, :], bank(2 + g % 2).rearrange("p (h j s) -> p h j s", h=2, j=2)
                                         [:, :, 0:n, :], ACT.Copy).then_inc(sem["dT_done"], 1)

                def head_squares(t):
                    act.wait_ge(sem["do_ps"], 4 * L + 2 * t + 2)
                    nc.scalar.activation(d_sq[t], bank(t), ACT.Square).then_inc(sem["do_sq"], 1)

                def head_roots(t):
                    act.wait_ge(sem["do_ms"], 2 * L + t + 1)
                    nc.scalar.activation(d_std[:, 4 * t:4 * t + 4], d_ms[:, 4 * t:4 * t + 4], ACT.Sqrt).then_inc(sem["do_std"], 1)

                def heads_hi(t):
                    act.wait_ge(sem["yT_ps"], 2 * L + t + 1)
                    nc.scalar.activation(xTh[:, 0:DH, t * P:t * P + P], bank(t).rearrange("p (h s) -> p h s", h=DH), ACT.Copy,
                                         scale=lamv[:, 6:7]).then_inc(sem["xT_hi"], 1)

                exps2(0)
                exps2(1)
                hi_mix(12)
                act.wait_ge(*used_mix(L, 10))
                nc.scalar.activation(v2.rearrange("p t c -> p (t c)"), bank(0, 2), ACT.Copy).then_inc(sem["z2_v"], 1)
                exps2(2)
                copy_dT(0)
                copy_dT(1)
                hi_mix(13)
                exps2(3)
                head_squares(0)
                copy_dT(2)
                head_roots(0)
                copy_dT(3)
                heads_hi(0)
                head_squares(1)
                hi_mix(14)
                head_roots(1)
                heads_hi(1)
                hi(buf(1, GATE), nth(L, 1, GATE, 0), used_mix(L, 12))
                sqrt_table()
                update(3 * L + 4, NE + 3 * L + 3, (sem["acc_done"], 2 * L + 3), 4)
                norm(3 * L + 4, pf("norm2"), XT1 + 14 * L + 10)
                hi(buf(1, UP), nth(L, 1, UP, 0), used_mix(L, 13))
                ffn(L, 1, (sem["acc_done"], 2 * L + 3))

            sqrt_table()
            for t in range(TT):
                act.wait_ge(*((sem["stage_done"], NE + DEPTH2) if t else (sem["half_done"], NE + 3 * DEPTH2 + 1)))
                squares(t, ALL, bank(2 * t, 2))
                act.wait_ge(sem["sq_done"], 2 * LAST + t + 1)
                root(t)

        @block.vector
        def _(dve):
            ch = Chain(dve, sem["dve_chain"])

            def mean_eps(out, ss, width, eps):
                return dve.tensor_scalar(out, ss, 1.0 / width, eps, ALU.mult, ALU.add)

            def squares():
                dve.memset(hold[:, 0:1], 0.0)
                ch.step(dve.tensor_tensor_reduce(xn[:, 1, RIGHT], x[:, 1, RIGHT], x[:, 1, RIGHT], 1.0, 0.0, ALU.mult, ALU.add,
                                                 n_ss[:, 2:3]))

            def sums_of_squares(n):
                dve.wait_ge(sem["sq_done"], 2 * n + 2)
                ch.settle()
                dve.tensor_tensor(n_ss[:, 1:2], n_ss[:, 1:2], n_ss[:, 2:3], ALU.add).then_inc(sem["ss_ready"], 1)

            def norm(n, weight, part=None, parts=(xTh, xTl), between=lambda: None):
                inverse(n, 1)
                dve.wait_ge(sem["rstd_ready"], 2 * n + 2)
                dve.tensor_scalar(diag[:, 1, :], ident, n_rstd[:, 1:2], None, ALU.mult).then_inc(sem["diag_dve"], 1)
                between()
                for k in range(4 if part is None else 0, KD):
                    if k % 2 == 0:
                        if part is None:
                            dve.wait_ge(sem["xnT_ps"], 4 * n + k // 2 + 1)
                        else:
                            dve.wait_ge(sem["xT_hi"], part + k // 2 + 1)
                    turned = bank(4 + k // 2)[:, (k % 2) * S:(k % 2) * S + S]
                    if part is None:
                        v = dve.tensor_scalar(xT[:, k, :], turned, weight[:, k:k + 1], None, ALU.mult)
                    else:
                        v = dve.scalar_tensor_tensor(parts[1][:, k, :], turned, weight[:, k:k + 1], parts[0][:, k, :].bitcast(F32),
                                                     ALU.mult, ALU.subtract)
                        if k % 2:
                            v.then_inc(sem["xT_lo"], 1)
                if part is None:
                    v.then_inc(sem["xT_dve"], 1)

            def inverse(n, t):
                dve.wait_ge(sem["std_ready"], 2 * n + t + 1)
                dve.reciprocal(n_rstd[:, t:t + 1], n_std[:, t:t + 1]).then_inc(sem["rstd_ready"], 1)

            dve.memset(n_eps, EPS).then_inc(sem["ss_ready"], 1)

            def update(n, done, b=0):
                inverse(n, 0)
                dve.wait_ge(done[0], done[1])
                dve.tensor_copy(x[:, 1, RIGHT], bank(b + 3)).then_inc(sem["x_dve"], 1)
                dve.wait_ge(sem["x_dve"], n)
                squares()
                sums_of_squares(n)

            inverse(0, 0)
            dve.wait_ge(sem["x_in1"], 16)
            squares()
            sums_of_squares(0)

            def lo1(p):
                dve.wait_ge(sem["w1_hi"], p + 1)
                dve.tensor_tensor(w1l[p % 3], raw1[p % 2], w1h[p % 3].bitcast(F32), ALU.subtract).then_inc(sem["w1_lo"], 1)

            dve.wait_ge(sem["one_in"], 16)
            norm(0, one_f("norm1"), 0, (x1h, x1l), lambda: lo1(0))
            lbp = one_f("lb")
            ch.link(dve.tensor_tensor(lbm, lbp[:, 0:8], lbp[:, 8:16], ALU.max))
            dve.tensor_tensor(lbe[:, 0:8], lbp[:, 0:8], lbm, ALU.subtract)
            dve.tensor_tensor(lbe[:, 8:16], lbp[:, 8:16], lbm, ALU.subtract).then_inc(sem["lb_max"], 1)
            lo1(1)
            lo1(2)
            dve.wait_ge(sem["lb_exp"], 1)
            ch.link(dve.tensor_tensor(lbr, lbe[:, 0:8], lbe[:, 8:16], ALU.add))
            ch.link(dve.reciprocal(lbr, lbr))
            ch.link(dve.tensor_tensor(lb, lbe[:, 0:8], lbr, ALU.mult))
            ch.link(dve.tensor_scalar(oml, lb, -1.0, 1.0, ALU.mult, ALU.add))
            dve.tensor_scalar(lb, lb, LN_LEAST, None, ALU.max).then_inc(sem["lb_done"], 1)

            def scale_keys(d):
                k_raw, free = ((kf, sem["z_hf"]), (kb, sem["z_hb"]))[d]
                dve.wait_ge(free, 1)
                for h in range(HH):
                    v = dve.tensor_scalar(k_raw[:, h, :], k_raw[:, h, :], oml[:, d * HH + h:d * HH + h + 1], None, ALU.mult)
                v.then_inc(sem["k_scaled"], 1)

            def sums(d):
                lf = lev_e[0].rearrange("p (d h n) -> p d h n", d=2, h=HH)
                dve.wait_ge(sem["gate_lf"], d + 1)
                for h in range(HH):
                    to, steps = (bc[:, h, :], lf[:, 0, h, :]) if d == 0 else (rc[:, h, ::-1], lf[:, 1, h, ::-1])
                    ch.step(dve.tensor_tensor_scan(to, ones_s, steps, 0.0, ALU.mult, ALU.add))

            def exponents(i):
                w = LEVELS[i]
                n = HH * S // (2 * w)
                if i >= 2:
                    dve.wait_ge(sem["lev_k"], i - 1)
                    dve.wait_ge(sem["lev_q"], i - 1)
                eq = lev_e[i % 2][:, 0:HH * S].rearrange("p (n f w) -> p n f w", n=n, f=2)
                ek = lev_e[i % 2][:, HH * S:2 * HH * S].rearrange("p (n f w) -> p n f w", n=n, f=2)
                b = bc.rearrange("p h s -> p (h s)").rearrange("p (n f w) -> p n f w", n=n, f=2)
                r = rc.rearrange("p h s -> p (h s)").rearrange("p (n f w) -> p n f w", n=n, f=2)
                b_end = b[:, :, 0, w - 1:w].to_broadcast([P, n, w])
                r_end = r[:, :, 1, 0:1].to_broadcast([P, n, w])
                dve.tensor_tensor(eq[:, :, 1, :], b[:, :, 1, :], b_end, ALU.subtract)
                dve.tensor_tensor(ek[:, :, 0, :], b_end, b[:, :, 0, :], ALU.subtract)
                dve.tensor_tensor(eq[:, :, 0, :], r[:, :, 0, :], r_end, ALU.subtract)
                dve.tensor_tensor(ek[:, :, 1, :], r_end, r[:, :, 1, :], ALU.subtract).then_inc(sem["lev_sub"], 1)

            def decayed_q(i):
                dve.wait_ge(sem["lev_exp"], i + 1)
                if i == 1:
                    dve.wait_ge(sem["o_ps"], TT)
                if i >= 2:
                    dve.wait_ge(sem["lev_ps"], i - 1)
                dve.tensor_tensor(lev_qk[i % 2][:, 0:HH * S], hq.rearrange("p h s -> p (h s)"), lev_e[i % 2][:, 0:HH * S],
                                  ALU.mult).then_inc(sem["lev_q"], 1)

            def put(i):
                dve.wait_ge(sem["lev_ps"], i + 1)
                if i == 0:
                    dve.tensor_copy(at_off.rearrange("p h t c -> p (h t c)"), bank(0, 2)).then_inc(sem["lev_put"], 1)
                else:
                    dve.wait_ge(sem["lev_put"], i)
                    dve.wait_ge(sem["mask_in"], 16)
                    mask = masks[:, i - 1, :].bitcast(U32).unsqueeze(1).to_broadcast([P, HH * TT, P])
                    dve.copy_predicated(at_diag.rearrange("p h t c -> p (h t) c"), mask,
                                        bank(2 * (i % 2), 2).rearrange("p (n c) -> p n c", c=P)).then_inc(sem["lev_put"], 1)

            def maxima(g):
                t = g // len(GROUPS)
                dve.wait_ge(sem["sc_ps"], g + 1)
                if g >= 3:
                    dve.wait_ge(sem["eT_ps"], g - 2)
                for i, h in enumerate(GROUPS[g % len(GROUPS)]):
                    c = t * AH + h
                    ch.step(dve.tensor_tensor_reduce(a_s[g % 3][:, i, :], bank(g % 2)[:, i * S:i * S + S],
                                                     abias[:, h, P * (1 - t):P * (1 - t) + S], 1.0, -3e38, ALU.add, ALU.max,
                                                     a_mx[:, c:c + 1]))
                c = t * AH + GROUPS[g % len(GROUPS)][0]
                ch.settle()
                dve.tensor_scalar(a_nm[:, c:c + 3:2], a_mx[:, c:c + 3:2], -1.0, None, ALU.mult).then_inc(sem["sc_nm"], 1)

            def weigh(g):
                t = g // len(GROUPS)
                dve.wait_ge(sem["sc_exp"], g + 1)
                for i, h in enumerate(GROUPS[g % len(GROUPS)]):
                    c = t * AH + h
                    v = dve.tensor_tensor_reduce(a_s[g % 3][:, i, :], a_s[g % 3][:, i, :], count[:, P * (1 - t):P * (1 - t) + S],
                                                 1.0, 0.0, ALU.mult, ALU.add, a_den[:, c:c + 1])
                v.then_inc(sem["sc_cnt"], 1)

            def outputs(t):
                dve.wait_ge(sem["sc_cnt"], (t + 1) * len(GROUPS))
                ch.link(dve.reciprocal(a_rden[:, t * AH:t * AH + AH], a_den[:, t * AH:t * AH + AH]))
                dve.wait_ge(sem["o_ps"], t + 1)
                dve.wait_ge(sem["qkT_ps"], 2)
                rden = a_rden[:, t * AH:t * AH + AH].unsqueeze(2).to_broadcast([P, AH, AD])
                dve.tensor_tensor(mixed[:, t, 0:512].rearrange("p (h d) -> p h d", d=AD),
                                  bank(3).rearrange("p (h d) -> p h d", d=AD), rden, ALU.mult).then_inc(sem["o_put"], 1)

            def copy_eT(g):
                dve.wait_ge(sem["eT_ps"], g + 1)
                dve.tensor_copy(a_eT[1].rearrange("p h j s -> p (h j s)"), bank(2)).then_inc(sem["eT_dve"], 1)

            def lo_mixed(b, k0):
                for c in range(2):
                    k = k0 + 2 * c
                    dve.wait_ge(sem["xT_hi"], 5 + k // 2)
                    dve.tensor_tensor(x1l[:, k:k + 2, :].rearrange("p k s -> p (k s)"), bank(b + c),
                                      x1h[:, k:k + 2, :].rearrange("p k s -> p (k s)").bitcast(F32), ALU.subtract)\
                        .then_inc(sem["xT_lo"], 1)

            for p in range(3, 6):
                lo1(p)
            dve.wait_ge(sem["qk_sq"], 2)
            ch.link(dve.tensor_reduce(qk_ss, sqj.rearrange("p c t n -> p (c t n)").rearrange("p (h d) -> p h d", d=AD),
                                      AX.X, ALU.add))
            mean_eps(qk_ms, qk_ss, AD, EPS).then_inc(sem["qk_ms"], 1)
            lo1(6)
            dve.wait_ge(sem["qk_std"], 1)
            ch.link(dve.reciprocal(qk_rstd, qk_std))
            for c, (dst, free) in enumerate(((aq_tok, sem["z_q"]), (ak_tok, sem["z_k"]))):
                rstd = qk_rstd[:, 16 * c:16 * c + 16].unsqueeze(2).to_broadcast([P, 16, AD])
                dve.tensor_tensor(dst.rearrange("p t n -> p (t n)").rearrange("p (h d) -> p h d", d=AD),
                                  bank(Z_BANK[c], 2).rearrange("p (h d) -> p h d", d=AD), rstd, ALU.mult).then_inc(free, 1)
            lo1(7)
            lo1(8)
            dve.wait_ge(sem["qkT_ps"], 1)
            dve.tensor_scalar(qT.rearrange("p c s -> p (c s)"), bank(0, 2), one_f("q"), AD ** -0.5, ALU.mult, ALU.mult)\
                .then_inc(sem["qT_done"], 1)
            lo1(9)
            lo1(10)
            dve.wait_ge(sem["lb_done"], 1)
            dve.wait_ge(sem["band_in"], 32)
            maxima(0)
            maxima(1)
            scale_keys(0)
            weigh(0)
            weigh(1)
            for n in range(1, NG // 2):
                maxima(2 * n)
                copy_eT(2 * n - 1)
                maxima(2 * n + 1)
                lo1(10 + n)
                if n == 3:
                    outputs(0)
                weigh(2 * n)
                weigh(2 * n + 1)
                if n == 2:
                    scale_keys(1)
                    dve.wait_ge(sem["masks_zero"], 2)
            sums(0)
            copy_eT(NG - 1)
            lo1(14)
            sums(1)
            ch.settle()
            exponents(0)
            exponents(1)
            outputs(1)
            for i in range(NLEV):
                decayed_q(i)
                if i == 0:
                    lo1(15)
                if i >= 1:
                    put(i - 1)
                if i + 2 < NLEV:
                    exponents(i + 2)
                if i == 0:
                    dve.wait_ge(sem["z_ready"], 14)
                    dve.tensor_copy(hi_tok.rearrange("p t n -> p (t n)"), bank(Z_BANK[6], 2)).then_inc(sem["z_hi"], 1)
                if i == 3:
                    lo_mixed(4, 0)
            put(NLEV - 1)
            put(NLEV)
            dve.wait_ge(sem["w1_lo"], 18)
            lo1(18)
            dve.wait_ge(sem["ho_sq"], 1)
            ch.link(dve.tensor_reduce(o_ss, ho_sqj.rearrange("p (h d) -> p h d", d=HD),
                                      AX.X, ALU.add))
            mean_eps(o_ms, o_ss, HD, EPS).then_inc(sem["ho_ms"], 1)
            dve.wait_ge(sem["ho_std"], 1)
            ch.link(dve.reciprocal(o_rstd, o_std))
            dve.wait_ge(sem["gs_done"], 1)
            dve.wait_ge(sem["z_q"], 1)
            for t in range(TT):
                o_t = mixed[:, t, 512:1024].rearrange("p (h d) -> p h d", d=HD)
                for h in range(HH):
                    v = dve.scalar_tensor_tensor(o_t[:, h, :], bank(t)[:, h * HD:h * HD + HD], o_rstd[:, t * HH + h:t * HH + h + 1],
                                                 gs_tok[:, t, h * HD:h * HD + HD], ALU.mult, ALU.mult)
                v.then_inc(sem["ho_put"], 1)
            lo_mixed(2, 4)
            lo1(19)
            update(1, (sem["acc_done"], 1), 4)

            norm(1, one_f("norm2"))
            dve.tensor_scalar(xn[:, 1, :], x[:, 1, :], n_rstd[:, 1:2], None, ALU.mult).then_inc(sem["xn_dve"], 1)
            dve.wait_ge(sem["lg_ps"], 1)
            ch.link(dve.tensor_reduce(r_mx, bank(4)[:, 0:TT * NE].rearrange("p (t e) -> p t e", t=TT), AX.X, ALU.max))
            dve.tensor_scalar(r_nm, r_mx, -1.0, None, ALU.mult).then_inc(sem["lg_nm"], 1)
            dve.wait_ge(sem["lg_exp"], 1)
            ch.link(dve.reciprocal(r_rec, r_sum))
            for t in range(TT):
                v = dve.tensor_scalar(aff[:, t, :], aff_e[:, t, :], r_rec[:, t:t + 1], None, ALU.mult)
            v.then_inc(sem["aff_done"], 1)
            dve.wait_ge(sem["affT_ps"], 1)
            ch.link(dve.tensor_copy(topw, bank(5)[0:NE, 0:S]))
            for _ in range(CAP // 8):
                ch.link(dve.max(top8, topw))
                ch.link(dve.match_replace(topw, top8, topw, -1.0))
            ch.link(dve.tensor_scalar(chosen, topw, 0.0, None, ALU.is_lt))
            dve.wait_ge(sem["masks_zero"], 3)
            ch.link(dve.tensor_tensor_scan(place, ones_e, chosen, 0.0, ALU.mult, ALU.add))
            dve.tensor_tensor(place, place, chosen, ALU.mult).then_inc(sem["place_done"], 1)
            dve.wait_ge(sem["placeT_ps"], 1)
            ch.link(dve.tensor_copy(posT.rearrange("p t e -> p (t e)"), bank(6)[:, 0:TT * NE]))
            dve.tensor_tensor(hot_next, posT[:, :, 0:1].to_broadcast([P, TT, CAP]), rank.unsqueeze(1).to_broadcast([P, TT, CAP]),
                              ALU.is_equal).then_inc(sem["hot_done"], 1)
            dve.wait_ge(sem["tb_ps"], 1)
            dve.tensor_tensor(tb_rows, bank(7)[0:2 * DH, 0:TBW + 1], tb_future, ALU.add).then_inc(sem["tb_rows_done"], 1)
            for t in range(TT):
                v = dve.tensor_tensor(hot[:, t, 0:NE, :], posT[:, t, :].unsqueeze(2).to_broadcast([P, NE, CAP]),
                                      rank.unsqueeze(1).to_broadcast([P, NE, CAP]), ALU.is_equal)
                ch.step(v)
            dve.wait_ge(sem["masks_zero"], 4)
            ch.settle()

            def next_hot(e):
                dve.tensor_scalar(hot_next, hot[:, :, bass.ds(e, 1), :].rearrange("p t e c -> p t (e c)"), 1.0, None, ALU.mult)\
                    .then_inc(sem["hot_done"], 1)

            def next_tokens():
                dve.tensor_tensor(xin, bank(4)[:, 0:KD * CAP].rearrange("p (k c) -> p k c", k=KD),
                                  one_f("norm2").unsqueeze(2).to_broadcast([P, KD, CAP]), ALU.mult).then_inc(sem["xe_ready"], 1)

            with dve.Fori(0, NE) as e:
                dve.wait_ge(sem["xin_ps"], e + 1)
                next_tokens()
                for t in range(TT):
                    v = dve.tensor_scalar(hot_e[:, t, :, :], hot[:, t, bass.ds(e, 1), :].to_broadcast([P, Q4, CAP]),
                                          aff[:, t, bass.ds(e, 1)], None, ALU.mult)
                v.then_inc(sem["hote_done"], 1)
                for c in range(2):
                    dve.wait_ge(sem["used1"], 2 * e + c + 1)
                    dve.tensor_copy(u4[c], bank(5)).then_inc(sem["u4_done"], 1)
                next_hot(e + 1)
                for c in range(2):
                    dve.wait_ge(sem["esil_done"], 2 * e + c + 1)
                    dve.tensor_tensor(hidT[:, 4 * c:4 * c + 4, :].rearrange("p k c -> p (k c)"), e_sil[c],
                                      bank(6 + c)[:, 4 * CAP:8 * CAP], ALU.mult).then_inc(sem["ehid_done"], 1)
                dve.wait_ge(sem["used2"], 2 * e + 1)
                dve.tensor_copy(y4[1], bank(5)).then_inc(sem["y4_dve"], 1)

            before = ch.n
            with dve.Fori(0, DEPTH2) as L:
                ch.base, ch.n = dve.snap(LINKS * L + before), 0

                def lo(j, n):
                    dve.wait_ge(sem["w_hi"], sum(PIECES) * L + n + 1)
                    dve.tensor_tensor(wl[j], raw[j], wh[j].bitcast(F32), ALU.subtract).then_inc(raw_free[j], 1)

                def ffn(f):
                    q, n = STEPS * (2 * L + f), (3 * STEPS + MIX) * f + 2

                    def step(c, s, last=False):
                        i = 3 * s
                        lo(f if last else buf(f, GATE), n + i)
                        dve.wait_ge(raw_free[buf(f, DOWN)], nth(L, f, DOWN, s) + 1)
                        dve.wait_ge(sem["sil_done"], q + s + 1)
                        dve.scalar_tensor_tensor(f_hid[c].rearrange("p f s -> p (f s)"), f_sil[c], 0.5, bank(6 + c), ALU.mult, ALU.mult)\
                            .then_inc(sem["hid_t"], 1)
                        if not last:
                            lo(buf(f, UP), n + i + 1)
                            lo(buf(f, DOWN), n + i + 2)
                        dve.wait_ge(sem["hid_h"], q + s + 1)
                        dve.tensor_tensor(hidl[c].rearrange("p f s -> p (f s)"), f_hid[c].rearrange("p f s -> p (f s)"),
                                          hidh[c].rearrange("p f s -> p (f s)").bitcast(F32), ALU.subtract).then_inc(sem["hid_done"], 1)

                    with dve.Fori(0, STEPS // 2) as i:
                        step(0, 2 * i)
                        step(1, 2 * i + 1)
                    step(0, STEPS - 1, last=True)

                def lo_mix(m):
                    lo(buf_mix(m), 3 * STEPS + m)

                dve.tensor_scalar(prm, prm_all[:, bass.ds(L, 1), :].rearrange("p l n -> p (l n)"), 1.0, None, ALU.mult)\
                    .then_inc(sem["prm_ready"], 1)
                update(3 * L + 2, (sem["stage_done"], NE + L))
                dve.wait_ge(sem["prm_ready"], L + 1)
                norm(3 * L + 2, pf("norm0"), XT1 + 14 * L, between=lambda: lo(buf(0, GATE), 0))
                lo(buf(0, UP), 1)
                ch.link(dve.tensor_scalar(lc_y, pf("lam"), -1.0, None, ALU.mult))
                dve.tensor_tensor(lc_ab, lc_y, pf("lam"), ALU.max).then_inc(sem["lru_u"], 1)
                for i, (a, b) in enumerate((("lq1", "lk1"), ("lq2", "lk2"))):
                    v = dve.tensor_tensor_reduce(lam_j, pf(a), pf(b), 1.0, 0.0, ALU.mult, ALU.add, lamv[:, i:i + 1])
                    ch.link(v) if i == 0 else v.then_inc(sem["d_lamx"], 1)
                dve.wait_ge(sem["lru_c"], L + 1)
                ch.link(dve.tensor_scalar(lc_den, lc_u, 2.0, None, ALU.add))
                ch.link(dve.reciprocal(lc_den, lc_den))
                ch.link(dve.tensor_tensor(lc_z, lc_u, lc_den, ALU.mult))
                ch.link(dve.tensor_tensor(lc_z2, lc_z, lc_z, ALU.mult))
                ch.link(dve.tensor_scalar(lc_p, lc_z2, 1.0 / (2 * LOG1P_TERMS - 1), None, ALU.mult))
                for i in range(LOG1P_TERMS - 2, -1, -1):
                    ch.link(dve.scalar_tensor_tensor(lc_p, lc_p, 1.0 / (2 * i + 1), lc_z2 if i else lc_z, ALU.add, ALU.mult))
                ch.link(dve.tensor_scalar(lc_y, lc_y, 0.0, None, ALU.max))
                ch.link(dve.scalar_tensor_tensor(lc_p, lc_p, 2.0, lc_y, ALU.mult, ALU.add))
                dve.tensor_scalar(lc_c, lc_p, -LRU_C, None, ALU.mult)
                dve.tensor_scalar(lc_n, lc_p, LRU_C, None, ALU.mult).then_inc(sem["lru_b"], 1)
                dve.wait_ge(sem["d_lame"], L + 1)
                ch.link(dve.tensor_tensor(lamv[:, 4:5], lamv[:, 3:4], lamv[:, 2:3], ALU.subtract))
                ch.step(dve.tensor_tensor(lamv[:, 5:6], lamv[:, 4:5], pf("lam0"), ALU.subtract))
                ch.step(dve.tensor_tensor(lamv[:, 6:7], pf("subg"), pf("oml"), ALU.mult))
                neg_lam, sub_gain = lamv[:, 5:6], lamv[:, 6:7]
                ffn(0)

                lo_mix(0)
                update(3 * L + 3, (sem["acc_done"], 2 * L + 2))
                norm(3 * L + 3, pf("norm1"), XT1 + 14 * L + 4)
                for m in range(1, 6):
                    lo_mix(m)
                dve.wait_ge(sem["pads_zero"], 2)
                dve.wait_ge(*used_mix(L, 3))
                dve.wait_ge(sem["z2_0"], L + 1)
                ch.step(dve.tensor_tensor(sc_pad[:, :, 2:2 + S], scbc[:, 2:4, :], bank(2).rearrange("p (c s) -> p c s", c=2), ALU.mult))
                dve.tensor_copy(lx_pad[:, :, 3:3 + S], bank(3).rearrange("p (c s) -> p c s", c=2)).then_inc(sem["z2_1"], 1)
                lo_mix(6)
                dve.wait_ge(sem["z2_1"], L + 1)
                for c in range(2):
                    ch.step(dve.tensor_scalar(xr[:, c, :], lx_pad[:, c, 0:S], pf("lruw", 4 * c), pf("lrub", c), ALU.mult, ALU.add))
                for k in range(1, 4):
                    ch.settle()
                    for c in range(2):
                        v = dve.scalar_tensor_tensor(xr[:, c, :], lx_pad[:, c, k:k + S], pf("lruw", 4 * c + k), xr[:, c, :],
                                                     ALU.mult, ALU.add)
                        if k < 3 or c == 0:
                            ch.step(v)
                v.then_inc(sem["lru_xr"], 1)
                lo_mix(7)
                ch.settle()
                for c in range(2):
                    ch.step(dve.tensor_scalar(yc[:, c, :], sc_pad[:, c, 0:S], pf("scw", 3 * c), None, ALU.mult))
                for k in range(1, 3):
                    ch.settle()
                    for c in range(2):
                        ch.step(dve.scalar_tensor_tensor(yc[:, c, :], sc_pad[:, c, k:k + S], pf("scw", 3 * c + k), yc[:, c, :],
                                                         ALU.mult, ALU.add))
                ch.settle()
                ch.step(dve.tensor_tensor(yc, yc, scbc[:, 0:2, :], ALU.mult))
                lo_mix(8)
                dve.wait_ge(sem["z2_2"], L + 1)
                ch.link(dve.tensor_tensor(lg, lgate, lgate, ALU.mult))
                ch.link(dve.tensor_scalar(lg, lg, 0.044715, 1.0, ALU.mult, ALU.add))
                dve.tensor_tensor(lg, lg, lgate, ALU.mult).then_inc(sem["gelu_in"], 1)
                lo_mix(9)
                lo_mix(10)
                dve.wait_ge(sem["gelu_t"], L + 1)
                ch.step(dve.scalar_tensor_tensor(lg, lg, 1.0, lgate, ALU.add, ALU.mult))
                dve.wait_ge(sem["lru_a"], L + 1)
                ch.link(dve.tensor_tensor(rg, la, la, ALU.mult))
                ch.link(dve.scalar_tensor_tensor(lm, rg, 1.0, lm, ALU.add, ALU.mult))
                dve.tensor_scalar(lm, lm, SQRT_LEAST, None, ALU.max).then_inc(sem["lru_m"], 1)
                dve.wait_ge(sem["lru_xr"], L + 1)
                ch.link(dve.tensor_tensor(ig, ig, xr, ALU.mult))
                dve.wait_ge(sem["lru_sq"], L + 1)
                ch.link(dve.tensor_tensor(lm, lm, ig, ALU.mult))
                for c in range(2):
                    ch.step(dve.tensor_tensor_scan(xr[:, c, :], la[:, c, :], lm[:, c, :], 0.0, ALU.mult, ALU.add))
                ch.settle()
                ch.link(dve.scalar_tensor_tensor(lg.rearrange("p c s -> p (c s)"), lg.rearrange("p c s -> p (c s)"), 0.5,
                                                 xr.rearrange("p c s -> p (c s)"), ALU.mult, ALU.mult))

                def maxima2(g):
                    t, n = g // 2, P * (g // 2 + 1)
                    dve.wait_ge(sem["d_ps"], 4 * L + max(g, 1) + 1)
                    dve.memset(hold[:, 0:1], 0.0)
                    for m in range(2):
                        for i in range(2):
                            h, c = 2 * (g % 2) + i, 4 * g + 2 * m + i
                            ch.step(dve.tensor_tensor_reduce(d_e[g][:, m, i, :], d_scores(g, m, i),
                                                             tb[:, 2 * h + m, S - n:S], 1.0, -3e38, ALU.add, ALU.max, d_mx[:, c:c + 1]))
                    ch.settle()
                    dve.tensor_scalar(d_nm[:, 4 * g:4 * g + 4], d_mx[:, 4 * g:4 * g + 4], -1.0, None, ALU.mult).then_inc(sem["d_nmx"], 1)

                def combine(g):
                    n = P * (g // 2 + 1)
                    dve.wait_ge(sem["d_exp"], 4 * L + g + 1)
                    ch.link(dve.reciprocal(d_rd[:, 4 * g:4 * g + 4], d_den[:, 4 * g:4 * g + 4]))
                    ch.step(dve.tensor_scalar(d_c1[:, 2 * g:2 * g + 2], d_rd[:, 4 * g + 2:4 * g + 4], neg_lam, None, ALU.mult))
                    if g >= 2:
                        dve.wait_ge(sem["dT_ps"], 4 * L + g - 1)
                    for i in range(2):
                        ch.step(dve.tensor_scalar(d_attn[g % 2][:, i, 0:n], d_e[g][:, 0, i, :], d_rd[:, 4 * g + i:4 * g + i + 1],
                                                  None, ALU.mult))
                    ch.settle()
                    for i in range(2):
                        v = dve.scalar_tensor_tensor(d_attn[g % 2][:, i, 0:n], d_e[g][:, 1, i, :], d_c1[:, 2 * g + i:2 * g + i + 1],
                                                     d_attn[g % 2][:, i, 0:n], ALU.mult, ALU.add)
                    v.then_inc(sem["d_comb"], 1)

                dve.wait_ge(sem["tb_done"], 1)
                ch.link(dve.tensor_copy(y_h, y_cl))
                dve.tensor_tensor(y_l, y_cl, y_h.bitcast(F32), ALU.subtract).then_inc(sem["y_done"], 1)
                maxima2(0)
                maxima2(1)
                lo_mix(11)
                maxima2(2)
                combine(0)
                combine(1)
                lo_mix(12)
                maxima2(3)
                combine(2)

                def head_means(t):
                    dve.wait_ge(sem["do_sq"], 2 * L + t + 1)
                    ch.link(dve.tensor_reduce(d_ss[:, 4 * t:4 * t + 4], d_sq[t].rearrange("p (h d) -> p h d", d=P), AX.X, ALU.add))
                    mean_eps(d_ms[:, 4 * t:4 * t + 4], d_ss[:, 4 * t:4 * t + 4], P, SUBLN_EPS).then_inc(sem["do_ms"], 1)

                def head_norm(t):
                    dve.wait_ge(sem["do_std"], 2 * L + t + 1)
                    ch.link(dve.reciprocal(d_ss[:, 8 + 4 * t:12 + 4 * t], d_std[:, 4 * t:4 * t + 4]))
                    dve.tensor_tensor(xn[:, t, 0:512].rearrange("p (h d) -> p h d", d=P), bank(t).rearrange("p (h d) -> p h d", d=P),
                                      d_ss[:, 8 + 4 * t:12 + 4 * t].unsqueeze(2).to_broadcast([P, DH, P]), ALU.mult)\
                        .then_inc(sem["do_nrm"], 1)

                def heads_lo(t):
                    dve.wait_ge(sem["xT_hi"], XT1 + 14 * L + 9 + t)
                    dve.scalar_tensor_tensor(xTl[:, 0:DH, t * P:t * P + P], bank(t).rearrange("p (h s) -> p h s", h=DH), sub_gain,
                                             xTh[:, 0:DH, t * P:t * P + P].bitcast(F32), ALU.mult, ALU.subtract)\
                        .then_inc(sem["xT_lo"], 1)

                combine(3)
                head_means(0)
                lo_mix(13)
                head_norm(0)
                heads_lo(0)
                head_means(1)
                lo_mix(14)
                head_norm(1)
                heads_lo(1)
                lo(buf(1, GATE), 3 * STEPS + MIX)
                update(3 * L + 4, (sem["acc_done"], 2 * L + 3), 4)
                norm(3 * L + 4, pf("norm2"), XT1 + 14 * L + 10)
                lo(buf(1, UP), 3 * STEPS + MIX + 1)
                ffn(1)
            assert ch.n == LINKS, ch.n

            dve.wait_ge(sem["late_in"], 80)
            for t in range(TT):
                inverse(LAST, t)
                dve.wait_ge(sem["rstd_ready"], 2 * LAST + t + 1)
                dve.scalar_tensor_tensor(xn[:, t, :], bank(2 * t, 2), n_rstd[:, t:t + 1], fin_row, ALU.mult, ALU.mult)\
                    .then_inc(sem["fin_put"], 1)

        @block.gpsimd
        def _(pool):
            pool.memset(at_diag, 0.0).then_inc(sem["masks_zero"], 1)
            pool.memset(ones_s, 1.0).then_inc(sem["masks_zero"], 1)
            e_q = HH * S
            for i in range(NLEV + 1):
                if i < NLEV:
                    pool.wait_ge(sem["lev_exp"], i + 1)
                if i == 0:
                    pool.wait_ge(sem["k_scaled"], 2)
                if i == 1:
                    pool.wait_ge(sem["o_ps"], TT)
                if i >= 2:
                    pool.wait_ge(sem["lev_ps"], i - 1)
                if i < NLEV:
                    w = LEVELS[i]
                    n = HH * S // (2 * w)

                    def halves(a):
                        return a.rearrange("p (n f w) -> p n f w", n=n, f=2)

                    ek, kl = halves(lev_e[i % 2][:, e_q:2 * e_q]), halves(lev_qk[i % 2][:, e_q:2 * e_q])
                    kf_n, kb_n = [halves(k.rearrange("p h s -> p (h s)")) for k in (kf, kb)]
                    pool.tensor_tensor(kl[:, :, 0, :], kf_n[:, :, 0, :], ek[:, :, 0, :], ALU.mult)
                    pool.tensor_tensor(kl[:, :, 1, :], kb_n[:, :, 1, :], ek[:, :, 1, :], ALU.mult).then_inc(sem["lev_k"], 1)
                else:
                    pool.tensor_tensor(lev_qk[i % 2][:, e_q:2 * e_q], kf.rearrange("p h s -> p (h s)"),
                                       kb.rearrange("p h s -> p (h s)"), ALU.add).then_inc(sem["lev_k"], 1)
                if i in (2, 4):
                    p = 16 if i == 2 else 17
                    pool.wait_ge(sem["w1_hi"], p + 1)
                    pool.wait_ge(sem["w1_lo"], p)
                    pool.tensor_tensor(w1l[p % 3], raw1[p % 2], w1h[p % 3].bitcast(F32), ALU.subtract).then_inc(sem["w1_lo"], 1)
            pool.wait_ge(sem["z_hg"], 1)
            gs = gs_tok.rearrange("p t n -> p (t n)").rearrange("p (h d) -> p h d", d=HD)
            pool.tensor_tensor(gs, gs, one_f("onorm").unsqueeze(1).to_broadcast([P, TT * HH, HD]), ALU.mult).then_inc(sem["gs_done"], 1)
            pool.wait_ge(sem["acc_done"], 1)
            pool.memset(ones_e, 1.0).then_inc(sem["masks_zero"], 1)
            pool.memset(hot[:, :, NE, :], 0.0).then_inc(sem["masks_zero"], 1)
            pool.wait_ge(sem["used0"], 2 * NE)
            for j in range(3):
                pool.memset(hold[:, 1 + j:2 + j], 0.0).then_inc(raw_free[j], 1)
            pool.wait_ge(sem["stage_done"], NE)
            pool.memset(sc_pad[:, :, 0:2], 0.0).then_inc(sem["pads_zero"], 1)
            pool.memset(lx_pad[:, :, 0:3], 0.0).then_inc(sem["pads_zero"], 1)
            pool.wait_ge(sem["tb_in"], 16)
            pool.tensor_copy(tb, tb_raw[:, :, ::-1]).then_inc(sem["tb_done"], 1)


def kernel(**inputs):
    import concourse.bacc as bacc
    from concourse.bass_utils import run_bass_kernel_spmd

    a = {k: np.asarray(v) for k, v in inputs.items()}
    small, band, onehot, future = const_arrays()

    def cols(v):
        return np.reshape(v, (-1, P)).T

    def rows(v):
        return np.broadcast_to(np.reshape(v, (1, -1)), (P, v.size))

    def taps(w):
        return np.reshape(np.transpose(np.reshape(w, (w.shape[0], -1, P)), (2, 1, 0)), (P, -1))

    def diagonal(w):
        out = np.zeros((P, 2, P), np.float32)
        for i in range(4):
            r = 64 * (i % 2)
            out[r:r + 64, i // 2, r:r + 64] = w[i]
        return out.reshape(P, -1)

    lbs = [cols(a[n][r]) for r in range(2) for n in ("hgrn_lb_fwd", "hgrn_lb_bwd")]
    router = np.reshape(np.transpose(np.reshape(a["w_router"][0], (KD, P, NE)), (1, 0, 2)), (P, -1))
    one = np.concatenate([cols(a["norm1_w"][0]), cols(a["norm2_w"][0]),
                          np.tile(a["attn_q_norm_w"][0], 2)[:, None], np.tile(a["attn_k_norm_w"][0], 2)[:, None],
                          *lbs, rows(a["hgrn_out_norm_w"][0]), router], axis=1)
    layers = []
    for l in range(DEPTH2):
        lam0 = 0.8 - 0.6 * math.exp(-0.3 * l)
        layers.append(np.concatenate(
            [cols(a[n + "_norm_2"][l]) for n in ("ffn1", "mix", "ffn2")]
            + [rows(a[n + "_2"][l]) for n in ("lam_q1", "lam_k1", "lam_q2", "lam_k2")]
            + [cols(a["subln_gain_2"][l]), np.full((P, 1), lam0, np.float32), np.full((P, 1), 1.0 - lam0, np.float32),
               taps(a["sc_conv_w_2"][l]), taps(a["lru_conv_w_2"][l]), cols(a["lru_conv_b_2"][l]), cols(a["lru_ba_2"][l]),
               cols(a["lru_bx_2"][l]), cols(a["lru_lambda_2"][l]), diagonal(a["lru_wa_2"][l]), diagonal(a["lru_wx_2"][l])],
            axis=1))
    feed = [("x", a["x"][0]), ("w_in", a["w_in"][0]), ("w_out", a["w_out"][0]), ("w_expert_gate", a["w_expert_gate"][0]),
            ("w_expert_up", a["w_expert_up"][0]), ("w_expert_down", a["w_expert_down"][0]), ("rel_bias", a["rel_bias_2"]),
            ("ffn1_gate", a["ffn1_gate_2"]), ("ffn1_up", a["ffn1_up_2"]), ("ffn1_down", a["ffn1_down_2"]),
            ("w_in_2", a["w_in_2"]), ("w_out_2", a["w_out_2"]),
            ("ffn2_gate", a["ffn2_gate_2"]), ("ffn2_up", a["ffn2_up_2"]), ("ffn2_down", a["ffn2_down_2"]),
            ("small_constants", small), ("band_constants", band), ("bucket_constants", onehot), ("future_constants", future),
            ("first_block_params", one), ("layer_params", np.stack(layers)), ("final_norm", rows(a["final_norm_2"]))]
    nc = bacc.Bacc("TRN2", target_bir_lowering=False, num_devices=1)
    arrays, args = {}, []
    for name, v in feed:
        v = np.ascontiguousarray(v, dtype=np.float32)
        arrays[name] = v
        args.append(nc.dram_tensor(name, v.shape, F32, kind="ExternalInput").ap())
    args.append(nc.dram_tensor("out", (S, D), F32, kind="ExternalOutput").ap())
    two_blocks(nc, *args)
    r = run_bass_kernel_spmd(nc, [arrays], core_ids=[0])
    return r.results[0]["out"].reshape(1, S, D)
```
